# Optimizing a Trainium2 kernel written in Bass

```python
import math
import jax, jax.numpy as jnp
from jax import lax
import numpy as np

D_MODEL = 1024
BATCH = 1
SEQ = 1024
DEPTH = 1

PLE_DIM = 256
MIX_WIDTH = D_MODEL
POOL_WIDTH = MIX_WIDTH // 2
POOL_WINDOWS = (2, 4, 8, 16)
N_POOL_GROUPS = len(POOL_WINDOWS)
POOL_GROUP = POOL_WIDTH // N_POOL_GROUPS
HEAD_DIM = 64
ATTN_WIDTH = MIX_WIDTH - POOL_WIDTH
N_Q_HEADS = ATTN_WIDTH // HEAD_DIM
N_KV_HEADS = 2
GQA_GROUP = N_Q_HEADS // N_KV_HEADS
KV_WIDTH = N_KV_HEADS * HEAD_DIM
IN_WIDTH = POOL_WIDTH + ATTN_WIDTH + 2 * KV_WIDTH
WINDOW = 128
BLOCK = 128
D_FF = 4 * D_MODEL
LN_EPS = 1e-5
DEEPNORM_ALPHA = (2 * DEPTH) ** 0.25
DEEPNORM_BETA = (8 * DEPTH) ** -0.25
NEG_INF = -1e30


def layer_norm(x, g, b):
    xf = x.astype(jnp.float32)
    mu = jnp.mean(xf, axis=-1, keepdims=True)
    xc = xf - mu
    var = jnp.mean(xc * xc, axis=-1, keepdims=True)
    y = xc * lax.rsqrt(var + LN_EPS) * g.astype(jnp.float32) + b.astype(jnp.float32)
    return y.astype(x.dtype)

def alibi_slopes(n_heads):
    h = jnp.arange(1, n_heads + 1, dtype=jnp.float32)
    return jnp.exp2(-8.0 * h / n_heads)

def pool_mixer(u, w_pool, pool_scale):
    B, S, _ = u.shape
    uf = u.astype(jnp.float32)
    cs = jnp.pad(jnp.cumsum(uf, axis=1), ((0, 0), (1, 0), (0, 0)))
    t = jnp.arange(S)
    outs = []
    for g, w in enumerate(POOL_WINDOWS):
        sl = slice(g * POOL_GROUP, (g + 1) * POOL_GROUP)
        c = cs[..., sl]
        lo = jnp.maximum(t + 1 - w, 0)
        win_sum = c[:, 1:] - c[:, lo]
        count = (t + 1 - lo).astype(jnp.float32)[None, :, None]
        outs.append(win_sum / count - uf[..., sl])
    d = jnp.stack(outs, axis=2).astype(u.dtype)
    y = jnp.einsum('bsgc,gcd->bsgd', d, w_pool).reshape(B, S, POOL_WIDTH)
    return y * pool_scale

def sliding_window_attention(q, k, v, sinks):
    B, S = q.shape[:2]
    nb = S // BLOCK
    qb = q.reshape(B, nb, BLOCK, N_KV_HEADS, GQA_GROUP, HEAD_DIM)

    def band(a):
        ab = a.reshape(B, nb, BLOCK, N_KV_HEADS, HEAD_DIM)
        prev = jnp.pad(ab, ((0, 0), (1, 0), (0, 0), (0, 0), (0, 0)))[:, :-1]
        return jnp.concatenate([prev, ab], axis=2)

    kb, vb = band(k), band(v)
    scale = 1.0 / math.sqrt(HEAD_DIM)
    scores = jnp.einsum('bnqkgd,bnjkd->bnkgqj', qb, kb).astype(jnp.float32) * scale

    qi = jnp.arange(BLOCK)
    kj = jnp.arange(2 * BLOCK)
    dist = (qi[:, None] + BLOCK - kj[None, :])
    in_band = (dist >= 0) & (dist < WINDOW)
    key_pos = jnp.arange(nb)[:, None] * BLOCK - BLOCK + kj[None, :]
    mask = in_band[None] & (key_pos >= 0)[:, None, :]

    slopes = alibi_slopes(N_Q_HEADS).reshape(N_KV_HEADS, GQA_GROUP)
    bias = -slopes[:, :, None, None] * dist.astype(jnp.float32)[None, None]
    scores = jnp.where(mask[None, :, None, None], scores + bias[None, None], NEG_INF)

    sink = sinks.astype(jnp.float32).reshape(1, 1, N_KV_HEADS, GQA_GROUP, 1, 1)
    m = jnp.maximum(jnp.max(scores, axis=-1, keepdims=True), sink)
    e = jnp.exp(scores - m)
    denom = jnp.sum(e, axis=-1, keepdims=True) + jnp.exp(sink - m)
    probs = (e / denom).astype(v.dtype)
    out = jnp.einsum('bnkgqj,bnjkd->bnqkgd', probs, vb)
    return out.reshape(B, S, ATTN_WIDTH)

def first_inputs(seed: int = 0) -> dict:
    key = jax.random.key(seed)
    ks = jax.random.split(key, 16)
    f32 = jnp.float32

    def nrm(k, shape, std):
        return jax.random.normal(k, shape, f32) * std

    return {
        "x": nrm(ks[0], (BATCH, SEQ, D_MODEL), 1.0),
        "p": nrm(ks[1], (DEPTH, BATCH, SEQ, PLE_DIM), 1.0),
        "w_in": nrm(ks[2], (DEPTH, D_MODEL, IN_WIDTH), D_MODEL ** -0.5),
        "w_pool": nrm(ks[3], (DEPTH, N_POOL_GROUPS, POOL_GROUP, POOL_GROUP), POOL_GROUP ** -0.5),
        "pool_scale": 1.0 + nrm(ks[4], (DEPTH, POOL_WIDTH), 0.1),
        "attn_sinks": nrm(ks[5], (DEPTH, N_Q_HEADS), 0.5),
        "w_out": nrm(ks[6], (DEPTH, MIX_WIDTH, D_MODEL), MIX_WIDTH ** -0.5 * DEEPNORM_BETA),
        "ln1_g": 1.0 + nrm(ks[7], (DEPTH, D_MODEL), 0.05),
        "ln1_b": nrm(ks[8], (DEPTH, D_MODEL), 0.02),
        "w_ff1": nrm(ks[9], (DEPTH, D_MODEL, D_FF), D_MODEL ** -0.5),
        "w_ff2": nrm(ks[10], (DEPTH, D_FF, D_MODEL), D_FF ** -0.5 * DEEPNORM_BETA),
        "ln2_g": 1.0 + nrm(ks[11], (DEPTH, D_MODEL), 0.05),
        "ln2_b": nrm(ks[12], (DEPTH, D_MODEL), 0.02),
        "w_ple": nrm(ks[13], (DEPTH, PLE_DIM, D_MODEL), PLE_DIM ** -0.5),
        "w_ple_gate": nrm(ks[14], (DEPTH, D_MODEL, D_MODEL), D_MODEL ** -0.5),
        "b_ple_gate": nrm(ks[15], (DEPTH, D_MODEL), 0.02),
    }

def first_block(x, p, w_in, w_pool, pool_scale, attn_sinks, w_out, ln1_g, ln1_b,
              w_ff1, w_ff2, ln2_g, ln2_b, w_ple, w_ple_gate, b_ple_gate):
    B, S, _ = x.shape
    h = x
    for i in range(DEPTH):
        z = h @ w_in[i]
        u_pool = z[..., :POOL_WIDTH]
        q = z[..., POOL_WIDTH:POOL_WIDTH + ATTN_WIDTH].reshape(B, S, N_Q_HEADS, HEAD_DIM)
        k = z[..., POOL_WIDTH + ATTN_WIDTH:POOL_WIDTH + ATTN_WIDTH + KV_WIDTH].reshape(B, S, N_KV_HEADS, HEAD_DIM)
        v = z[..., POOL_WIDTH + ATTN_WIDTH + KV_WIDTH:].reshape(B, S, N_KV_HEADS, HEAD_DIM)

        y_pool = pool_mixer(u_pool, w_pool[i], pool_scale[i])
        y_attn = sliding_window_attention(q, k, v, attn_sinks[i])
        mix = jnp.concatenate([y_pool, y_attn], axis=-1) @ w_out[i]
        h = layer_norm(DEEPNORM_ALPHA * h + mix, ln1_g[i], ln1_b[i])

        ff = jnp.square(jax.nn.relu(h @ w_ff1[i])) @ w_ff2[i]
        h = layer_norm(DEEPNORM_ALPHA * h + ff, ln2_g[i], ln2_b[i])

        gate = jax.nn.sigmoid(h @ w_ple_gate[i] + b_ple_gate[i])
        h = h + gate * (p[i] @ w_ple[i])
    return h


CHUNK = 64
N_PREV_CHUNKS = 8
BAND = (N_PREV_CHUNKS + 1) * CHUNK
H_A = 8
H_B = 8
W_A = H_A * HEAD_DIM
W_B = H_B * HEAD_DIM
W_MIX = W_A + W_B
W_IN = 3 * W_MIX
REL_CLIP = 128
SB_BLOCK = 128
D_FF_2 = 2816
CONV_WIDTH = 3
N_MOD = 6
EPS = 1e-6


def rms_norm(x):
    xf = x.astype(jnp.float32)
    y = xf * lax.rsqrt(jnp.mean(xf * xf, axis=-1, keepdims=True) + EPS)
    return y.astype(x.dtype)

def modulate(h, shift, scale):
    return h * (1 + scale[:, None, :]) + shift[:, None, :]

def rel_bias_band(rel_bias):
    q_pos = N_PREV_CHUNKS * CHUNK + jnp.arange(CHUNK)
    k_pos = jnp.arange(BAND)
    dist = jnp.clip(q_pos[:, None] - k_pos[None, :], -REL_CLIP, REL_CLIP) + REL_CLIP
    return rel_bias[:, dist]

def chunked_rel_attention(q, k, v, rel_bias):
    b, s, h, dh = q.shape
    n_chunks = s // CHUNK
    qc = q.reshape(b, n_chunks, CHUNK, h, dh)
    pad = ((0, 0), (N_PREV_CHUNKS, 0), (0, 0), (0, 0), (0, 0))
    kp = jnp.pad(k.reshape(b, n_chunks, CHUNK, h, dh), pad)
    vp = jnp.pad(v.reshape(b, n_chunks, CHUNK, h, dh), pad)
    band_idx = jnp.arange(n_chunks)[:, None] + jnp.arange(N_PREV_CHUNKS + 1)[None, :]
    kb = kp[:, band_idx].reshape(b, n_chunks, BAND, h, dh)
    vb = vp[:, band_idx].reshape(b, n_chunks, BAND, h, dh)
    scores = jnp.einsum("bcqhd,bckhd->bhcqk", qc, kb).astype(jnp.float32) * (dh ** -0.5)
    scores = scores + rel_bias_band(rel_bias).astype(jnp.float32)[None, :, None]
    key_chunk = (jnp.arange(n_chunks)[:, None] - N_PREV_CHUNKS
                 + (jnp.arange(BAND) // CHUNK)[None, :])
    scores = jnp.where((key_chunk >= 0)[None, None, :, None, :], scores, -jnp.inf)
    probs = jax.nn.softmax(scores, axis=-1).astype(v.dtype)
    out = jnp.einsum("bhcqk,bckhd->bcqhd", probs, vb)
    return out.reshape(b, s, h * dh)

def stick_breaking_attention(q, k, v):
    b, s, h, dh = q.shape
    scale = dh ** -0.5
    outs = []
    for blk in range(s // SB_BLOCK):
        q_start = blk * SB_BLOCK
        k_end = q_start + SB_BLOCK
        logits = jnp.einsum("bqhd,bkhd->bhqk", q[:, q_start:k_end],
                            k[:, :k_end]).astype(jnp.float32) * scale
        strict = (q_start + jnp.arange(SB_BLOCK))[:, None] > jnp.arange(k_end)[None, :]
        log_beta = jax.nn.log_sigmoid(logits)
        log_keep = jnp.where(strict, jax.nn.log_sigmoid(-logits), 0.0)
        log_tail = lax.cumsum(log_keep, axis=3, reverse=True) - log_keep
        weights = jnp.where(strict, jnp.exp(log_beta + log_tail), 0.0).astype(v.dtype)
        outs.append(jnp.einsum("bhqk,bkhd->bqhd", weights, v[:, :k_end]))
    return jnp.concatenate(outs, axis=1).reshape(b, s, h * dh)

def causal_depthwise_conv(u, w, bias):
    s = u.shape[1]
    up = jnp.pad(u, ((0, 0), (CONV_WIDTH - 1, 0), (0, 0)))
    y = w[0] * up[:, 0:s]
    for i in range(1, CONV_WIDTH):
        y = y + w[i] * up[:, i:i + s]
    return y + bias

def hybrid_layer(x, c_act, w_ada, b_ada, w_in, rel_bias, g_a, g_b, w_out,
                 w_up, conv_w, conv_b, w_down):
    b, s, _ = x.shape
    mod = c_act @ w_ada + b_ada
    shift_mix, scale_mix, gate_mix, shift_ffn, scale_ffn, gate_ffn = jnp.split(mod, N_MOD, axis=-1)

    h = modulate(rms_norm(x), shift_mix, scale_mix)
    proj = h @ w_in
    cuts = [W_A, 2 * W_A, 3 * W_A, 3 * W_A + W_B, 3 * W_A + 2 * W_B]
    qa, ka, va, qb, kb, vb = jnp.split(proj, cuts, axis=-1)
    oa = chunked_rel_attention(qa.reshape(b, s, H_A, HEAD_DIM), ka.reshape(b, s, H_A, HEAD_DIM),
                               va.reshape(b, s, H_A, HEAD_DIM), rel_bias)
    ob = stick_breaking_attention(qb.reshape(b, s, H_B, HEAD_DIM), kb.reshape(b, s, H_B, HEAD_DIM),
                                  vb.reshape(b, s, H_B, HEAD_DIM))
    mixed = jnp.concatenate([rms_norm(oa) * g_a, rms_norm(ob) * g_b], axis=-1) @ w_out
    x = x + gate_mix[:, None, :] * mixed

    h = modulate(rms_norm(x), shift_ffn, scale_ffn)
    gate, val = jnp.split(causal_depthwise_conv(h @ w_up, conv_w, conv_b), 2, axis=-1)
    x = x + gate_ffn[:, None, :] * ((jax.nn.silu(gate) * val) @ w_down)
    return x

def second_inputs(seed: int = 0) -> dict:
    key = jax.random.key(seed)
    ks = jax.random.split(key, 14)
    f32 = jnp.float32
    nrm = lambda k, shape: jax.random.normal(k, shape, dtype=f32)
    return {
        "x": nrm(ks[0], (BATCH, SEQ, D_MODEL)),
        "c": nrm(ks[1], (BATCH, D_MODEL)),
        "w_ada": nrm(ks[2], (DEPTH, D_MODEL, N_MOD * D_MODEL)) * D_MODEL ** -0.5,
        "b_ada": nrm(ks[3], (DEPTH, N_MOD * D_MODEL)) * 0.02,
        "w_in": nrm(ks[4], (DEPTH, D_MODEL, W_IN)) * D_MODEL ** -0.5,
        "rel_bias": nrm(ks[5], (DEPTH, H_A, 2 * REL_CLIP + 1)) * 0.5,
        "g_a": 1.0 + 0.1 * nrm(ks[6], (DEPTH, W_A)),
        "g_b": 1.0 + 0.1 * nrm(ks[7], (DEPTH, W_B)),
        "w_out": nrm(ks[8], (DEPTH, W_MIX, D_MODEL)) * W_MIX ** -0.5,
        "w_up": nrm(ks[9], (DEPTH, D_MODEL, 2 * D_FF_2)) * D_MODEL ** -0.5,
        "conv_w": nrm(ks[10], (DEPTH, CONV_WIDTH, 2 * D_FF_2)) * CONV_WIDTH ** -0.5,
        "conv_b": nrm(ks[11], (DEPTH, 2 * D_FF_2)) * 0.02,
        "w_down": nrm(ks[12], (DEPTH, D_FF_2, D_MODEL)) * D_FF_2 ** -0.5,
        "final_g": 1.0 + 0.1 * nrm(ks[13], (D_MODEL,)),
    }

def second_block(x, c, w_ada, b_ada, w_in, rel_bias, g_a, g_b, w_out, w_up, conv_w,
              conv_b, w_down, final_g):
    c_act = jax.nn.silu(c)
    for l in range(DEPTH):
        x = hybrid_layer(x, c_act, w_ada[l], b_ada[l], w_in[l], rel_bias[l], g_a[l], g_b[l],
                         w_out[l], w_up[l], conv_w[l], conv_b[l], w_down[l])
    return rms_norm(x) * final_g


def setup_inputs(seed=0):
    out = dict(first_inputs(seed))
    for name, value in second_inputs(seed + 1).items():
        if name != "x":
            out[name + "_2"] = value
    return out


def reference(
    x, p, w_in, w_pool, pool_scale, attn_sinks, w_out, ln1_g, ln1_b, w_ff1, w_ff2, ln2_g, ln2_b,
    w_ple, w_ple_gate, b_ple_gate, c_2, w_ada_2, b_ada_2, w_in_2, rel_bias_2, g_a_2, g_b_2,
    w_out_2, w_up_2, conv_w_2, conv_b_2, w_down_2, final_g_2,
):
    x = first_block(
        x, p, w_in, w_pool, pool_scale, attn_sinks, w_out, ln1_g, ln1_b, w_ff1, w_ff2, ln2_g,
        ln2_b, w_ple, w_ple_gate, b_ple_gate,
    )
    return second_block(
        x, c_2, w_ada_2, b_ada_2, w_in_2, rel_bias_2, g_a_2, g_b_2, w_out_2, w_up_2, conv_w_2,
        conv_b_2, w_down_2, final_g_2,
    )


_drawn_inputs = setup_inputs


def setup_inputs(seed=0):
    import zlib

    import numpy as np

    out = dict(_drawn_inputs(seed))
    spreads = {}
    factors = {'attn_sinks': 8.0, 'ln1_b': 2.676, 'b_ple_gate': 8.0, 'conv_b_2': 5.569}
    for name, (base, spread) in spreads.items():
        noise = np.random.default_rng([zlib.crc32(name.encode()), seed]).standard_normal(out[name].shape)
        drawn = base * np.exp(spread * noise) if base else spread * noise
        out[name] = __import__('jax').numpy.asarray(drawn.astype(out[name].dtype))
    for name, factor in factors.items():
        out[name] = (out[name] * factor).astype(out[name].dtype)
    return out
```

```python
import concourse.bass as bass
from concourse import mybir
from contextlib import ExitStack

F32 = mybir.dt.float32
F32R = mybir.dt.float32r
I32 = mybir.dt.int32
ALU = mybir.AluOpType
ACT = mybir.ActivationFunctionType
ds = bass.ds

P = 128
D = 1024
S = 1024
KT = D // P
RT = S // P
HB = 512
ALPHA = 2.0 ** 0.25
LN_EPS = 1e-5
RMS_EPS = 1e-6
QSCALE = 0.125
DFF = 4096
DFF2 = 2816
W1 = 2
WA = 5
BIG = 1e30

SEGMENTS = [
    ("in", 1, ["S"] * 6 + ["D"] * 4),
    ("out", 1, ["M"] * 8),
    ("ff", 8, ["S"] * 4 + ["M"] * 4),
    ("gate", 4, ["D"] * 2),
    ("in2a", 2, ["S"] * 6),
    ("in2b", 2, ["S"] * 6),
    ("out2", 1, ["M"] * 8),
    ("up", 5, ["S"] * 8 + ["M"] * 4),
    ("uplast", 1, ["S"] * 4 + ["M"] * 2),
]


def stream_table():
    table, unit, tile, chunk, loads = {}, 0, 0, 0, [0, 0]
    for name, n, units in SEGMENTS:
        rows, at = [], list(loads)
        t = 0
        for c, u in enumerate(units):
            slot = (unit + c) % 2
            at[slot] += 32 if u == "D" else 16
            rows.append((u, slot, at[slot], t))
            t += u != "M"
        per = [at[0] - loads[0], at[1] - loads[1]]
        table[name] = dict(n=n, rows=rows, unit=unit, tile=tile, chunk=chunk, per=per,
                           tiles=t, units=len(units))
        unit += n * len(units)
        tile += n * t
        chunk += n * ((units.count("M") + 3) // 4)
        loads = [loads[0] + n * per[0], loads[1] + n * per[1]]
    return table


SEG = stream_table()


class Chain:

    def __init__(self, eng, sem):
        self.eng, self.sem, self.base, self.n, self.at = eng, sem, 0, 0, None

    def enter(self, i, per):
        self.base += self.n
        self.at, self.per, self.n = i, per, 0

    def leave(self, times):
        assert self.n == self.per, (self.n, self.per)
        self.base, self.at, self.n = self.base + times * self.per, None, 0

    def link(self, ins):
        ins.then_inc(self.sem, 1)
        self.n += 1
        if self.at is None:
            self.eng.wait_ge(self.sem, self.base + self.n)
        else:
            self.eng.wait_ge(self.sem, self.at * self.per + (self.base + self.n))


def build(nc, x, p, w_in, w_pool, pool_scale, attn_sinks, w_out, ln1_g, ln1_b, w_ff1, w_ff2,
          ln2_g, ln2_b, w_ple, w_ple_gate, b_ple_gate, c_2, w_ada_2, b_ada_2, w_in_2, rel_rev,
          g_a_2, g_b_2, w_out_2, w_up_2, conv_w_2, conv_b_2, w_down_2, final_g_2, out,
          stop=99):
    x, p, w_in, w_pool, w_out = x[0], p[0, 0], w_in[0], w_pool[0], w_out[0]
    w_ff1, w_ff2, w_ple, w_ple_gate = w_ff1[0], w_ff2[0], w_ple[0], w_ple_gate[0]
    w_ada, w_in2, w_out2, w_up, w_down = w_ada_2[0], w_in_2[0], w_out_2[0], w_up_2[0], w_down_2[0]
    out = out[0]

    ctx = ExitStack()
    with ctx:
        ctx.enter_context(nc.allow_non_contiguous_dma("per-feature vectors go to partitions"))

        def sem(name):
            return ctx.enter_context(nc.semaphore(name))

        top = [(nc.sbuf_base + 63) // 64 * 64]

        def region(nbytes):
            at = top[0]
            top[0] += nbytes
            return at

        def place(name, shape, dt, at):
            return nc.alloc_sbuf_tensor_at(name, shape, dt, offset=at)

        KB = 1024
        R_T = region(64 * KB)
        R_A = region(32 * KB)
        R_H = region(32 * KB)
        R_M = region(32 * KB)
        R_S = region(20 * KB)
        R_W = region(10 * KB)
        R_B = region(26 * KB)

        def small(name, shape, dt=F32):
            n = 4
            for s_ in shape[1:]:
                n *= s_
            return place(name, shape, dt, region((n + 31) // 32 * 32))

        actT_hi = place("actT_hi", [P, KT, S], F32R, R_T)
        actT_lo = place("actT_lo", [P, KT, S], F32R, R_T + 32 * KB)
        acc = place("acc", [P, RT, D], F32, R_A)
        ypool = place("ypool", [P, 4, S], F32, R_A)
        o1 = place("o1", [P, RT, HB], F32, R_A + 16 * KB)
        hid_hi = place("hid_hi", [P, 4, S], F32R, R_H)
        hid_lo = place("hid_lo", [P, 4, S], F32R, R_H + 16 * KB)
        rows2 = place("rows2", [P, RT, D], F32, R_H)
        p_rows = place("p_rows", [P, RT, 256], F32, R_H + 8 * KB)
        mv_hi = place("mv_hi", [P, 4, D], F32R, R_M)
        mv_lo = place("mv_lo", [P, 4, D], F32R, R_M + 16 * KB)
        q_hi = place("q_hi", [P, S], F32R, R_M)
        q_lo = place("q_lo", [P, S], F32R, R_M + 4 * KB)
        k_hi = place("k_hi", [P, S], F32R, R_M + 8 * KB)
        k_lo = place("k_lo", [P, S], F32R, R_M + 12 * KB)
        v_hi = place("v_hi", [P, RT, P], F32R, R_M + 16 * KB)
        v_lo = place("v_lo", [P, RT, P], F32R, R_M + 20 * KB)
        evac_att = place("evac_att", [P, 2, S], F32, R_M + 24 * KB)
        st_hi = place("st_hi", [P, 2, 10, P], F32R, R_S)
        st_lo = place("st_lo", [P, 2, 10, P], F32R, R_S + 10 * KB)
        raw = place("raw", [P, 2, 10 * P], F32, R_W)
        evac = place("evac", [P, 2, S], F32, R_B)
        row_a = place("row_a", [P, D], F32, R_B + 8 * KB)
        row_b = place("row_b", [P, D], F32, R_B + 12 * KB)
        gprod = place("gprod", [P, 2, S], F32, R_B + 8 * KB)
        AW = 6 * D // 8
        ada_raw = place("ada_raw", [P, 2, AW], F32, R_B + 16 * KB)
        ada_acc = place("ada_acc", [P, AW], F32, R_B + 22 * KB)
        gated1 = place("gated1", [P, D], F32, R_B + 16 * KB)
        gated2 = place("gated2", [P, D], F32, R_B + 8 * KB)
        cv = place("cv", [P, 2, S], F32, R_B + 16 * KB)
        sq_junk = place("sq_junk", [P, D], F32, R_B + 20 * KB)
        row_g = place("row_g", [P, D], F32, R_B + 16 * KB)
        bias1 = place("bias1", [P, 8, 2 * P], F32, R_B)
        sums = place("sums", [P, 2, S], F32, R_B + 8 * KB)
        d_hi = place("d_hi", [P, S], F32R, R_B + 16 * KB)
        d_lo = place("d_lo", [P, S], F32R, R_B + 20 * KB)
        prob1 = place("prob1", [P, 2, 2 * P], F32, R_B + 8 * KB)
        pT1_hi = place("pT1_hi", [P, 2, 2 * P], F32R, R_B + 10 * KB)
        pT1_lo = place("pT1_lo", [P, 2, 2 * P], F32R, R_B + 12 * KB)
        NA = WA * P
        prob2 = place("prob2", [P, 2, NA], F32, R_B)
        pT2_hi = place("pT2_hi", [P, 2, NA], F32R, R_B + 5 * KB)
        pT2_lo = place("pT2_lo", [P, 2, NA], F32R, R_B + 10 * KB)
        bias2 = place("bias2", [P, 2, NA], F32, R_B + 15 * KB)
        bias_up = place("bias_up", [P, 2, NA], F32, R_B + 20 * KB)
        logit = place("logit", [P, 3, HB], F32, R_B)
        soft = place("soft", [P, 2, HB], F32, R_B + 6 * KB)
        sp_hi = place("sp_hi", [P, 2, HB], F32R, R_B + 10 * KB)
        sp_lo = place("sp_lo", [P, 2, HB], F32R, R_B + 14 * KB)
        wt_hi = place("wt_hi", [P, 2, HB], F32R, R_B + 18 * KB)
        wt_lo = place("wt_lo", [P, 2, HB], F32R, R_B + 22 * KB)
        pw = place("pw", [P, 4, P], F32, R_H)
        pwr_hi = place("pwr_hi", [P, 4, P], F32R, R_H + 2 * KB)
        pwr_lo = place("pwr_lo", [P, 4, P], F32R, R_H + 4 * KB)
        tri_f = place("tri_f", [P, 2, P], F32, R_H + 6 * KB)
        ident = small("ident", [P, P])
        flip = small("flip", [P, P])
        tri = small("tri", [P, 2, P], F32R)
        keep = small("keep", [P, P])
        drop = small("drop", [P, P])
        ones = small("ones", [P, P])
        diag = small("diag", [P, P])
        modT = small("modT", [P, 48])
        b_ada = small("b_ada", [P, 48])
        c_col = small("c_col", [P, 8])
        c_act = small("c_act", [P, 8])
        pscale = small("pscale", [P, 4])
        b_gate = small("b_gate", [P, 8])
        gab = small("gab", [P, 8])
        cw = small("cw", [P, 3, 44])
        cb = small("cb", [P, 44])
        sink = small("sink", [P, 8])
        wcount = small("wcount", [P, 16])
        stats = small("stats", [P, 2, 6])
        mv2 = small("mv2", [P, 2])
        std = small("std", [P, 1])
        rstd = small("rstd", [P, 1])
        nmr = small("nmr", [P, 1])
        ssq = small("ssq", [P, 16])
        rms = small("rms", [P, 16])
        rinv = small("rinv", [P, 16])
        mx = small("mx", [P, 16])
        nmx = small("nmx", [P, 16])
        den = small("den", [P, 16])
        sden = small("sden", [P, 16])
        eps = small("eps", [P, 2])
        tmp512 = small("tmp512", [P, 1])
        eps_one = small("eps_one", [P, 1])
        wcnt_i = small("wcnt_i", [P, 16], I32)
        assert top[0] <= nc.sbuf_usable_end, top[0]

        pd = ctx.enter_context(nc.psum_tensor("pd", [P, 2, 2 * HB], F32))
        pt = ctx.enter_context(nc.psum_tensor("pt", [P, 4, HB], F32))

        ext = nc.dram_tensor("rel_ext", [8, 768], F32)

        raw_in = [sem("raw_in0"), sem("raw_in1")]
        split_hi = sem("split_hi")
        w_ready = sem("w_ready")
        tile_done = sem("tile_done")
        m_rows = sem("m_rows")
        t_free = sem("t_free")
        x_used = sem("x_used")
        m_free = sem("m_free")
        tp_done = sem("tp_done")
        tp_hi = sem("tp_hi")
        tp_lo = sem("tp_lo")
        x_in = sem("x_in")
        x_back = [sem(f"x_back{r}") for r in range(RT)]
        consts = sem("consts")
        setup = sem("setup")
        gsetup = sem("gsetup")
        vecs = sem("vecs")
        vchain = sem("vchain")
        achain = sem("achain")
        d_ready = sem("d_ready")
        pool_mm = sem("pool_mm")
        pool_out = sem("pool_out")
        pw_split = sem("pw_split")
        v_done = sem("v_done")
        s_done = sem("s_done")
        nm_ready = sem("nm_ready")
        p_ready = sem("p_ready")
        pt_done = sem("pt_done")
        pt_hi_s = sem("pt_hi_s")
        pt_lo_s = sem("pt_lo_s")
        pv_done = sem("pv_done")
        sink_e = sem("sink_e")
        yp_hi = sem("yp_hi")
        yp_lo = sem("yp_lo")
        row_rd = sem("row_rd")
        bias_cp = sem("bias_cp")
        gb_rows = sem("gb_rows")
        cv_done = sem("cv_done")
        silu_done = sem("silu_done")
        g_in = sem("g_in")
        act_one = sem("act_one")
        o_done = sem("o_done")
        row_done = sem("row_done")
        stat_in = sem("stat_in")
        std_done = sem("std_done")
        gb_in = sem("gb_in")
        ada_in = [sem("ada_in0"), sem("ada_in1")]
        ada_used = sem("ada_used")
        ada_full = sem("ada_full")
        ada_mm = sem("ada_mm")
        c_ready = sem("c_ready")
        p_in = sem("p_in")
        ple_done = sem("ple_done")
        ple_free = sem("ple_free")
        gp_ready = sem("gp_ready")
        gp_mm = sem("gp_mm")
        gp_added = sem("gp_added")
        ss_done = sem("ss_done")
        sq_done = sem("sq_done")
        diag_rdy = sem("diag_rdy")
        bc_mm = sem("bc_mm")
        ext_in = sem("ext_in")
        ext_out = sem("ext_out")
        bias_in = sem("bias_in")
        bias_mm = sem("bias_mm")
        bias_rdy = sem("bias_rdy")
        b_s = sem("b_s")
        b_l = sem("b_l")
        b_t = sem("b_t")
        b_exp = sem("b_exp")
        b_ln = sem("b_ln")
        b_sp = sem("b_sp")
        b_c = sem("b_c")
        b_sub = sem("b_sub")
        b_w = sem("b_w")
        b_ws = sem("b_ws")
        b_pv = sem("b_pv")
        fin_rdy = sem("fin_rdy")
        stored = [sem("stored0"), sem("stored1")]

        def row_base(name):
            return {"h1": 0, "h2": 8}[name]

        UPH = {"up": 0, "uplast": 4 * 5}
        TILE = {n: SEG[n]["tile"] for n in SEG}
        CH = {n: SEG[n]["chunk"] for n in SEG}
        UN = {n: SEG[n]["unit"] for n in SEG}
        order = [s_[0] for s_ in SEGMENTS]

        TPJ, n_ = {}, 0
        for name, k in (("x", 16), ("o1", 8), ("h1", 16), ("h2", 16), ("p", 4), ("m1", 16), ("o2", 16), ("m2", 16)):
            TPJ[name] = n_
            n_ += k

        BSTEPS = [(hh, hf, kt) for hh in range(2) for hf in range(2) for kt in range(4 * hf + 3, -1, -1)]
        NB = len(BSTEPS)

        def bcols(hf, kt):
            q0 = max(kt * P, hf * HB)
            return q0, (hf + 1) * HB - q0, q0 - hf * HB

        block = ctx.enter_context(nc.Block())

        @block.sync
        def _(sp):
            w_in_t = w_in.rearrange("(k p) n -> p k n", p=P)
            ff1_t = w_ff1.rearrange("(k p) n -> p k n", p=P)
            gate_t = w_ple_gate.rearrange("(k p) n -> p k n", p=P)
            ple_t = w_ple.rearrange("(k p) n -> p k n", p=P)
            in2_t = w_in2.rearrange("(k p) n -> p k n", p=P)
            up_t = w_up.rearrange("(k p) n -> p k n", p=P)

            def raw_k(slot, a, b):
                return raw[:, slot, a * P:b * P].rearrange("p (k n) -> p k n", n=P)

            def room(name, i, c):
                g = UN[name] + c
                if i is None:
                    if g >= 2:
                        sp.wait_ge(w_ready, g - 1)
                else:
                    sp.wait_ge(w_ready, i * SEG[name]["units"] + (g - 1))

            for r in range(RT):
                sp.dma_start(acc[:, r, :], x[r * P:(r + 1) * P, :]).then_inc(x_in, 16)
            for c, (u, slot, _, _) in enumerate(SEG["in"]["rows"]):
                room("in", None, c)
                if c < 6:
                    col = c * P if c < 4 else 1024 + (c - 4) * P
                    sp.dma_start(raw_k(slot, 0, 8), w_in_t[:, :, col:col + P]).then_inc(raw_in[slot], 16)
                else:
                    for hh in range(2):
                        col = 512 + 64 * (c - 6) + 256 * hh
                        sp.dma_start(raw_k(slot, 0, 8)[:, :, 64 * hh:64 * hh + 64],
                                     w_in_t[:, :, col:col + 64]).then_inc(raw_in[slot], 16)
            sp.wait_ge(tp_done, TPJ["o1"] + 8)
            sp.wait_ge(yp_lo, 4)
            for r in range(RT):
                sp.dma_start(acc[:, r, :], x[r * P:(r + 1) * P, :]).then_inc(x_back[r], 16)
            for c, (u, slot, _, _) in enumerate(SEG["out"]["rows"]):
                room("out", None, c)
                sp.dma_start(raw[:, slot, 0:D], w_out[c * P:(c + 1) * P, :]).then_inc(raw_in[slot], 16)
            with sp.Fori(0, SEG["ff"]["n"]) as i:
                for c, (u, slot, _, _) in enumerate(SEG["ff"]["rows"]):
                    room("ff", i, c)
                    if u == "S":
                        sp.dma_start(raw_k(slot, 0, 8), ff1_t[:, :, ds((i * 4 + c) * P, P)]).then_inc(raw_in[slot], 16)
                    else:
                        sp.dma_start(raw[:, slot, 0:D], w_ff2[ds((i * 4 + (c - 4)) * P, P), :]).then_inc(raw_in[slot], 16)
            with sp.Fori(0, SEG["gate"]["n"]) as i:
                for c, (u, slot, _, _) in enumerate(SEG["gate"]["rows"]):
                    room("gate", i, c)
                    sp.dma_start(raw_k(slot, 0, 8), gate_t[:, :, ds((i * 2 + c) * P, P)]).then_inc(raw_in[slot], 16)
                    sp.dma_start(raw_k(slot, 8, 10), ple_t[:, :, ds((i * 2 + c) * P, P)]).then_inc(raw_in[slot], 16)
            for name, base in (("in2a", 0), ("in2b", 1536)):
                with sp.Fori(0, SEG[name]["n"]) as i:
                    for c, (u, slot, _, _) in enumerate(SEG[name]["rows"]):
                        room(name, i, c)
                        col = i * (2 * P) + (base + (c // 3) * P + (c % 3) * 512)
                        sp.dma_start(raw_k(slot, 0, 8), in2_t[:, :, ds(col, P)]).then_inc(raw_in[slot], 16)
            for c, (u, slot, _, _) in enumerate(SEG["out2"]["rows"]):
                room("out2", None, c)
                sp.dma_start(raw[:, slot, 0:D], w_out2[c * P:(c + 1) * P, :]).then_inc(raw_in[slot], 16)

            def up_units(name, i, i0):
                nh = sum(r_[0] == "S" for r_ in SEG[name]["rows"]) // 2
                for c, (u, slot, _, _) in enumerate(SEG[name]["rows"]):
                    room(name, None if isinstance(i, int) else i, c)
                    if u == "S":
                        col = i * (4 * P) + ((c // 2) * P + (c % 2) * DFF2 + i0 * 4 * P)
                        sp.dma_start(raw_k(slot, 0, 8), up_t[:, :, ds(col, P)]).then_inc(raw_in[slot], 16)
                    else:
                        row = i * (4 * P) + ((c - 2 * nh) * P + i0 * 4 * P)
                        sp.dma_start(raw[:, slot, 0:D], w_down[ds(row, P), :]).then_inc(raw_in[slot], 16)

            with sp.Fori(0, SEG["up"]["n"]) as i:
                up_units("up", i, 0)
            up_units("uplast", 0, SEG["up"]["n"])

        @block.gpsimd
        def _(pool):
            g_n = [0]

            def then(ins):
                g_n[0] += 1
                ins.then_inc(gsetup, 1)

            then(pool.memset(ident[:, :], 0.0))
            then(pool.memset(flip[:, :], 0.0))
            then(pool.memset(ones[:, :], 1.0))
            then(pool.memset(tri_f[:, :, :], 1.0))
            then(pool.memset(keep[:, :], 1.0))
            then(pool.memset(drop[:, :], 0.0))
            then(pool.memset(eps[:, 0:1], LN_EPS))
            then(pool.memset(eps[:, 1:2], RMS_EPS))
            then(pool.iota(wcnt_i[:, :], pattern=[[1, 16]], base=1, channel_multiplier=0))
            then(pool.iota(bias1[:, 0, :].bitcast(I32), pattern=[[1, 2 * P]], base=-P, channel_multiplier=-1))
            pool.wait_ge(gsetup, g_n[0])
            then(pool.tensor_copy(bias1[:, 7, :], bias1[:, 0, :].bitcast(I32)))
            then(pool.affine_select(out=ident[:, :], in_=ident[:, :], compare_op=ALU.not_equal, fill=1.0,
                                    base=0, pattern=[[-1, P]], channel_multiplier=1))
            then(pool.affine_select(out=flip[:, :], in_=flip[:, :], compare_op=ALU.not_equal, fill=1.0,
                                    base=-(P - 1), pattern=[[1, P]], channel_multiplier=1))
            then(pool.affine_select(out=tri_f[:, 0, :], in_=tri_f[:, 0, :], compare_op=ALU.is_ge, fill=0.0,
                                    base=0, pattern=[[-1, P]], channel_multiplier=1))
            then(pool.affine_select(out=tri_f[:, 1, :], in_=tri_f[:, 1, :], compare_op=ALU.is_gt, fill=0.0,
                                    base=0, pattern=[[1, P]], channel_multiplier=-1))
            then(pool.affine_select(out=keep[:, :], in_=keep[:, :], compare_op=ALU.is_gt, fill=0.0,
                                    base=0, pattern=[[1, P]], channel_multiplier=-1))
            then(pool.affine_select(out=drop[:, :], in_=drop[:, :], compare_op=ALU.is_gt, fill=-BIG,
                                    base=0, pattern=[[1, P]], channel_multiplier=-1))
            pool.wait_ge(gsetup, g_n[0])
            for h in range(8):
                if h == 7:
                    pool.wait_ge(gsetup, g_n[0])
                then(pool.tensor_scalar(bias1[:, h, :], bias1[:, 7, :], 2.0 ** -(h + 1), None, ALU.mult))
            pool.wait_ge(gsetup, g_n[0])
            then(pool.affine_select(out=bias1[:, :, :], in_=bias1[:, :, :], compare_op=ALU.is_ge, fill=-BIG,
                                    base=P, pattern=[[0, 8], [-1, 2 * P]], channel_multiplier=1))
            pool.wait_ge(gsetup, g_n[0])
            pool.affine_select(out=bias1[:, :, :], in_=bias1[:, :, :], compare_op=ALU.is_gt, fill=-BIG,
                               base=0, pattern=[[0, 8], [1, 2 * P]], channel_multiplier=-1).then_inc(consts, 1)

            def split(name, i, c):
                seg = SEG[name]
                u, slot, load, t = seg["rows"][c]
                g, size = UN[name] + c, (10 * P if name == "gate" else 8 * P)
                at = 0 if i is None else i

                def val(per, base):
                    return base if i is None else at * per + base
                pool.wait_ge(raw_in[slot], val(seg["per"][slot], load))
                if u == "M":
                    m = c - sum(r_[0] != "M" for r_ in seg["rows"])
                    j, ch = m % 4, CH[name] + m // 4
                    if name == "out" and m == 0:
                        pool.wait_ge(pv_done, 64)
                    if name == "out2" and m == 0:
                        pool.wait_ge(b_pv, 4 * NB)
                    if j == 0 and ch > 0:
                        pool.wait_ge(m_rows, val(8, 8 * ch))
                    hi, lo = mv_hi[:, j, :], mv_lo[:, j, :]
                else:
                    T = TILE[name] + t
                    if i is not None or T >= 2:
                        pool.wait_ge(tile_done, val(seg["tiles"], T - 1))
                    hi = st_hi[:, T % 2, 0:size // P, :].rearrange("p k n -> p (k n)")
                    lo = st_lo[:, T % 2, 0:size // P, :].rearrange("p k n -> p (k n)")
                src = raw[:, slot, 0:size]
                nk = size // P
                pool.tensor_tensor(hi.rearrange("p (k n) -> p k n", n=P), src.rearrange("p (k n) -> p k n", n=P),
                                   ones[:, :].unsqueeze(1).to_broadcast([P, nk, P]), ALU.mult).then_inc(split_hi, 1)
                pool.wait_ge(split_hi, val(seg["units"], g + 1))
                pool.tensor_tensor(lo, src, hi.bitcast(F32), ALU.subtract).then_inc(w_ready, 1)

            for name in order:
                if SEG[name]["n"] == 1:
                    for c in range(SEG[name]["units"]):
                        split(name, None, c)
                else:
                    with pool.Fori(0, SEG[name]["n"]) as i:
                        for c in range(SEG[name]["units"]):
                            split(name, i, c)

        @block.tensor
        def _(pe):
            pe.wait_ge(consts, 1)

            def passes(out_ap, a_hi, a_lo, b_hi, b_lo, start, stop, check=False):
                pe.matmul(out_ap, a_hi, b_hi, start=start, stop=False, skip_group_check=check)
                pe.matmul(out_ap, a_hi, b_lo, start=False, stop=False, skip_group_check=check)
                return pe.matmul(out_ap, a_lo, b_hi, start=False, stop=stop, skip_group_check=check)

            def transposes(name, src, kts, halves=(0, 1)):
                for half in halves:
                    for n, kt in enumerate(kts):
                        job = TPJ[name] + half * len(kts) + n
                        if job >= 4:
                            pe.wait_ge(tp_lo, job - 3)
                        for r in range(4):
                            last = pe.transpose(pt[:, job % 4, r * P:(r + 1) * P],
                                                src[:, half * 4 + r, kt * P:(kt + 1) * P], ident[:, :])
                        last.then_inc(tp_done, 1)

            def tile_mm(slot, nk=8):
                for half in range(2):
                    for k in range(nk):
                        last = passes(pd[:, slot, half * HB:(half + 1) * HB], st_hi[:, slot, k, :],
                                      st_lo[:, slot, k, :], actT_hi[:, k, half * HB:(half + 1) * HB],
                                      actT_lo[:, k, half * HB:(half + 1) * HB], k == 0, k == nk - 1)
                return last

            def tile(i, per_u, u, per_t, t, rows=None):
                pe.wait_ge(w_ready, i * per_u + (u + 1))
                if not isinstance(i, int) or t + per_t * i >= 2:
                    pe.wait_ge(t_free, i * per_t + (t - 1))
                if rows is not None:
                    pe.wait_ge(m_free, i * 8 + rows)
                tile_mm(t % 2).then_inc(tile_done, 1)

            def row_mm(r, hi, lo, ks, nk):
                slot = r % 2
                for n in range(2):
                    for j in range(nk):
                        last = passes(pd[:, slot, n * HB:(n + 1) * HB], hi[:, ks + j, r * P:(r + 1) * P],
                                      lo[:, ks + j, r * P:(r + 1) * P], mv_hi[:, j, n * HB:(n + 1) * HB],
                                      mv_lo[:, j, n * HB:(n + 1) * HB], j == 0, j == nk - 1)
                last.then_inc(m_rows, 1)

            def row(r, i, ch, hi, lo, ks, nk, tiles=None):
                if r < 2 and tiles is not None:
                    pe.wait_ge(t_free, tiles)
                if not isinstance(i, int) or 8 * (ch + i) + r >= 2:
                    pe.wait_ge(m_free, i * 8 + (8 * ch + r - 1))
                row_mm(r, hi, lo, ks, nk)

            pe.wait_ge(x_in, 16 * RT)
            transposes("x", acc, range(8))

            def pool_mix(g):
                pe.wait_ge(d_ready, g + 1)
                pe.wait_ge(pw_split, 1)
                if g:
                    pe.wait_ge(pool_out, g)
                for half in range(2):
                    last = passes(pt[:, half, :], pwr_hi[:, g, :], pwr_lo[:, g, :],
                                  d_hi[:, half * HB:(half + 1) * HB], d_lo[:, half * HB:(half + 1) * HB],
                                  True, True)
                last.then_inc(pool_mm, 1)

            def v_rows(t, n, i=0, per=0):
                pe.wait_ge(t_free, i * 6 + (t + 1))
                for r in range(RT):
                    last = pe.transpose(pt[:, 2 + r // 4, (r % 4) * P:(r % 4 + 1) * P],
                                        evac_att[:, t % 2, r * P:(r + 1) * P], ident[:, :])
                last.then_inc(v_done, 1)

            def soft_pair(W, prob, pT_hi, pT_lo, st, i=0, per=0):
                def scores(s):
                    hh, qt = s // 8, s % 8
                    n = min(qt, W - 1) + 1
                    k0 = (qt - n + 1) * P
                    if s >= 2:
                        pe.wait_ge(pt_lo_s, i * per + (st + s - 1))
                    b = slice(64 * hh, 64 * hh + 64)
                    for c0 in range(0, n * P, HB):
                        c1 = min(c0 + HB, n * P)
                        last = passes(pd[:, s % 2, c0:c1], q_hi[b, qt * P:(qt + 1) * P],
                                      q_lo[b, qt * P:(qt + 1) * P], k_hi[b, k0 + c0:k0 + c1],
                                      k_lo[b, k0 + c0:k0 + c1], True, True)
                    last.then_inc(s_done, 1)

                def turn(s):
                    pe.wait_ge(p_ready, i * per + (st + s + 1))
                    for j in range(min(s % 8, W - 1) + 1):
                        last = pe.transpose(pd[:, s % 2, j * P:(j + 1) * P],
                                            prob[:, s % 2, j * P:(j + 1) * P], ident[:, :])
                    last.then_inc(pt_done, 1)

                def outputs(s):
                    hh, qt = s // 8, s % 8
                    n = min(qt, W - 1) + 1
                    pe.wait_ge(pt_lo_s, i * per + (st + s + 1))
                    for j in range(n):
                        kt = qt - n + 1 + j
                        last = passes(pt[:, hh, qt * 64:(qt + 1) * 64], pT_hi[:, s % 2, j * P:(j + 1) * P],
                                      pT_lo[:, s % 2, j * P:(j + 1) * P], v_hi[:, kt, 64 * hh:64 * hh + 64],
                                      v_lo[:, kt, 64 * hh:64 * hh + 64], j == 0, j == n - 1)
                    last.then_inc(pv_done, 1)

                scores(0)
                for s in range(16):
                    if s + 1 < 16:
                        scores(s + 1)
                    turn(s)
                    if s:
                        outputs(s - 1)
                outputs(15)

            pe.wait_ge(tp_lo, TPJ["x"] + 16)
            for t in range(6):
                tile(0, 0, t, 0, t)
                if t == 5:
                    pool_mix(3)
                elif 1 <= t <= 3:
                    pool_mix(t - 1)
            v_rows(5, 0)
            for j in range(4):
                if j:
                    pe.wait_ge(x_used, 6 + j)
                tile(0, 0, 6 + j, 0, 6 + j)
                pe.wait_ge(x_used, 7 + j)
                soft_pair(W1, prob1, pT1_hi, pT1_lo, 16 * j)
            pe.wait_ge(o_done, 4)
            transposes("o1", o1, range(4))

            def out_chunks(ch, u, hi, lo, name, tiles):
                for c in range(2):
                    pe.wait_ge(w_ready, u + 4 * c + 4)
                    for r in range(RT):
                        row(r, 0, ch + c, hi, lo, 4 * c, 4, tiles)
                        if c == 1 and name and r == 5:
                            pe.wait_ge(row_done, row_base(name) + 4)
                            transposes(name, acc, range(8), (0,))
                if name:
                    pe.wait_ge(row_done, row_base(name) + 8)
                    transposes(name, acc, range(8), (1,))

            pe.wait_ge(yp_lo, 4)
            pe.wait_ge(tp_lo, TPJ["o1"] + 8)
            out_chunks(0, UN["out"], actT_hi, actT_lo, "h1", 10)

            pe.wait_ge(tp_lo, TPJ["h1"] + 16)

            def ff_chunk(i):
                for j in range(4):
                    tile(i, 8, UN["ff"] + j, 4, TILE["ff"] + j, 16 if j < 2 else None)
                pe.wait_ge(x_used, i * 4 + (TILE["ff"] + 4))
                pe.wait_ge(w_ready, i * 8 + (UN["ff"] + 8))
                for r in range(RT):
                    if r < 2:
                        pe.wait_ge(t_free, i * 4 + (TILE["ff"] + 4))
                    row(r, i, CH["ff"], hid_hi, hid_lo, 0, 4)
                    if r == 0:
                        pe.wait_ge(ada_full, i + 1)
                        for j in range(AW // P):
                            last = pe.matmul(pt[:, 3, j:j + 1], ada_acc[:, j * P:(j + 1) * P], ones[:, 0:1],
                                             start=True, stop=True)
                        last.then_inc(ada_mm, 1)
                    if isinstance(i, int) and r == 5:
                        pe.wait_ge(row_done, 12)
                        transposes("h2", acc, range(8), (0,))

            with pe.Fori(0, 7) as i:
                ff_chunk(i)
            ff_chunk(7)
            pe.wait_ge(row_done, 16)
            transposes("h2", acc, range(8), (1,))
            pe.wait_ge(p_in, 16)
            transposes("p", p_rows, range(2))
            pe.wait_ge(tp_lo, TPJ["p"] + 4)

            def gate_tile(i, c):
                pe.wait_ge(w_ready, i * 2 + (UN["gate"] + c + 1))
                pe.wait_ge(m_free, 80)
                pe.wait_ge(ple_free, i * 2 + (c + 1))
                for half in range(2):
                    for k in range(2):
                        last = passes(pd[:, 0, half * HB:(half + 1) * HB], st_hi[:, c, 8 + k, :],
                                      st_lo[:, c, 8 + k, :], hid_hi[:, k, half * HB:(half + 1) * HB],
                                      hid_lo[:, k, half * HB:(half + 1) * HB], k == 0, k == 1)
                last.then_inc(ple_done, 1)
                pe.wait_ge(t_free, i * 2 + (TILE["gate"] + c))
                for half in range(2):
                    for k in range(8):
                        last = passes(pd[:, 1, half * HB:(half + 1) * HB], st_hi[:, c, k, :],
                                      st_lo[:, c, k, :], actT_hi[:, k, half * HB:(half + 1) * HB],
                                      actT_lo[:, k, half * HB:(half + 1) * HB], k == 0, k == 7)
                last.then_inc(tile_done, 1)

            def gate_back(i, c):
                pe.wait_ge(gp_ready, i * 2 + (c + 2))
                pe.wait_ge(x_used, i * 2 + (TILE["gate"] + c - 1))
                for r in range(RT):
                    last = pe.transpose(pt[:, 2 * c + r // 4, (r % 4) * P:(r % 4 + 1) * P],
                                        gprod[:, c, r * P:(r + 1) * P], ident[:, :])
                last.then_inc(gp_mm, 1)

            with pe.Fori(0, 4) as i:
                gate_tile(i, 0)
                gate_tile(i, 1)
                gate_back(i, 0)
                gate_back(i, 1)

            pe.wait_ge(row_rd, 1)
            transposes("m1", rows2, range(8))
            pe.wait_ge(tp_lo, TPJ["m1"] + 16)

            def proj(name, i, pp):
                for c in range(3):
                    tile(i, 6, UN[name] + 3 * pp + c, 6, TILE[name] + 3 * pp + c)
                v_rows(TILE[name] + 3 * pp + 2, 0, i)
                pe.wait_ge(x_used, i * 6 + (TILE[name] + 3 * pp + 3))

            def bias_flip(i, pp):
                pe.wait_ge(bias_in, i * 32 + (16 * pp + 16))
                for hh in range(2):
                    if hh:
                        pe.wait_ge(bias_cp, i * 4 + (2 * pp + hh))
                    for c0 in range(0, NA, HB):
                        c1 = min(c0 + HB, NA)
                        last = pe.matmul(pt[:, 2 + c0 // HB, 0:c1 - c0], flip[:, :], bias_up[:, hh, c0:c1],
                                         start=True, stop=True)
                    last.then_inc(bias_mm, 1)

            with pe.Fori(0, 2) as i:
                for pp in range(2):
                    proj("in2a", i, pp)
                    bias_flip(i, pp)
                    pe.wait_ge(bias_rdy, i * 4 + (2 * pp + 2))
                    soft_pair(WA, prob2, pT2_hi, pT2_lo, 64 + 16 * pp, i, 32)

            def stick_pair(i, pp):
                st, per = NB * pp, 2 * NB

                def at(sem_, n):
                    pe.wait_ge(sem_, i * per + (st + n))

                def seg(s):
                    return BSTEPS[s][0] * 2 + BSTEPS[s][1]

                def scores(s):
                    hh, hf, kt = BSTEPS[s]
                    q0, n, _ = bcols(hf, kt)
                    if s >= 2:
                        at(b_l, s - 1)
                    b = slice(64 * hh, 64 * hh + 64)
                    passes(pd[:, s % 2, 0:n], k_hi[b, kt * P:(kt + 1) * P], k_lo[b, kt * P:(kt + 1) * P],
                           q_hi[b, q0:q0 + n], q_lo[b, q0:q0 + n], True, True).then_inc(b_s, 1)

                def sums_of(s, which, sm):
                    hh, hf, kt = BSTEPS[s]
                    _, n, co = bcols(hf, kt)
                    first = which == 0 and (s == 0 or seg(s) != seg(s - 1))
                    o = pt[:, 2 + seg(s) % 2, co:co + n]
                    pe.matmul(o, tri[:, which, :], sp_hi[:, s % 2, 0:n], start=first, stop=False,
                              skip_group_check=True)
                    last = pe.matmul(o, tri[:, which, :], sp_lo[:, s % 2, 0:n], start=False, stop=True,
                                     skip_group_check=True)
                    if sm is not None:
                        last.then_inc(sm, 1)

                def outputs(s):
                    hh, hf, kt = BSTEPS[s]
                    q0, n, _ = bcols(hf, kt)
                    at(b_ws, s + 1)
                    for j in range(n // P):
                        qt = q0 // P + j
                        last = passes(pt[:, hh, qt * 64:(qt + 1) * 64], wt_hi[:, s % 2, j * P:(j + 1) * P],
                                      wt_lo[:, s % 2, j * P:(j + 1) * P], v_hi[:, kt, 64 * hh:64 * hh + 64],
                                      v_lo[:, kt, 64 * hh:64 * hh + 64], s % 12 == 0 and j == 0, False, True)
                    last.then_inc(b_pv, 1)

                scores(0)
                for s in range(NB + 2):
                    if s + 1 < NB:
                        scores(s + 1)
                    if 2 <= s:
                        at(b_sub, s - 1)
                        if s - 1 < NB and seg(s - 1) == seg(s - 2):
                            sums_of(s - 2, 1, None)
                    if 1 <= s <= NB:
                        at(b_sp, s)
                        sums_of(s - 1, 0, b_c)
                    if 2 <= s:
                        outputs(s - 2)

            with pe.Fori(0, 2) as i:
                for pp in range(2):
                    proj("in2b", i, pp)
                    stick_pair(i, pp)

            for n in range(16):
                pe.wait_ge(diag_rdy, n + 1)
                if n == 0:
                    pe.wait_ge(o_done, 12)
                pe.matmul(pt[:, n // 4, (n % 4) * P:(n % 4 + 1) * P], ones[:, :], diag[:, :],
                          start=True, stop=True).then_inc(bc_mm, 1)
            pe.wait_ge(row_rd, 2)
            pe.wait_ge(gb_rows, 2)
            transposes("o2", rows2, range(8))
            pe.wait_ge(tp_lo, TPJ["o2"] + 16)
            out_chunks(CH["out2"], UN["out2"], actT_hi, actT_lo, None, TILE["up"])
            pe.wait_ge(row_rd, 3)
            transposes("m2", rows2, range(8))
            pe.wait_ge(tp_lo, TPJ["m2"] + 16)

            def up_chunk(name, i, nh):
                for j in range(2 * nh):
                    tile(i, 12, UN[name] + j, 8, TILE[name] + j, 8 * CH[name] if j < 2 else None)
                pe.wait_ge(x_used, i * 8 + (TILE[name] + 2 * nh))
                pe.wait_ge(w_ready, i * 12 + (UN[name] + 3 * nh))
                for r in range(RT):
                    if r < 2:
                        pe.wait_ge(t_free, i * 8 + (TILE[name] + 2 * nh))
                    row(r, i, CH[name], hid_hi, hid_lo, 0, nh)

            with pe.Fori(0, 5) as i:
                up_chunk("up", i, 4)
            up_chunk("uplast", 0, 2)

        @block.scalar
        def _(act):
            def vec(out_ap, in_ap):
                act.dma_start(out_ap, in_ap).then_inc(vecs, 16)

            def spread(a, off, n):
                return bass.AP(a.tensor, off, [[0, P], [1, n]])

            vec(pw[:, :, :], w_pool.rearrange("g c d -> c g d"))
            vec(pscale[:, :], pool_scale[0].rearrange("(g p) -> p g", p=P))
            vec(sink[:, :], spread(attn_sinks, 0, 8))
            vec(c_col[:, :], c_2[0].rearrange("(k p) -> p k", p=P))
            vec(b_ada[:, :], b_ada_2[0].rearrange("(k p) -> p k", p=P))
            vec(b_gate[:, :], b_ple_gate[0].rearrange("(k p) -> p k", p=P))
            vec(gab[:, 0:4], g_a_2[0].rearrange("(k p) -> p k", p=P))
            vec(gab[:, 4:8], g_b_2[0].rearrange("(k p) -> p k", p=P))
            vec(cw[:, :, :], conv_w_2[0].rearrange("w (k p) -> p w k", p=P))
            vec(cb[:, :], conv_b_2[0].rearrange("(k p) -> p k", p=P))

            act.wait_ge(act_one, 1)
            act.activation(tmp512[:, :], eps_one[:, :], ACT.Copy).then_inc(ple_free, 1)

            def tp_plain(name, n, hi_of, lanes=1):
                for b in n:
                    job = TPJ[name] + b
                    act.wait_ge(tp_done, job + 1)
                    act.activation(hi_of(b), pt[:, job % 4, :], ACT.Copy).then_inc(tp_hi, 1)

            def tp_scaled(name, scale_of, bias_of):
                for b in range(16):
                    job = TPJ[name] + b
                    act.wait_ge(tp_done, job + 1)
                    if b >= 2:
                        act.wait_ge(tp_lo, job - 1)
                    kt = b % 8
                    bias = bias_of(kt) if bias_of else 0.0
                    act.activation(evac[:, 0, (b % 2) * HB:(b % 2 + 1) * HB], pt[:, job % 4, :], ACT.Identity,
                                   bias=bias, scale=scale_of(kt)).then_inc(tp_hi, 1)

            def to_actT(nk, k0=0):
                def f(b):
                    half, kt = b // nk, b % nk
                    return actT_hi[:, k0 + kt, half * HB:(half + 1) * HB]
                return f

            def tile_out(i, per, t, buf, func=ACT.Copy, **kw):
                act.wait_ge(tile_done, i * per + (t + 1))
                if not isinstance(i, int) or t + per * i >= 2:
                    act.wait_ge(x_used, i * per + (t - 1))
                act.activation(buf[:, t % 2, :], pd[:, t % 2, :], func, **kw).then_inc(t_free, 1)

            tp_plain("x", range(16), to_actT(8))
            act.wait_ge(vecs, 16 * 10)
            act.activation(c_act[:, :], c_col[:, :], ACT.Sigmoid).then_inc(c_ready, 1)
            for t in range(5):
                tile_out(0, 0, t, evac_att)
                if t:
                    act.wait_ge(pool_mm, t)
                    act.activation(ypool[:, t - 1, :], pt[:, 0:2, :].rearrange("p a b -> p (a b)"), ACT.Copy,
                                   scale=pscale[:, t - 1:t]).then_inc(pool_out, 1)
            tile_out(0, 0, 5, evac_att)

            def soft_pair(prob, pT_hi, W, st, sinks, i=0, per=0):
                def exps(s):
                    n = (min(s % 8, W - 1) + 1) * P
                    act.wait_ge(nm_ready, i * per + (st + s + 1))
                    act.activation(prob[:, s % 2, 0:n], prob[:, s % 2, 0:n], ACT.Exp, bias=nmx[:, s:s + 1],
                                   accum_out=den[:, s:s + 1]).then_inc(p_ready, 1)

                def parts(s):
                    n = (min(s % 8, W - 1) + 1) * P
                    act.wait_ge(pt_done, i * per + (st + s + 1))
                    if s >= 2:
                        act.wait_ge(pv_done, i * per + (st + s - 1))
                    act.activation(pT_hi[:, s % 2, 0:n], pd[:, s % 2, 0:n], ACT.Copy).then_inc(pt_hi_s, 1)

                for s in range(16):
                    exps(s)
                    if s:
                        parts(s - 1)
                parts(15)
                if sinks is not None:
                    for hh in range(2):
                        h = sinks + 4 * hh
                        act.activation(sden[:, 8 * hh:8 * hh + 8], nmx[:, 8 * hh:8 * hh + 8], ACT.Exp,
                                       bias=sink[:, h:h + 1]).then_inc(sink_e, 1)

            for j in range(4):
                tile_out(0, 0, 6 + j, evac_att, scale=QSCALE)
                soft_pair(prob1, pT1_hi, W1, 16 * j, j)
            act.wait_ge(o_done, 4)
            act.dma_start(row_a[:, :], spread(ln1_g, 0, D)).then_inc(gb_in, 16)
            act.dma_start(row_b[:, :], spread(ln1_b, 0, D)).then_inc(gb_in, 16)
            act.wait_ge(tile_done, 10)
            for g in range(4):
                act.activation(actT_hi[:, g, :], ypool[:, g, :], ACT.Copy).then_inc(yp_hi, 1)
            tp_plain("o1", range(8), to_actT(4, 4))

            def std_of(n):
                act.wait_ge(stat_in, n + 1)
                act.activation(std[:, :], mv2[:, 1:2], ACT.Sqrt, bias=eps[:, 0:1]).then_inc(std_done, 1)

            def norm_rows(name, base):
                for r in range(6):
                    std_of(base + r)
                tp_plain(name, range(8), to_actT(8))
                std_of(base + 6)
                std_of(base + 7)

            norm_rows("h1", 0)
            tp_plain("h1", range(8, 16), to_actT(8))
            act.dma_start(row_a[:, :], spread(ln2_g, 0, D)).then_inc(gb_in, 16)
            act.dma_start(row_b[:, :], spread(ln2_b, 0, D)).then_inc(gb_in, 16)

            def ff_tiles(i):
                for j in range(4):
                    tile_out(i, 4, TILE["ff"] + j, evac, ACT.Relu)
                    for k in (2 * j, 2 * j + 1):
                        act.wait_ge(ada_used, i * 8 + (k + 1))
                        act.dma_start(ada_raw[:, k % 2, :], w_ada[k * P:(k + 1) * P, ds(i * AW, AW)])\
                            .then_inc(ada_in[k % 2], 16)

            with act.Fori(0, 7) as i:
                ff_tiles(i)
            ff_tiles(7)
            norm_rows("h2", 8)
            act.wait_ge(m_rows, 80)
            act.dma_start(p_rows[:, :, :], p.rearrange("(r q) n -> q r n", q=P)).then_inc(p_in, 16)
            tp_plain("h2", range(8, 16), to_actT(8))
            tp_plain("p", range(4), lambda b: hid_hi[:, b % 2, (b // 2) * HB:(b // 2 + 1) * HB])

            def gate_out(i, c):
                act.wait_ge(ple_done, i * 2 + (c + 1))
                act.wait_ge(gp_ready, i * 2 + (c + 1))
                act.activation(evac[:, 0, :], pd[:, 0, :], ACT.Copy).then_inc(ple_free, 1)
                act.wait_ge(tile_done, i * 2 + (TILE["gate"] + c + 1))
                act.activation(evac[:, 1, :], pd[:, 1, :], ACT.Sigmoid,
                               bias=b_gate[:, ds(i * 2 + c, 1)]).then_inc(t_free, 1)

            with act.Fori(0, 4) as i:
                gate_out(i, 0)
                gate_out(i, 1)

            def row_squares(n0):
                for r in range(RT):
                    act.activation(rows2[:, r, :], acc[:, r, :], ACT.Square,
                                   accum_out=ssq[:, r:r + 1]).then_inc(sq_done, 1)
                act.wait_ge(sq_done, n0 + RT)
                act.activation(rms[:, 0:8], ssq[:, 0:8], ACT.Sqrt, bias=eps[:, 1:2], scale=1.0 / D)\
                    .then_inc(ss_done, 1)

            act.wait_ge(x_used, TILE["in2a"])
            row_squares(0)
            tp_scaled("m1", lambda k: modT[:, 8 + k:9 + k], lambda k: modT[:, k:k + 1])

            def proj_out(name, i, pp):
                t = TILE[name] + 3 * pp
                tile_out(i, 6, t, evac_att, scale=QSCALE)
                tile_out(i, 6, t + 1, evac_att)
                tile_out(i, 6, t + 2, evac_att)

            rel_ap = rel_rev
            act.dma_start(ext.ap()[:, 511:767], rel_ap[:, 0:256]).then_inc(ext_in, 16)
            act.dma_start(ext.ap()[:, 0:511].unsqueeze(2), bass.AP(rel_rev.tensor, 0, [[257, 8], [0, 511], [1, 1]])).then_inc(ext_in, 16)
            act.wait_ge(ext_in, 32)
            with act.Fori(0, 2) as i:
                for pp in range(2):
                    act.dma_start(bias_up[:, :, :], bass.AP(ext, i * (4 * 768) + 2 * pp * 768,
                                                            [[1, P], [768, 2], [1, NA]])).then_inc(bias_in, 16)
                    proj_out("in2a", i, pp)
                    for hh in range(2):
                        act.wait_ge(bias_mm, i * 4 + (2 * pp + hh + 1))
                        act.activation(bias2[:, hh, :], pt[:, 2:4, :].rearrange("p a b -> p (a b)")[:, 0:NA],
                                       ACT.Copy).then_inc(bias_cp, 1)
                    soft_pair(prob2, pT2_hi, WA, 64 + 16 * pp, None, i, 32)

            def stick_pair(i, pp):
                st, per = NB * pp, 2 * NB

                def at(sem_, n):
                    act.wait_ge(sem_, i * per + (st + n))

                def cols(s):
                    return bcols(*BSTEPS[s][1:])[1]

                for s in range(NB + 2):
                    if s < NB:
                        n = cols(s)
                        at(b_s, s + 1)
                        if s >= 3:
                            at(b_ws, s - 2)
                        act.activation(logit[:, s % 3, 0:n], pd[:, s % 2, 0:n], ACT.Copy).then_inc(b_l, 1)
                    if s >= 2:
                        at(b_sub, s - 1)
                        n = cols(s - 2)
                        act.activation(logit[:, (s - 2) % 3, 0:n], logit[:, (s - 2) % 3, 0:n], ACT.Exp)\
                            .then_inc(b_w, 1)
                    if s < NB:
                        n = cols(s)
                        at(b_t, s + 1)
                        act.activation(soft[:, s % 2, 0:n], soft[:, s % 2, 0:n], ACT.Exp).then_inc(b_exp, 1)
                        at(b_exp, s + 1)
                        act.activation(soft[:, s % 2, 0:n], soft[:, s % 2, 0:n], ACT.Ln, bias=1.0)\
                            .then_inc(b_ln, 1)

            with act.Fori(0, 2) as i:
                for pp in range(2):
                    proj_out("in2b", i, pp)
                    stick_pair(i, pp)

            act.wait_ge(o_done, 12)
            for n in range(16):
                r, h = n // 2, n % 2
                if n >= 2:
                    act.wait_ge(sq_done, 8 + n - 1)
                act.activation(evac[:, 0, 0:HB] if n % 2 else evac[:, 0, HB:D], rows2[:, r, h * HB:(h + 1) * HB],
                               ACT.Square, accum_out=ssq[:, n:n + 1]).then_inc(sq_done, 1)
            act.wait_ge(sq_done, 24)
            act.activation(rms[:, 0:16], ssq[:, 0:16], ACT.Sqrt, bias=eps[:, 1:2], scale=1.0 / HB)\
                .then_inc(ss_done, 1)
            act.wait_ge(bc_mm, 16)
            ptf = pt[:, :, :].rearrange("p a b -> p (a b)")
            act.activation(row_a[:, :], ptf[:, 0:D], ACT.Copy).then_inc(gb_rows, 1)
            act.activation(row_b[:, :], ptf[:, D:2 * D], ACT.Copy).then_inc(gb_rows, 1)
            tp_scaled("o2", lambda k: gab[:, k:k + 1], None)
            act.wait_ge(row_done, 24)
            row_squares(24)
            tp_scaled("m2", lambda k: modT[:, 32 + k:33 + k], lambda k: modT[:, 24 + k:25 + k])

            def up_out(name, i, nh):
                for j in range(nh):
                    t = TILE[name] + 2 * j
                    tile_out(i, 8, t, evac)
                    tile_out(i, 8, t + 1, evac)
                    act.wait_ge(cv_done, i * 4 + (UPH[name] + j + 1))
                    act.activation(cv[:, 0, :], cv[:, 0, :], ACT.Silu).then_inc(silu_done, 1)

            with act.Fori(0, 5) as i:
                up_out("up", i, 4)
            up_out("uplast", 0, 2)
            act.wait_ge(x_used, TILE["uplast"] + 4)
            act.dma_start(row_g[:, :], spread(final_g_2, 0, D)).then_inc(g_in, 16)
            def store(r):
                act.wait_ge(fin_rdy, r + 1)
                act.dma_start(out[r * P:(r + 1) * P, :], evac[:, r % 2, :]).then_inc(stored[r % 2], 16)

            for r in range(RT):
                act.wait_ge(row_done, 24 + r + 1)
                act.activation(sq_junk[:, :], acc[:, r, :], ACT.Square,
                               accum_out=ssq[:, r:r + 1]).then_inc(sq_done, 1)
                act.wait_ge(sq_done, 32 + r + 1)
                act.activation(rms[:, r:r + 1], ssq[:, r:r + 1], ACT.Sqrt, bias=eps[:, 1:2], scale=1.0 / D)\
                    .then_inc(ss_done, 1)
                if r:
                    store(r - 1)
            store(RT - 1)
            act.wait_ge(stored[0], 64)
            act.wait_ge(stored[1], 64)

        @block.vector
        def _(dve):
            ch = Chain(dve, vchain)
            link = ch.link

            def split(hi, lo, src, sem_):
                link(dve.tensor_copy(hi, src))
                dve.tensor_tensor(lo, src, hi.bitcast(F32), ALU.subtract).then_inc(sem_, 1)

            dve.wait_ge(consts, 1)
            dve.memset(eps_one[:, :], 1.0).then_inc(act_one, 1)
            link(dve.tensor_copy(tri[:, :, :], tri_f[:, :, :]))
            link(dve.tensor_copy(wcount[:, :], wcnt_i[:, :]))
            link(dve.reciprocal(wcount[:, :], wcount[:, :]))

            def tp_lo_plain(name, n, hi_of, lo_of):
                for b in n:
                    job = TPJ[name] + b
                    dve.wait_ge(tp_hi, job + 1)
                    dve.tensor_tensor(lo_of(b), pt[:, job % 4, :], hi_of(b).bitcast(F32), ALU.subtract)\
                        .then_inc(tp_lo, 1)

            def tp_lo_scaled(name):
                for b in range(16):
                    job = TPJ[name] + b
                    half, kt = b // 8, b % 8
                    c = slice(half * HB, (half + 1) * HB)
                    dve.wait_ge(tp_hi, job + 1)
                    split(actT_hi[:, kt, c], actT_lo[:, kt, c], evac[:, 0, (b % 2) * HB:(b % 2 + 1) * HB], tp_lo)

            def T(t_, nk, k0=0):
                return lambda b: t_[:, k0 + b % nk, (b // nk) * HB:(b // nk + 1) * HB]

            tp_lo_plain("x", range(16), T(actT_hi, 8), T(actT_lo, 8))
            dve.wait_ge(vecs, 16 * 10)
            split(pwr_hi[:, :, :], pwr_lo[:, :, :], pw[:, :, :], pw_split)
            dve.wait_ge(c_ready, 1)
            dve.tensor_tensor(c_act[:, :], c_act[:, :], c_col[:, :], ALU.mult).then_inc(ada_used, 2)
            for g in range(4):
                dve.wait_ge(t_free, g + 1)
                u = evac_att[:, g % 2, :]
                if g:
                    dve.wait_ge(d_ready, g)
                src, w = u, 1
                for step in range(g + 1):
                    dst = sums[:, step % 2, :]
                    link(dve.tensor_copy(dst[:, 0:w], src[:, 0:w]))
                    link(dve.tensor_tensor(dst[:, w:S], src[:, w:S], src[:, 0:S - w], ALU.add))
                    src, w = dst, 2 * w
                link(dve.tensor_tensor(src[:, 0:w], src[:, 0:w], wcount[:, 0:w], ALU.mult))
                link(dve.tensor_tensor(src[:, 0:w], src[:, 0:w], u[:, 0:w], ALU.subtract))
                link(dve.scalar_tensor_tensor(out=src[:, w:S], in0=src[:, w:S], scalar=1.0 / w, in1=u[:, w:S],
                                              op0=ALU.mult, op1=ALU.subtract))
                dve.sem_inc(x_used, 1)
                if g:
                    dve.wait_ge(pool_mm, g)
                split(d_hi[:, :], d_lo[:, :], src, d_ready)
            dve.wait_ge(t_free, 5)
            split(k_hi[:, :], k_lo[:, :], evac_att[:, 0, :], x_used)

            def v_split(i, n, per):
                dve.wait_ge(v_done, i * per + n)
                split(v_hi[:, :, :].rearrange("p a b -> p (a b)"), v_lo[:, :, :].rearrange("p a b -> p (a b)"),
                      pt[:, 2:4, :].rearrange("p a b -> p (a b)"), x_used)

            v_split(0, 1, 0)

            def soft_pair(prob, pT_hi, pT_lo, W, bias_ap, st, sinks, o_out, i=0, per=0):
                def top(s):
                    n = (min(s % 8, W - 1) + 1) * P
                    dve.wait_ge(s_done, i * per + (st + s + 1))
                    if s >= 2:
                        dve.wait_ge(pt_done, i * per + (st + s - 1))
                    dve.memset(nmx[:, s:s + 1], 0.0)
                    link(dve.tensor_tensor_reduce(out=prob[:, s % 2, 0:n], in0=pd[:, s % 2, :][:, 0:n],
                                                  in1=bias_ap(s // 8)[:, W * P - n:W * P], scale=1.0,
                                                  scalar=-3e38, op0=ALU.add, op1=ALU.max,
                                                  accum_out=mx[:, s:s + 1]))
                    if sinks is None:
                        dve.tensor_scalar(nmx[:, s:s + 1], mx[:, s:s + 1], -1.0, None, ALU.mult)\
                            .then_inc(nm_ready, 1)
                    else:
                        h = sinks + 4 * (s // 8)
                        dve.tensor_scalar(nmx[:, s:s + 1], mx[:, s:s + 1], sink[:, h:h + 1], -1.0,
                                          ALU.max, ALU.mult).then_inc(nm_ready, 1)

                def low(s):
                    n = (min(s % 8, W - 1) + 1) * P
                    dve.wait_ge(pt_hi_s, i * per + (st + s + 1))
                    dve.tensor_tensor(pT_lo[:, s % 2, 0:n], pd[:, s % 2, 0:n], pT_hi[:, s % 2, 0:n].bitcast(F32),
                                      ALU.subtract).then_inc(pt_lo_s, 1)

                for s in range(16):
                    top(s)
                    if s:
                        low(s - 1)
                low(15)
                dve.wait_ge(pv_done, i * per + (st + 16))
                if sinks is not None:
                    dve.wait_ge(sink_e, 2 * (sinks + 1))
                    link(dve.tensor_tensor(den[:, :], den[:, :], sden[:, :], ALU.add))
                link(dve.reciprocal(rinv[:, :], den[:, :]))
                for hh in range(2):
                    last = dve.tensor_tensor(o_out(hh), pt[:, hh, :].rearrange("p (r c) -> p r c", c=64),
                                             rinv[:, 8 * hh:8 * hh + 8].unsqueeze(2).to_broadcast([P, 8, 64]),
                                             ALU.mult)
                last.then_inc(o_done, 1)

            for j in range(4):
                dve.wait_ge(t_free, 7 + j)
                split(q_hi[:, :], q_lo[:, :], evac_att[:, j % 2, :], x_used)
                soft_pair(prob1, pT1_hi, pT1_lo, W1, lambda hh: bias1[:, j + 4 * hh, :], 16 * j, j,
                          lambda hh: o1[:, :, (j + 4 * hh) * 64:(j + 4 * hh + 1) * 64])
            for g in range(4):
                dve.wait_ge(yp_hi, g + 1)
                dve.tensor_tensor(actT_lo[:, g, :], ypool[:, g, :], actT_hi[:, g, :].bitcast(F32), ALU.subtract)\
                    .then_inc(yp_lo, 1)
            tp_lo_plain("o1", range(8), T(actT_hi, 4, 4), T(actT_lo, 4, 4))

            def pdr(r):
                return pd[:, r % 2, :]

            def stat(r):
                link(dve.bn_stats(out=stats[:, 0, :], in_=acc[:, r, 0:HB]))
                link(dve.bn_stats(out=stats[:, 1, :], in_=acc[:, r, HB:D]))
                dve.bn_aggr(out=mv2[:, :], in_=stats[:, :, :]).then_inc(stat_in, 1)

            def finish(r, n):
                dve.wait_ge(std_done, n)
                link(dve.reciprocal(rstd[:, :], std[:, :]))
                link(dve.scalar_tensor_tensor(out=nmr[:, :], in0=mv2[:, 0:1], scalar=-1.0, in1=rstd[:, :],
                                              op0=ALU.mult, op1=ALU.mult))
                link(dve.tensor_scalar(acc[:, r, :], acc[:, r, :], rstd[:, :], nmr[:, :], ALU.mult, ALU.add))
                link(dve.tensor_tensor(acc[:, r, :], acc[:, r, :], row_a[:, :], ALU.mult))
                dve.tensor_tensor(acc[:, r, :], acc[:, r, :], row_b[:, :], ALU.add).then_inc(row_done, 1)

            def add_row(r, scale=None):
                if scale is None:
                    return dve.tensor_tensor(acc[:, r, :], acc[:, r, :], pdr(r), ALU.add)
                return dve.scalar_tensor_tensor(out=acc[:, r, :], in0=acc[:, r, :], scalar=scale, in1=pdr(r),
                                                op0=ALU.mult, op1=ALU.add)

            def norm_chunk(ch_, name, base, extra=None):
                for r in range(RT):
                    dve.wait_ge(m_rows, 8 * ch_ + r + 1)
                    add_row(r).then_inc(m_free, 1)
                    if r == 0 and extra:
                        extra()
                    dve.wait_ge(m_free, 8 * ch_ + r + 1)
                    stat(r)
                    finish(r, base + r + 1)
                    if r == 5:
                        tp_lo_plain(name, range(8), T(actT_hi, 8), T(actT_lo, 8))
                tp_lo_plain(name, range(8, 16), T(actT_hi, 8), T(actT_lo, 8))
                if name == "h1":
                    for r in range(RT):
                        link(dve.tensor_scalar(acc[:, r, :], acc[:, r, :], ALPHA, None, ALU.mult))

            for r in range(RT):
                dve.wait_ge(x_back[r], 16)
                dve.wait_ge(m_rows, r + 1)
                add_row(r, ALPHA).then_inc(m_free, 1)
            dve.wait_ge(gb_in, 32)
            dve.wait_ge(m_free, 8)
            norm_chunk(1, "h1", 0)

            def ff_tiles(i):
                for j in range(4):
                    t = TILE["ff"] + j
                    xs = evac[:, t % 2, :]
                    dve.wait_ge(t_free, i * 4 + (t + 1))
                    link(dve.tensor_tensor(xs, xs, xs, ALU.mult))
                    dve.wait_ge(m_rows, i * 8 + 16)
                    split(hid_hi[:, j, :], hid_lo[:, j, :], xs, x_used)
                    for k in (2 * j, 2 * j + 1):
                        dve.wait_ge(ada_in[k % 2], i * 64 + 16 * (k // 2 + 1))
                        if k == 0:
                            ins = dve.tensor_scalar(ada_acc[:, :], ada_raw[:, 0, :], c_act[:, 0:1], None, ALU.mult)
                        else:
                            ins = dve.scalar_tensor_tensor(out=ada_acc[:, :], in0=ada_raw[:, k % 2, :],
                                                           scalar=c_act[:, k:k + 1], in1=ada_acc[:, :],
                                                           op0=ALU.mult, op1=ALU.add)
                        ins.then_inc(ada_used, 1)
                        dve.wait_ge(ada_used, i * 8 + (k + 3))
                dve.sem_inc(ada_full, 1)

            def mod_cols(i):
                dve.wait_ge(ada_mm, i + 1)
                link(dve.tensor_tensor(modT[:, ds(i * 6, 6)], pt[:, 3, 0:6], b_ada[:, ds(i * 6, 6)], ALU.add))

            with dve.Fori(0, 7) as i:
                ch.enter(i, 4 * 2 + 1)
                ff_tiles(i)
                for r in range(RT):
                    dve.wait_ge(m_rows, i * 8 + (16 + r + 1))
                    add_row(r).then_inc(m_free, 1)
                    if r == 0:
                        mod_cols(i)
            ch.leave(7)
            ff_tiles(7)
            dve.wait_ge(gb_in, 64)
            dve.wait_ge(m_free, 72)

            def last_mod():
                mod_cols(7)
                link(dve.tensor_scalar(modT[:, 8:16], modT[:, 8:16], 1.0, None, ALU.add))
                link(dve.tensor_scalar(modT[:, 32:40], modT[:, 32:40], 1.0, None, ALU.add))

            norm_chunk(9, "h2", 8, last_mod)
            hp = [lambda b: hid_hi[:, b % 2, (b // 2) * HB:(b // 2 + 1) * HB],
                  lambda b: hid_lo[:, b % 2, (b // 2) * HB:(b // 2 + 1) * HB]]
            tp_lo_plain("p", range(4), *hp)
            dve.sem_inc(gp_ready, 1)

            def gate_prod(i, c):
                dve.wait_ge(t_free, i * 2 + (TILE["gate"] + c + 1))
                dve.wait_ge(ple_free, i * 2 + (c + 2))
                dve.tensor_tensor(gprod[:, c, :], evac[:, 0, :], evac[:, 1, :], ALU.mult).then_inc(gp_ready, 1)

            def gate_add(i, c):
                dve.wait_ge(gp_mm, i * 2 + (c + 1))
                col = acc[:, :, ds((i * 2 + c) * P, P)]
                dve.tensor_tensor(col, col, pt[:, 2 * c:2 * c + 2, :].rearrange("p a (b n) -> p (a b) n", n=P),
                                  ALU.add).then_inc(x_used, 1)

            with dve.Fori(0, 4) as i:
                gate_prod(i, 0)
                gate_prod(i, 1)
                gate_add(i, 0)
                gate_add(i, 1)

            def scaled_rows(n, rd):
                dve.wait_ge(ss_done, n)
                link(dve.reciprocal(rinv[:, 0:8], rms[:, 0:8]))
                for r in range(RT):
                    last = dve.tensor_scalar(rows2[:, r, :], acc[:, r, :], rinv[:, r:r + 1], None, ALU.mult)
                last.then_inc(row_rd, 1)

            scaled_rows(1, 1)
            tp_lo_scaled("m1")

            def proj_split(name, i, pp, nv):
                t = TILE[name] + 3 * pp
                for n, (hi, lo) in enumerate(((q_hi, q_lo), (k_hi, k_lo))):
                    dve.wait_ge(t_free, i * 6 + (t + n + 1))
                    split(hi[:, :], lo[:, :], evac_att[:, (t + n) % 2, :], x_used)
                v_split(i, nv + pp, 2)

            def rows_of(i, col):
                return rows2[:, :, ds(i * 256 + col, 64)]

            with dve.Fori(0, 2) as i:
                ch.enter(i, 2 * (3 + 16 + 1))
                for pp in range(2):
                    proj_split("in2a", i, pp, 2)
                    dve.wait_ge(bias_cp, i * 4 + (2 * pp + 2))
                    dve.memset(bias2[0:64, :, 576:640], -BIG).then_inc(bias_rdy, 1)
                    dve.memset(bias2[64:128, :, 0:64], -BIG).then_inc(bias_rdy, 1)
                    dve.wait_ge(bias_rdy, i * 4 + (2 * pp + 2))
                    soft_pair(prob2, pT2_hi, pT2_lo, WA, lambda hh: bias2[:, hh, :], 64 + 16 * pp, None,
                              lambda hh: rows_of(i, (2 * pp + hh) * 64), i, 32)
            ch.leave(2)

            def stick_pair(i, pp):
                st, per = NB * pp, 2 * NB

                def at(sem_, n):
                    dve.wait_ge(sem_, i * per + (st + n))

                def geo(s):
                    hh, hf, kt = BSTEPS[s]
                    _, n, co = bcols(hf, kt)
                    return n, co, kt >= 4 * hf, 2 + (hh * 2 + hf) % 2

                for s in range(NB + 2):
                    if s >= 2:
                        n, co, onto, bank = geo(s - 2)
                        lg = logit[:, (s - 2) % 3, 0:n]
                        at(b_c, s - 1)
                        ins = dve.tensor_tensor(lg, lg, pt[:, bank, co:co + n], ALU.subtract)
                        if onto:
                            link(ins)
                            ins = dve.tensor_tensor(lg[:, 0:P], lg[:, 0:P], drop[:, :], ALU.add)
                        ins.then_inc(b_sub, 1)
                    if s < NB:
                        n = geo(s)[0]
                        at(b_l, s + 1)
                        dve.tensor_scalar(soft[:, s % 2, 0:n], logit[:, s % 3, 0:n], 30.0, None, ALU.min)\
                            .then_inc(b_t, 1)
                    if 1 <= s <= NB:
                        z = s - 1
                        n, co, onto, bank = geo(z)
                        sf = soft[:, z % 2, 0:n]
                        at(b_ln, z + 1)
                        link(dve.tensor_tensor(sf, sf, logit[:, z % 3, 0:n], ALU.max))
                        if onto:
                            link(dve.tensor_tensor(sf[:, 0:P], sf[:, 0:P], keep[:, :], ALU.mult))
                        split(sp_hi[:, z % 2, 0:n], sp_lo[:, z % 2, 0:n], sf, b_sp)
                    if s >= 2:
                        z = s - 2
                        n = geo(z)[0]
                        at(b_w, z + 1)
                        split(wt_hi[:, z % 2, 0:n], wt_lo[:, z % 2, 0:n], logit[:, z % 3, 0:n], b_ws)
                at(b_pv, NB)
                for hh in range(2):
                    last = dve.tensor_copy(rows_of(i, HB + (2 * pp + hh) * 64),
                                           pt[:, hh, :].rearrange("p (r c) -> p r c", c=64))
                last.then_inc(o_done, 1)

            with dve.Fori(0, 2) as i:
                ch.enter(i, 2 * (3 + 24 * 3 + 16 * 2))
                for pp in range(2):
                    proj_split("in2b", i, pp, 6)
                    stick_pair(i, pp)
            ch.leave(2)

            for n in range(16):
                if n:
                    dve.wait_ge(bc_mm, n)
                col = 16 + n if n < 8 else 40 + n - 8
                dve.tensor_scalar(diag[:, :], ident[:, :], modT[:, col:col + 1], None, ALU.mult)\
                    .then_inc(diag_rdy, 1)
            dve.wait_ge(ss_done, 2)
            link(dve.reciprocal(rinv[:, :], rms[:, :]))
            for n in range(16):
                r, h = n // 2, n % 2
                last = dve.tensor_scalar(rows2[:, r, h * HB:(h + 1) * HB], rows2[:, r, h * HB:(h + 1) * HB],
                                         rinv[:, n:n + 1], None, ALU.mult)
            last.then_inc(row_rd, 1)
            tp_lo_scaled("o2")

            def gated_row(r, row_gate, gt, mf, sem_wait):
                sem_wait()
                dve.wait_ge(m_free, mf)
                link(dve.tensor_tensor(gt[:, :], pdr(r), row_gate[:, :], ALU.mult))
                dve.tensor_tensor(acc[:, r, :], acc[:, r, :], gt[:, :], ALU.add).then_inc(m_free, 1)

            dve.wait_ge(gb_rows, 2)
            for c in range(2):
                for r in range(RT):
                    ch_ = CH["out2"] + c
                    gated_row(r, row_a, gated1, 8 * ch_ + r, lambda: dve.wait_ge(m_rows, 8 * ch_ + r + 1))
                    if c:
                        dve.wait_ge(m_free, 8 * ch_ + r + 1)
                        dve.sem_inc(row_done, 1)
            scaled_rows(3, 3)
            tp_lo_scaled("m2")

            def up_tiles(name, i, nh):
                for j in range(nh):
                    dve.wait_ge(x_used, i * 8 + (TILE[name] + 2 * j))
                    for v in range(2):
                        t = TILE[name] + 2 * j + v
                        f = i * 4 + (UPH[name] + j + 22 * v)
                        u = evac[:, t % 2, :]
                        y = cv[:, v, :]
                        dve.wait_ge(t_free, i * 8 + (t + 1))
                        link(dve.tensor_scalar(y, u, cw[:, 2, ds(f, 1)], cb[:, ds(f, 1)], ALU.mult, ALU.add))
                        link(dve.scalar_tensor_tensor(out=y[:, 1:S], in0=u[:, 0:S - 1], scalar=cw[:, 1, ds(f, 1)],
                                                      in1=y[:, 1:S], op0=ALU.mult, op1=ALU.add))
                        ins = dve.scalar_tensor_tensor(out=y[:, 2:S], in0=u[:, 0:S - 2], scalar=cw[:, 0, ds(f, 1)],
                                                       in1=y[:, 2:S], op0=ALU.mult, op1=ALU.add)
                        if v == 0:
                            ins.then_inc(cv_done, 1)
                            dve.wait_ge(cv_done, i * 4 + (UPH[name] + j + 1))
                            dve.sem_inc(x_used, 1)
                        else:
                            link(ins)
                    dve.wait_ge(silu_done, i * 4 + (UPH[name] + j + 1))
                    link(dve.tensor_tensor(cv[:, 0, :], cv[:, 0, :], cv[:, 1, :], ALU.mult))
                    dve.wait_ge(m_rows, i * 8 + 8 * CH[name])
                    split(hid_hi[:, j, :], hid_lo[:, j, :], cv[:, 0, :], x_used)

            with dve.Fori(0, 5) as i:
                ch.enter(i, 4 * (2 + 3 + 2) + 8)
                up_tiles("up", i, 4)
                for r in range(RT):
                    gated_row(r, row_b, gated2, i * 8 + (8 * CH["up"] + r), lambda: dve.wait_ge(m_rows, i * 8 + (8 * CH["up"] + r + 1)))
            ch.leave(5)
            up_tiles("uplast", 0, 2)
            for r in range(RT):
                gated_row(r, row_b, gated2, 8 * CH["uplast"] + r, lambda: dve.wait_ge(m_rows, 8 * CH["uplast"] + r + 1))
                dve.wait_ge(m_free, 8 * CH["uplast"] + r + 1)
                dve.sem_inc(row_done, 1)
            dve.wait_ge(g_in, 16)
            for r in range(RT):
                dve.wait_ge(ss_done, 4 + r)
                link(dve.reciprocal(rinv[:, r:r + 1], rms[:, r:r + 1]))
                if r >= 2:
                    dve.wait_ge(stored[r % 2], 16 * (r // 2))
                dve.scalar_tensor_tensor(out=evac[:, r % 2, :], in0=acc[:, r, :], scalar=rinv[:, r:r + 1],
                                         in1=row_g[:, :], op0=ALU.mult, op1=ALU.mult).then_inc(fin_rdy, 1)


_INS = ["x", "p", "w_in", "w_pool", "pool_scale", "attn_sinks", "w_out", "ln1_g", "ln1_b", "w_ff1", "w_ff2",
        "ln2_g", "ln2_b", "w_ple", "w_ple_gate", "b_ple_gate", "c_2", "w_ada_2", "b_ada_2", "w_in_2",
        "rel_bias_2", "g_a_2", "g_b_2", "w_out_2", "w_up_2", "conv_w_2", "conv_b_2", "w_down_2", "final_g_2"]


def kernel(**inputs):
    import numpy as _np
    import concourse.bacc as _bacc
    from concourse import mybir as _mybir
    from concourse.bass_utils import run_bass_kernel_spmd as _run

    nc = _bacc.Bacc("TRN2", target_bir_lowering=False, num_devices=1, dynamic_dma_scratch_size=1024)
    arrays, args = {}, []
    for name in _INS:
        a = _np.asarray(inputs[name])
        if name == "rel_bias_2":
            a = a[0, :, ::-1]
        a = _np.ascontiguousarray(a)
        arrays[f"in_{name}"] = a
        args.append(nc.dram_tensor(f"in_{name}", a.shape, _mybir.dt.from_np(a.dtype), kind="ExternalInput").ap())
    args.append(nc.dram_tensor("out_0", (1, S, D), F32, kind="ExternalOutput").ap())
    build(nc, *args)
    r = _run(nc, [arrays], core_ids=[0])
    return r.results[0]["out_0"]
```

```python
import concourse.bass as bass
from concourse import mybir
from contextlib import ExitStack

F32 = mybir.dt.float32
F32R = mybir.dt.float32r
I32 = mybir.dt.int32
ALU = mybir.AluOpType
ACT = mybir.ActivationFunctionType
ds = bass.ds

P = 128
D = 1024
S = 1024
KT = D // P
RT = S // P
HB = 512
ALPHA = 2.0 ** 0.25
LN_EPS = 1e-5
RMS_EPS = 1e-6
QSCALE = 0.125
DFF = 4096
DFF2 = 2816
W1 = 2
WA = 5
BIG = 1e30

SEGMENTS = [
    ("in", 1, ["S"] * 6 + ["D"] * 4),
    ("out", 1, ["M"] * 8),
    ("ff", 8, ["S"] * 4 + ["M"] * 4),
    ("gate", 4, ["D"] * 2),
    ("in2a", 2, ["S"] * 6),
    ("in2b", 2, ["S"] * 6),
    ("out2", 1, ["M"] * 8),
    ("up", 5, ["S"] * 8 + ["M"] * 4),
    ("uplast", 1, ["S"] * 4 + ["M"] * 2),
]


def stream_table():
    table, unit, tile, chunk, loads = {}, 0, 0, 0, [0, 0]
    for name, n, units in SEGMENTS:
        rows, at = [], list(loads)
        t = 0
        for c, u in enumerate(units):
            slot = (unit + c) % 2
            at[slot] += 32 if u == "D" else 16
            rows.append((u, slot, at[slot], t))
            t += u != "M"
        per = [at[0] - loads[0], at[1] - loads[1]]
        table[name] = dict(n=n, rows=rows, unit=unit, tile=tile, chunk=chunk, per=per,
                           tiles=t, units=len(units))
        unit += n * len(units)
        tile += n * t
        chunk += n * ((units.count("M") + 3) // 4)
        loads = [loads[0] + n * per[0], loads[1] + n * per[1]]
    return table


SEG = stream_table()


class Chain:

    def __init__(self, eng, sem):
        self.eng, self.sem, self.base, self.n, self.at = eng, sem, 0, 0, None

    def enter(self, i, per):
        self.base += self.n
        self.at, self.per, self.n = i, per, 0

    def leave(self, times):
        assert self.n == self.per, (self.n, self.per)
        self.base, self.at, self.n = self.base + times * self.per, None, 0

    def link(self, ins):
        ins.then_inc(self.sem, 1)
        self.n += 1
        if self.at is None:
            self.eng.wait_ge(self.sem, self.base + self.n)
        else:
            self.eng.wait_ge(self.sem, self.at * self.per + (self.base + self.n))


def build(nc, x, p, w_in, w_pool, pool_scale, attn_sinks, w_out, ln1_g, ln1_b, w_ff1, w_ff2,
          ln2_g, ln2_b, w_ple, w_ple_gate, b_ple_gate, c_2, w_ada_2, b_ada_2, w_in_2, rel_rev,
          g_a_2, g_b_2, w_out_2, w_up_2, conv_w_2, conv_b_2, w_down_2, final_g_2, out):
    x, p, w_in, w_pool, w_out = x[0], p[0, 0], w_in[0], w_pool[0], w_out[0]
    w_ff1, w_ff2, w_ple, w_ple_gate = w_ff1[0], w_ff2[0], w_ple[0], w_ple_gate[0]
    w_ada, w_in2, w_out2, w_up, w_down = w_ada_2[0], w_in_2[0], w_out_2[0], w_up_2[0], w_down_2[0]
    out = out[0]

    ctx = ExitStack()
    with ctx:
        ctx.enter_context(nc.allow_non_contiguous_dma("per-feature vectors go to partitions"))

        def sem(name):
            return ctx.enter_context(nc.semaphore(name))

        top = [(nc.sbuf_base + 63) // 64 * 64]

        def region(nbytes):
            at = top[0]
            top[0] += nbytes
            return at

        def place(name, shape, dt, at):
            return nc.alloc_sbuf_tensor_at(name, shape, dt, offset=at)

        KB = 1024
        R_T = region(64 * KB)
        R_A = region(32 * KB)
        R_H = region(32 * KB)
        R_M = region(32 * KB)
        R_S = region(20 * KB)
        R_W = region(10 * KB)
        R_B = region(26 * KB)

        def small(name, shape, dt=F32):
            n = 4
            for s_ in shape[1:]:
                n *= s_
            return place(name, shape, dt, region((n + 31) // 32 * 32))

        actT_hi = place("actT_hi", [P, KT, S], F32R, R_T)
        actT_lo = place("actT_lo", [P, KT, S], F32R, R_T + 32 * KB)
        acc = place("acc", [P, RT, D], F32, R_A)
        ypool = place("ypool", [P, 4, S], F32, R_A)
        o1 = place("o1", [P, RT, HB], F32, R_A + 16 * KB)
        hid_hi = place("hid_hi", [P, 4, S], F32R, R_H)
        hid_lo = place("hid_lo", [P, 4, S], F32R, R_H + 16 * KB)
        rows2 = place("rows2", [P, RT, D], F32, R_H)
        p_rows = place("p_rows", [P, RT, 256], F32, R_H + 8 * KB)
        mv_hi = place("mv_hi", [P, 4, D], F32R, R_M)
        mv_lo = place("mv_lo", [P, 4, D], F32R, R_M + 16 * KB)

        def qkv_set(name, q_at, kv_at):
            return dict(
                q=(place(f"q_hi{name}", [P, S], F32R, q_at), place(f"q_lo{name}", [P, S], F32R, q_at + 4 * KB)),
                k=(place(f"k_hi{name}", [P, S], F32R, kv_at), place(f"k_lo{name}", [P, S], F32R, kv_at + 4 * KB)),
                v=(place(f"v_hi{name}", [P, RT, P], F32R, kv_at + 8 * KB),
                   place(f"v_lo{name}", [P, RT, P], F32R, kv_at + 12 * KB)))

        att1 = [qkv_set("1a", R_M, R_H + 8 * KB)]
        att1.append(dict(att1[0], q=(place("q_hi1b", [P, S], F32R, R_H + 24 * KB),
                                     place("q_lo1b", [P, S], F32R, R_H + 28 * KB))))
        att2 = [qkv_set("2a", R_M, R_M + 8 * KB), qkv_set("2b", R_A, R_A + 8 * KB)]
        evac_att = place("evac_att", [P, 2, S], F32, R_M + 24 * KB)
        v_cols = place("v_cols", [P, S], F32, R_A + 24 * KB)
        st_hi = place("st_hi", [P, 2, 10, P], F32R, R_S)
        st_lo = place("st_lo", [P, 2, 10, P], F32R, R_S + 10 * KB)
        raw = place("raw", [P, 2, 10 * P], F32, R_W)
        evac = place("evac", [P, 2, S], F32, R_B)
        row_a = place("row_a", [P, D], F32, R_B + 8 * KB)
        row_b = place("row_b", [P, D], F32, R_B + 12 * KB)
        gprod = place("gprod", [P, 2, S], F32, R_B + 8 * KB)
        AW = 6 * D // 8
        ada_raw = place("ada_raw", [P, 2, AW], F32, R_B + 16 * KB)
        ada_acc = place("ada_acc", [P, AW], F32, R_B + 22 * KB)
        gated1 = place("gated1", [P, D], F32, R_B + 16 * KB)
        gated2 = place("gated2", [P, D], F32, R_B + 8 * KB)
        cv = place("cv", [P, 2, S], F32, R_B + 16 * KB)
        sq_junk = place("sq_junk", [P, D], F32, R_B + 20 * KB)
        row_g = place("row_g", [P, D], F32, R_B + 16 * KB)
        bias1 = place("bias1", [P, 8, 2 * P], F32, R_B)
        sums = place("sums", [P, 2, S], F32, R_B + 8 * KB)
        d_hi = place("d_hi", [P, S], F32R, R_B + 16 * KB)
        d_lo = place("d_lo", [P, S], F32R, R_B + 20 * KB)
        prob1 = place("prob1", [P, 2, 2 * P], F32, R_B + 8 * KB)
        pT1_hi = place("pT1_hi", [P, 2, 2 * P], F32R, R_B + 10 * KB)
        pT1_lo = place("pT1_lo", [P, 2, 2 * P], F32R, R_B + 12 * KB)
        NA = WA * P
        prob2 = place("prob2", [P, 2, NA], F32, R_B)
        pT2_hi = place("pT2_hi", [P, 2, NA], F32R, R_B + 5 * KB)
        pT2_lo = place("pT2_lo", [P, 2, NA], F32R, R_B + 10 * KB)
        bias2 = place("bias2", [P, 2, NA], F32, R_B + 15 * KB)
        bias_up = place("bias_up", [P, 2, NA], F32, R_B + 20 * KB)
        logit = place("logit", [P, 3, HB], F32, R_B)
        soft = place("soft", [P, 2, HB], F32, R_B + 6 * KB)
        sp_hi = place("sp_hi", [P, 2, HB], F32R, R_B + 10 * KB)
        sp_lo = place("sp_lo", [P, 2, HB], F32R, R_B + 14 * KB)
        wt_hi = place("wt_hi", [P, 2, HB], F32R, R_B + 18 * KB)
        wt_lo = place("wt_lo", [P, 2, HB], F32R, R_B + 22 * KB)
        pw = place("pw", [P, 4, P], F32, R_H)
        pwr_hi = place("pwr_hi", [P, 4, P], F32R, R_H + 2 * KB)
        pwr_lo = place("pwr_lo", [P, 4, P], F32R, R_H + 4 * KB)
        tri_f = place("tri_f", [P, 2, P], F32, R_H + 6 * KB)
        ident = small("ident", [P, P])
        flip = small("flip", [P, P])
        tri = small("tri", [P, 2, P], F32R)
        keep = small("keep", [P, P])
        drop = small("drop", [P, P])
        ones = small("ones", [P, P])
        diag = small("diag", [P, P])
        modT = small("modT", [P, 48])
        b_ada = small("b_ada", [P, 48])
        c_col = small("c_col", [P, 8])
        c_act = small("c_act", [P, 8])
        pscale = small("pscale", [P, 4])
        b_gate = small("b_gate", [P, 8])
        gab = small("gab", [P, 8])
        cw = small("cw", [P, 3, 44])
        cb = small("cb", [P, 44])
        sink = small("sink", [P, 8])
        wcount = small("wcount", [P, 16])
        stats = small("stats", [P, 2, 6])
        mv2 = small("mv2", [P, 2])
        std = small("std", [P, 1])
        rstd = small("rstd", [P, 1])
        nmr = small("nmr", [P, 1])
        ssq = small("ssq", [P, 16])
        rms = small("rms", [P, 16])
        rinv = small("rinv", [P, 16])
        mx = small("mx", [P, 16])
        nmx = small("nmx", [P, 16])
        den = small("den", [P, 16])
        sden = small("sden", [P, 16])
        eps = small("eps", [P, 2])
        tmp512 = small("tmp512", [P, 1])
        eps_one = small("eps_one", [P, 1])
        wcnt_i = small("wcnt_i", [P, 16], I32)
        assert top[0] <= nc.sbuf_usable_end, top[0]

        pd = ctx.enter_context(nc.psum_tensor("pd", [P, 2, 2 * HB], F32))
        pt = ctx.enter_context(nc.psum_tensor("pt", [P, 4, HB], F32))

        x_mid = nc.dram_tensor("x_mid", [S, D], F32).ap()
        ptT = pt[:, 2:4, :].rearrange("p a b -> p (a b)")

        ext = nc.dram_tensor("rel_ext", [8, 768], F32)

        raw_in = [sem("raw_in0"), sem("raw_in1")]
        split_hi = sem("split_hi")
        w_ready = sem("w_ready")
        tile_done = sem("tile_done")
        m_rows = sem("m_rows")
        t_free = sem("t_free")
        x_used = sem("x_used")
        m_free = sem("m_free")
        tp_done = sem("tp_done")
        tp_hi = sem("tp_hi")
        tp_lo = sem("tp_lo")
        jb_done = sem("jb_done")
        jb_hi = sem("jb_hi")
        jb_lo = sem("jb_lo")
        mid_out = sem("mid_out")
        mid_in = sem("mid_in")
        x_in = sem("x_in")
        x_back = [sem(f"x_back{r}") for r in range(RT)]
        consts = sem("consts")
        setup = sem("setup")
        gsetup = sem("gsetup")
        vecs = sem("vecs")
        vchain = sem("vchain")
        achain = sem("achain")
        d_ready = sem("d_ready")
        pool_mm = sem("pool_mm")
        pool_out = sem("pool_out")
        pw_split = sem("pw_split")
        v_done = sem("v_done")
        s_done = sem("s_done")
        nm_ready = sem("nm_ready")
        p_ready = sem("p_ready")
        pt_done = sem("pt_done")
        pt_hi_s = sem("pt_hi_s")
        pt_lo_s = sem("pt_lo_s")
        pv_done = sem("pv_done")
        sink_e = sem("sink_e")
        yp_hi = sem("yp_hi")
        yp_lo = sem("yp_lo")
        row_rd = sem("row_rd")
        bias_cp = sem("bias_cp")
        gb_rows = sem("gb_rows")
        cv_done = sem("cv_done")
        silu_done = sem("silu_done")
        g_in = sem("g_in")
        act_one = sem("act_one")
        o_done = sem("o_done")
        row_done = sem("row_done")
        stat_in = sem("stat_in")
        std_done = sem("std_done")
        gb_in = sem("gb_in")
        ada_in = [sem("ada_in0"), sem("ada_in1")]
        ada_used = sem("ada_used")
        ada_full = sem("ada_full")
        ada_mm = sem("ada_mm")
        c_ready = sem("c_ready")
        p_in = sem("p_in")
        ple_done = sem("ple_done")
        ple_free = sem("ple_free")
        gp_ready = sem("gp_ready")
        gp_mm = sem("gp_mm")
        gp_added = sem("gp_added")
        ss_done = sem("ss_done")
        sq_done = sem("sq_done")
        diag_rdy = sem("diag_rdy")
        bc_mm = sem("bc_mm")
        ext_in = sem("ext_in")
        ext_out = sem("ext_out")
        bias_in = sem("bias_in")
        bias_mm = sem("bias_mm")
        bias_rdy = sem("bias_rdy")
        b_s = sem("b_s")
        b_l = sem("b_l")
        b_t = sem("b_t")
        b_exp = sem("b_exp")
        b_ln = sem("b_ln")
        b_sp = sem("b_sp")
        b_c = sem("b_c")
        b_sub = sem("b_sub")
        b_w = sem("b_w")
        b_ws = sem("b_ws")
        b_pv = sem("b_pv")
        fin_rdy = sem("fin_rdy")
        stored = [sem("stored0"), sem("stored1")]

        def row_base(name):
            return {"h1": 0, "h2": 8}[name]

        UPH = {"up": 0, "uplast": 4 * 5}
        TILE = {n: SEG[n]["tile"] for n in SEG}
        CH = {n: SEG[n]["chunk"] for n in SEG}
        UN = {n: SEG[n]["unit"] for n in SEG}
        order = [s_[0] for s_ in SEGMENTS]

        TPJ, n_ = {}, 0
        for name, k in (("x", 16), ("o1", 8), ("h1", 16), ("h2", 16), ("p", 4), ("m1", 16), ("o2", 16), ("m2", 16)):
            TPJ[name] = n_
            n_ += k

        BSTEPS = [(hh, hf, kt) for hh in range(2) for hf in range(2) for kt in range(4 * hf + 3, -1, -1)]
        NB = len(BSTEPS)

        def bcols(hf, kt):
            q0 = max(kt * P, hf * HB)
            return q0, (hf + 1) * HB - q0, q0 - hf * HB

        JOBS1 = [("Q", 0), ("Q", 1)]
        JOBS2 = [("V", 0), ("V", 1), ("Q", 0), ("Q", 1), ("K", 0), ("K", 1), ("T", 0), ("T", 1)]
        NJ1, NJ2, NL2 = len(JOBS1), len(JOBS2), 6

        def job_plan(jobs, before, steps, total):
            work = [(e, kind, half, k) for e, (kind, half) in enumerate(jobs) if kind != "T" for k in range(KT)]
            parts = [[] for _ in range(total)]
            rest = work[before:]
            for g, w in enumerate(rest):
                parts[g * steps // len(rest)].append(w)
            for e, (kind, half) in enumerate(jobs):
                if kind == "T":
                    parts[total - 2 + half].append((e, kind, half, KT - 1))
            return work[:before], parts

        PLAN1 = job_plan(JOBS1, 0, 14, 16)
        PLAN_A = job_plan(JOBS2, KT, 14, 16)
        PLAN_B = job_plan(JOBS2, 0, 21, NB)
        PLAN_ALONE = job_plan(JOBS2, 0, 14, 16)

        def ended(part):
            return [(e, kind, half) for e, kind, half, k in part if k == KT - 1]

        block = ctx.enter_context(nc.Block())

        @block.sync
        def _(sp):
            w_in_t = w_in.rearrange("(k p) n -> p k n", p=P)
            ff1_t = w_ff1.rearrange("(k p) n -> p k n", p=P)
            gate_t = w_ple_gate.rearrange("(k p) n -> p k n", p=P)
            ple_t = w_ple.rearrange("(k p) n -> p k n", p=P)
            in2_t = w_in2.rearrange("(k p) n -> p k n", p=P)
            up_t = w_up.rearrange("(k p) n -> p k n", p=P)

            def raw_k(slot, a, b):
                return raw[:, slot, a * P:b * P].rearrange("p (k n) -> p k n", n=P)

            def room(name, i, c):
                g = UN[name] + c
                if i is None:
                    if g >= 2:
                        sp.wait_ge(w_ready, g - 1)
                else:
                    sp.wait_ge(w_ready, i * SEG[name]["units"] + (g - 1))

            for r in range(RT):
                sp.dma_start(acc[:, r, :], x[r * P:(r + 1) * P, :]).then_inc(x_in, 16)
            for c, (u, slot, _, _) in enumerate(SEG["in"]["rows"]):
                room("in", None, c)
                if c < 6:
                    col = c * P if c < 4 else 1024 + (c - 4) * P
                    sp.dma_start(raw_k(slot, 0, 8), w_in_t[:, :, col:col + P]).then_inc(raw_in[slot], 16)
                else:
                    for hh in range(2):
                        col = 512 + 64 * (c - 6) + 256 * hh
                        sp.dma_start(raw_k(slot, 0, 8)[:, :, 64 * hh:64 * hh + 64],
                                     w_in_t[:, :, col:col + 64]).then_inc(raw_in[slot], 16)
            sp.wait_ge(tp_done, TPJ["o1"] + 8)
            sp.wait_ge(yp_lo, 4)
            for r in range(RT):
                sp.dma_start(acc[:, r, :], x[r * P:(r + 1) * P, :]).then_inc(x_back[r], 16)
            for c, (u, slot, _, _) in enumerate(SEG["out"]["rows"]):
                room("out", None, c)
                sp.dma_start(raw[:, slot, 0:D], w_out[c * P:(c + 1) * P, :]).then_inc(raw_in[slot], 16)
            with sp.Fori(0, SEG["ff"]["n"]) as i:
                for c, (u, slot, _, _) in enumerate(SEG["ff"]["rows"]):
                    room("ff", i, c)
                    if u == "S":
                        sp.dma_start(raw_k(slot, 0, 8), ff1_t[:, :, ds((i * 4 + c) * P, P)]).then_inc(raw_in[slot], 16)
                    else:
                        sp.dma_start(raw[:, slot, 0:D], w_ff2[ds((i * 4 + (c - 4)) * P, P), :]).then_inc(raw_in[slot], 16)
            with sp.Fori(0, SEG["gate"]["n"]) as i:
                for c, (u, slot, _, _) in enumerate(SEG["gate"]["rows"]):
                    room("gate", i, c)
                    sp.dma_start(raw_k(slot, 0, 8), gate_t[:, :, ds((i * 2 + c) * P, P)]).then_inc(raw_in[slot], 16)
                    sp.dma_start(raw_k(slot, 8, 10), ple_t[:, :, ds((i * 2 + c) * P, P)]).then_inc(raw_in[slot], 16)
            sp.wait_ge(x_used, TILE["in2a"])
            for r in range(RT):
                sp.dma_start(x_mid[r * P:(r + 1) * P, :], acc[:, r, :]).then_inc(mid_out, 16)
            for name, base in (("in2a", 0), ("in2b", 1536)):
                with sp.Fori(0, SEG[name]["n"]) as i:
                    for c, (u, slot, _, _) in enumerate(SEG[name]["rows"]):
                        room(name, i, c)
                        at = (base + (c + 2) % 3 * 512) // P + c // 3
                        sp.dma_start(raw_k(slot, 0, 8), in2_t[:, :, ds((i * 2 + at) * P, P)]).then_inc(raw_in[slot], 16)
            for c, (u, slot, _, _) in enumerate(SEG["out2"]["rows"]):
                room("out2", None, c)
                sp.dma_start(raw[:, slot, 0:D], w_out2[c * P:(c + 1) * P, :]).then_inc(raw_in[slot], 16)

            def up_units(name, i, i0):
                nh = sum(r_[0] == "S" for r_ in SEG[name]["rows"]) // 2
                for c, (u, slot, _, _) in enumerate(SEG[name]["rows"]):
                    room(name, None if isinstance(i, int) else i, c)
                    if u == "S":
                        col = i * (4 * P) + ((c // 2) * P + (c % 2) * DFF2 + i0 * 4 * P)
                        sp.dma_start(raw_k(slot, 0, 8), up_t[:, :, ds(col, P)]).then_inc(raw_in[slot], 16)
                    else:
                        row = i * (4 * P) + ((c - 2 * nh) * P + i0 * 4 * P)
                        sp.dma_start(raw[:, slot, 0:D], w_down[ds(row, P), :]).then_inc(raw_in[slot], 16)

            with sp.Fori(0, SEG["up"]["n"]) as i:
                up_units("up", i, 0)
            up_units("uplast", 0, SEG["up"]["n"])

        @block.gpsimd
        def _(pool):
            g_n = [0]

            def then(ins):
                g_n[0] += 1
                ins.then_inc(gsetup, 1)

            then(pool.memset(ident[:, :], 0.0))
            then(pool.memset(flip[:, :], 0.0))
            then(pool.memset(ones[:, :], 1.0))
            then(pool.memset(tri_f[:, :, :], 1.0))
            then(pool.memset(keep[:, :], 1.0))
            then(pool.memset(drop[:, :], 0.0))
            then(pool.memset(eps[:, 0:1], LN_EPS))
            then(pool.memset(eps[:, 1:2], RMS_EPS))
            then(pool.iota(wcnt_i[:, :], pattern=[[1, 16]], base=1, channel_multiplier=0))
            then(pool.iota(bias1[:, 0, :].bitcast(I32), pattern=[[1, 2 * P]], base=-P, channel_multiplier=-1))
            pool.wait_ge(gsetup, g_n[0])
            then(pool.tensor_copy(bias1[:, 7, :], bias1[:, 0, :].bitcast(I32)))
            then(pool.affine_select(out=ident[:, :], in_=ident[:, :], compare_op=ALU.not_equal, fill=1.0,
                                    base=0, pattern=[[-1, P]], channel_multiplier=1))
            then(pool.affine_select(out=flip[:, :], in_=flip[:, :], compare_op=ALU.not_equal, fill=1.0,
                                    base=-(P - 1), pattern=[[1, P]], channel_multiplier=1))
            then(pool.affine_select(out=tri_f[:, 0, :], in_=tri_f[:, 0, :], compare_op=ALU.is_ge, fill=0.0,
                                    base=0, pattern=[[-1, P]], channel_multiplier=1))
            then(pool.affine_select(out=tri_f[:, 1, :], in_=tri_f[:, 1, :], compare_op=ALU.is_gt, fill=0.0,
                                    base=0, pattern=[[1, P]], channel_multiplier=-1))
            then(pool.affine_select(out=keep[:, :], in_=keep[:, :], compare_op=ALU.is_gt, fill=0.0,
                                    base=0, pattern=[[1, P]], channel_multiplier=-1))
            then(pool.affine_select(out=drop[:, :], in_=drop[:, :], compare_op=ALU.is_gt, fill=-BIG,
                                    base=0, pattern=[[1, P]], channel_multiplier=-1))
            pool.wait_ge(gsetup, g_n[0])
            for h in range(8):
                if h == 7:
                    pool.wait_ge(gsetup, g_n[0])
                then(pool.tensor_scalar(bias1[:, h, :], bias1[:, 7, :], 2.0 ** -(h + 1), None, ALU.mult))
            pool.wait_ge(gsetup, g_n[0])
            then(pool.affine_select(out=bias1[:, :, :], in_=bias1[:, :, :], compare_op=ALU.is_ge, fill=-BIG,
                                    base=P, pattern=[[0, 8], [-1, 2 * P]], channel_multiplier=1))
            pool.wait_ge(gsetup, g_n[0])
            pool.affine_select(out=bias1[:, :, :], in_=bias1[:, :, :], compare_op=ALU.is_gt, fill=-BIG,
                               base=0, pattern=[[0, 8], [1, 2 * P]], channel_multiplier=-1).then_inc(consts, 1)

            def split(name, i, c):
                seg = SEG[name]
                u, slot, load, t = seg["rows"][c]
                g, size = UN[name] + c, (10 * P if name == "gate" else 8 * P)
                at = 0 if i is None else i

                def val(per, base):
                    return base if i is None else at * per + base
                pool.wait_ge(raw_in[slot], val(seg["per"][slot], load))
                if u == "M":
                    m = c - sum(r_[0] != "M" for r_ in seg["rows"])
                    j, ch = m % 4, CH[name] + m // 4
                    if name == "out" and m == 0:
                        pool.wait_ge(s_done, 48)
                    if name == "out2" and m == 0:
                        pool.wait_ge(b_pv, 3 * NB)
                    if j == 0 and ch > 0:
                        pool.wait_ge(m_rows, val(8, 8 * ch))
                    hi, lo = mv_hi[:, j, :], mv_lo[:, j, :]
                else:
                    T = TILE[name] + t
                    if name in ("in2a", "in2b"):
                        w = T - TILE["in2a"] - 2
                        pool.wait_ge(jb_done, val(2 * NJ2, 4 * NJ1 + NJ2 * (w // 3) + 2 * (w % 3) + 2))
                    elif name == "in" and T >= 8:
                        pool.wait_ge(jb_done, NJ1 * (T - 7))
                    elif i is not None or T >= 2:
                        pool.wait_ge(tile_done, val(seg["tiles"], T - 1))
                    hi = st_hi[:, T % 2, 0:size // P, :].rearrange("p k n -> p (k n)")
                    lo = st_lo[:, T % 2, 0:size // P, :].rearrange("p k n -> p (k n)")
                src = raw[:, slot, 0:size]
                nk = size // P
                pool.tensor_tensor(hi.rearrange("p (k n) -> p k n", n=P), src.rearrange("p (k n) -> p k n", n=P),
                                   ones[:, :].unsqueeze(1).to_broadcast([P, nk, P]), ALU.mult).then_inc(split_hi, 1)
                pool.wait_ge(split_hi, val(seg["units"], g + 1))
                pool.tensor_tensor(lo, src, hi.bitcast(F32), ALU.subtract).then_inc(w_ready, 1)

            for name in order:
                if name == "in2a":
                    pool.wait_ge(tile_done, TILE["in2a"])
                if SEG[name]["n"] == 1:
                    for c in range(SEG[name]["units"]):
                        split(name, None, c)
                else:
                    with pool.Fori(0, SEG[name]["n"]) as i:
                        for c in range(SEG[name]["units"]):
                            split(name, i, c)

        @block.tensor
        def _(pe):
            pe.wait_ge(consts, 1)

            def passes(out_ap, a_hi, a_lo, b_hi, b_lo, start, stop, check=False):
                pe.matmul(out_ap, a_hi, b_hi, start=start, stop=False, skip_group_check=check)
                pe.matmul(out_ap, a_hi, b_lo, start=False, stop=False, skip_group_check=check)
                return pe.matmul(out_ap, a_lo, b_hi, start=False, stop=stop, skip_group_check=check)

            def transposes(name, src, kts, halves=(0, 1)):
                for half in halves:
                    for n, kt in enumerate(kts):
                        job = TPJ[name] + half * len(kts) + n
                        if job >= 4:
                            pe.wait_ge(tp_lo, job - 3)
                        for r in range(4):
                            last = pe.transpose(pt[:, job % 4, r * P:(r + 1) * P],
                                                src[:, half * 4 + r, kt * P:(kt + 1) * P], ident[:, :])
                        last.then_inc(tp_done, 1)

            def tile_mm(slot, nk=8):
                for half in range(2):
                    for k in range(nk):
                        last = passes(pd[:, slot, half * HB:(half + 1) * HB], st_hi[:, slot, k, :],
                                      st_lo[:, slot, k, :], actT_hi[:, k, half * HB:(half + 1) * HB],
                                      actT_lo[:, k, half * HB:(half + 1) * HB], k == 0, k == nk - 1)
                return last

            def tile(i, per_u, u, per_t, t, rows=None):
                pe.wait_ge(w_ready, i * per_u + (u + 1))
                if not isinstance(i, int) or t + per_t * i >= 2:
                    pe.wait_ge(t_free, i * per_t + (t - 1))
                if rows is not None:
                    pe.wait_ge(m_free, i * 8 + rows)
                tile_mm(t % 2).then_inc(tile_done, 1)

            def row_mm(r, hi, lo, ks, nk):
                slot = r % 2
                for n in range(2):
                    for j in range(nk):
                        last = passes(pd[:, slot, n * HB:(n + 1) * HB], hi[:, ks + j, r * P:(r + 1) * P],
                                      lo[:, ks + j, r * P:(r + 1) * P], mv_hi[:, j, n * HB:(n + 1) * HB],
                                      mv_lo[:, j, n * HB:(n + 1) * HB], j == 0, j == nk - 1)
                last.then_inc(m_rows, 1)

            def row(r, i, ch, hi, lo, ks, nk, tiles=None):
                if r < 2 and tiles is not None:
                    pe.wait_ge(t_free, tiles)
                if not isinstance(i, int) or 8 * (ch + i) + r >= 2:
                    pe.wait_ge(m_free, i * 8 + (8 * ch + r - 1))
                row_mm(r, hi, lo, ks, nk)

            pe.wait_ge(x_in, 16 * RT)
            transposes("x", acc, range(8))

            def pool_mix(g):
                pe.wait_ge(d_ready, g + 1)
                pe.wait_ge(pw_split, 1)
                if g:
                    pe.wait_ge(pool_out, g)
                for half in range(2):
                    last = passes(pt[:, half, :], pwr_hi[:, g, :], pwr_lo[:, g, :],
                                  d_hi[:, half * HB:(half + 1) * HB], d_lo[:, half * HB:(half + 1) * HB],
                                  True, True)
                last.then_inc(pool_mm, 1)

            def v_rows(t):
                pe.wait_ge(t_free, t + 1)
                for r in range(RT):
                    last = pe.transpose(pt[:, 2 + r // 4, (r % 4) * P:(r % 4 + 1) * P],
                                        evac_att[:, t % 2, r * P:(r + 1) * P], ident[:, :])
                last.then_inc(v_done, 1)

            def product(bank, slot, half, k):
                return passes(pd[:, 0, bank * HB:(bank + 1) * HB], st_hi[:, slot, k, :], st_lo[:, slot, k, :],
                              actT_hi[:, k, half * HB:(half + 1) * HB], actT_lo[:, k, half * HB:(half + 1) * HB],
                              k == 0, k == KT - 1)

            def jobs1(j, part):
                for e, _, half, k in part:
                    if k == 0:
                        if half == 0:
                            pe.wait_ge(w_ready, 7 + j)
                        if j:
                            pe.wait_ge(jb_lo, NJ1 * j + e - 1)
                    last = product(half, j % 2, half, k)
                    if k == KT - 1:
                        last.then_inc(jb_done, 1)

            def jobs2(i, q, part):
                for e, kind, half, k in part:
                    if k == 0 or kind == "T":
                        if kind != "T" and half == 0:
                            pe.wait_ge(w_ready, i * 6 + (UN["in2a"] + 3 * q + e // 2 + 1))
                        if e in (2, 3):
                            pe.wait_ge(jb_hi, i * (2 * NJ2) + (4 * NJ1 + NJ2 * q + e - 1))
                        elif e < 2:
                            pe.wait_ge(jb_lo, i * (2 * NL2) + (4 * NJ1 + NL2 * q + e - 1))
                        else:
                            pe.wait_ge(jb_lo, i * (2 * NL2) + (4 * NJ1 + NL2 * q + e - 3))
                    if kind == "T":
                        for r in range(4):
                            last = pe.transpose(pd[:, 0, half * HB + r * P:half * HB + (r + 1) * P],
                                                v_cols[:, (4 * half + r) * P:(4 * half + r + 1) * P], ident[:, :])
                    else:
                        last = product(half, (3 * q + e // 2) % 2, half, k)
                    if k == KT - 1:
                        last.then_inc(jb_done, 1)

            def soft_pair(W, prob, pT_hi, pT_lo, kv, st, i, per, pair, qk_ready, v_ready, before, beside):
                (q_hi, q_lo), (k_hi, k_lo), (v_hi, v_lo) = kv["q"], kv["k"], kv["v"]

                def scores(s):
                    hh, qt = s // 8, s % 8
                    n = min(qt, W - 1) + 1
                    k0 = (qt - n + 1) * P
                    if s >= 1:
                        pe.wait_ge(nm_ready, i * per + (st + s))
                    else:
                        qk_ready()
                    b = slice(64 * hh, 64 * hh + 64)
                    for c0 in range(0, n * P, HB):
                        c1 = min(c0 + HB, n * P)
                        last = passes(pd[:, 1, c0:c1], q_hi[b, qt * P:(qt + 1) * P],
                                      q_lo[b, qt * P:(qt + 1) * P], k_hi[b, k0 + c0:k0 + c1],
                                      k_lo[b, k0 + c0:k0 + c1], True, True)
                    last.then_inc(s_done, 1)

                def turn(s):
                    pe.wait_ge(p_ready, i * per + (st + s + 1))
                    if s >= 1:
                        pe.wait_ge(pt_lo_s, i * per + (st + s))
                    for j in range(min(s % 8, W - 1) + 1):
                        last = pe.transpose(ptT[:, j * P:(j + 1) * P],
                                            prob[:, s % 2, j * P:(j + 1) * P], ident[:, :])
                    last.then_inc(pt_done, 1)

                def outputs(s):
                    hh, qt = s // 8, s % 8
                    n = min(qt, W - 1) + 1
                    if s == 0:
                        v_ready()
                        if st or pair:
                            pe.wait_ge(o_done, i * 2 + pair)
                    pe.wait_ge(pt_lo_s, i * per + (st + s + 1))
                    for j in range(n):
                        kt = qt - n + 1 + j
                        last = passes(pt[:, hh, qt * 64:(qt + 1) * 64], pT_hi[:, s % 2, j * P:(j + 1) * P],
                                      pT_lo[:, s % 2, j * P:(j + 1) * P], v_hi[:, kt, 64 * hh:64 * hh + 64],
                                      v_lo[:, kt, 64 * hh:64 * hh + 64], j == 0, j == n - 1)
                    last.then_inc(pv_done, 1)

                scores(0)
                before()
                for s in range(16):
                    if s + 1 < 16:
                        scores(s + 1)
                    beside(s)
                    turn(s)
                    if s:
                        outputs(s - 1)
                outputs(15)

            pe.wait_ge(tp_lo, TPJ["x"] + 16)
            for t in range(6):
                tile(0, 0, t, 0, t)
                if t == 5:
                    pool_mix(3)
                elif 1 <= t <= 3:
                    pool_mix(t - 1)
            v_rows(5)
            pe.wait_ge(t_free, 6)
            for part in PLAN1[1]:
                jobs1(0, part)

            def nothing(s=0):
                pass

            for j in range(4):
                soft_pair(W1, prob1, pT1_hi, pT1_lo, att1[j % 2], 16 * j, 0, 0, j,
                          lambda: pe.wait_ge(jb_lo, NJ1 * j + 2),
                          lambda: pe.wait_ge(x_used, 6),
                          nothing, lambda s: jobs1(j + 1, PLAN1[1][s]) if j < 3 else None)
            pe.wait_ge(o_done, 4)
            pe.sem_inc(tile_done, 4)
            transposes("o1", o1, range(4))

            def out_chunks(ch, u, hi, lo, name, tiles):
                for c in range(2):
                    pe.wait_ge(w_ready, u + 4 * c + 4)
                    for r in range(RT):
                        row(r, 0, ch + c, hi, lo, 4 * c, 4, tiles)
                        if c == 1 and name and r == 5:
                            pe.wait_ge(row_done, row_base(name) + 4)
                            transposes(name, acc, range(8), (0,))
                if name:
                    pe.wait_ge(row_done, row_base(name) + 8)
                    transposes(name, acc, range(8), (1,))

            pe.wait_ge(yp_lo, 4)
            pe.wait_ge(tp_lo, TPJ["o1"] + 8)
            out_chunks(0, UN["out"], actT_hi, actT_lo, "h1", 10)

            pe.wait_ge(tp_lo, TPJ["h1"] + 16)

            def ff_chunk(i):
                for j in range(4):
                    tile(i, 8, UN["ff"] + j, 4, TILE["ff"] + j, 16 if j < 2 else None)
                pe.wait_ge(x_used, i * 4 + (TILE["ff"] + 4))
                pe.wait_ge(w_ready, i * 8 + (UN["ff"] + 8))
                for r in range(RT):
                    if r < 2:
                        pe.wait_ge(t_free, i * 4 + (TILE["ff"] + 4))
                    row(r, i, CH["ff"], hid_hi, hid_lo, 0, 4)
                    if r == 0:
                        pe.wait_ge(ada_full, i + 1)
                        for j in range(AW // P):
                            last = pe.matmul(pt[:, 3, j:j + 1], ada_acc[:, j * P:(j + 1) * P], ones[:, 0:1],
                                             start=True, stop=True)
                        last.then_inc(ada_mm, 1)
                    if isinstance(i, int) and r == 5:
                        pe.wait_ge(row_done, 12)
                        transposes("h2", acc, range(8), (0,))

            with pe.Fori(0, 7) as i:
                ff_chunk(i)
            ff_chunk(7)
            pe.wait_ge(row_done, 16)
            transposes("h2", acc, range(8), (1,))
            pe.wait_ge(p_in, 16)
            transposes("p", p_rows, range(2))
            pe.wait_ge(tp_lo, TPJ["p"] + 4)

            def gate_tile(i, c):
                pe.wait_ge(w_ready, i * 2 + (UN["gate"] + c + 1))
                pe.wait_ge(m_free, 80)
                pe.wait_ge(ple_free, i * 2 + (c + 1))
                for half in range(2):
                    for k in range(2):
                        last = passes(pd[:, 0, half * HB:(half + 1) * HB], st_hi[:, c, 8 + k, :],
                                      st_lo[:, c, 8 + k, :], hid_hi[:, k, half * HB:(half + 1) * HB],
                                      hid_lo[:, k, half * HB:(half + 1) * HB], k == 0, k == 1)
                last.then_inc(ple_done, 1)
                pe.wait_ge(t_free, i * 2 + (TILE["gate"] + c))
                for half in range(2):
                    for k in range(8):
                        last = passes(pd[:, 1, half * HB:(half + 1) * HB], st_hi[:, c, k, :],
                                      st_lo[:, c, k, :], actT_hi[:, k, half * HB:(half + 1) * HB],
                                      actT_lo[:, k, half * HB:(half + 1) * HB], k == 0, k == 7)
                last.then_inc(tile_done, 1)

            def gate_back(i, c):
                pe.wait_ge(gp_ready, i * 2 + (c + 2))
                pe.wait_ge(x_used, i * 2 + (TILE["gate"] + c - 1))
                for r in range(RT):
                    last = pe.transpose(pt[:, 2 * c + r // 4, (r % 4) * P:(r % 4 + 1) * P],
                                        gprod[:, c, r * P:(r + 1) * P], ident[:, :])
                last.then_inc(gp_mm, 1)

            with pe.Fori(0, 4) as i:
                gate_tile(i, 0)
                gate_tile(i, 1)
                gate_back(i, 0)
                gate_back(i, 1)

            pe.wait_ge(row_rd, 1)
            transposes("m1", rows2, range(8))
            pe.wait_ge(tp_lo, TPJ["m1"] + 16)

            def bias_flip(i, pp):
                pe.wait_ge(bias_in, i * 32 + (16 * pp + 16))
                for hh in range(2):
                    if hh:
                        pe.wait_ge(bias_cp, i * 4 + (2 * pp + hh))
                    for c0 in range(0, NA, HB):
                        c1 = min(c0 + HB, NA)
                        last = pe.matmul(pt[:, 2 + c0 // HB, 0:c1 - c0], flip[:, :], bias_up[:, hh, c0:c1],
                                         start=True, stop=True)
                    last.then_inc(bias_mm, 1)

            pe.wait_ge(t_free, TILE["in2a"])
            for part in PLAN_ALONE[1]:
                jobs2(0, 0, part)

            def a_ready(i, pp, n):
                pe.wait_ge(jb_lo, i * (2 * NL2) + (4 * NJ1 + NL2 * pp + n))

            with pe.Fori(0, 2) as i:
                for pp in range(2):
                    def before():
                        jobs2(i, pp + 1, PLAN_A[0])
                        bias_flip(i, pp)

                    soft_pair(WA, prob2, pT2_hi, pT2_lo, att2[pp], 64 + 16 * pp, i, 32, 4 + pp,
                              lambda: a_ready(i, pp, 4), lambda: a_ready(i, pp, 6),
                              before, lambda s: jobs2(i, pp + 1, PLAN_A[1][s]))

            def stick_pair(pair, kv):
                (q_hi, q_lo), (k_hi, k_lo), (v_hi, v_lo) = kv["q"], kv["k"], kv["v"]

                def at(sem_, n):
                    pe.wait_ge(sem_, NB * pair + n)

                def seg(s):
                    return BSTEPS[s][0] * 2 + BSTEPS[s][1]

                def scores(s):
                    hh, hf, kt = BSTEPS[s]
                    q0, n, _ = bcols(hf, kt)
                    if s >= 2:
                        at(b_l, s - 1)
                    elif s == 0:
                        pe.wait_ge(jb_lo, 4 * NJ1 + NL2 * (4 + pair) + 4)
                    b = slice(64 * hh, 64 * hh + 64)
                    passes(pd[:, 1, (s % 2) * HB:(s % 2) * HB + n], k_hi[b, kt * P:(kt + 1) * P], k_lo[b, kt * P:(kt + 1) * P],
                           q_hi[b, q0:q0 + n], q_lo[b, q0:q0 + n], True, True).then_inc(b_s, 1)

                def sums_of(s, which, sm):
                    hh, hf, kt = BSTEPS[s]
                    _, n, co = bcols(hf, kt)
                    first = which == 0 and (s == 0 or seg(s) != seg(s - 1))
                    o = pt[:, 2 + seg(s) % 2, co:co + n]
                    pe.matmul(o, tri[:, which, :], sp_hi[:, s % 2, 0:n], start=first, stop=False,
                              skip_group_check=True)
                    last = pe.matmul(o, tri[:, which, :], sp_lo[:, s % 2, 0:n], start=False, stop=True,
                                     skip_group_check=True)
                    if sm is not None:
                        last.then_inc(sm, 1)

                def outputs(s):
                    hh, hf, kt = BSTEPS[s]
                    q0, n, _ = bcols(hf, kt)
                    if s == 0:
                        pe.wait_ge(jb_lo, 4 * NJ1 + NL2 * (5 + pair))
                        pe.wait_ge(o_done, 8 + pair)
                    at(b_ws, s + 1)
                    for j in range(n // P):
                        qt = q0 // P + j
                        last = passes(pt[:, hh, qt * 64:(qt + 1) * 64], wt_hi[:, s % 2, j * P:(j + 1) * P],
                                      wt_lo[:, s % 2, j * P:(j + 1) * P], v_hi[:, kt, 64 * hh:64 * hh + 64],
                                      v_lo[:, kt, 64 * hh:64 * hh + 64], s % 12 == 0 and j == 0, False, True)
                    last.then_inc(b_pv, 1)

                scores(0)
                for s in range(NB + 2):
                    if s + 1 < NB:
                        scores(s + 1)
                    if s < NB and pair < 3:
                        jobs2(0, 5 + pair, PLAN_B[1][s])
                    if 2 <= s:
                        at(b_sub, s - 1)
                        if s - 1 < NB and seg(s - 1) == seg(s - 2):
                            sums_of(s - 2, 1, None)
                    if 1 <= s <= NB:
                        at(b_sp, s)
                        sums_of(s - 1, 0, b_c)
                    if 2 <= s:
                        outputs(s - 2)

            for pair in range(4):
                stick_pair(pair, att2[pair % 2])

            for n in range(16):
                pe.wait_ge(diag_rdy, n + 1)
                if n == 0:
                    pe.wait_ge(o_done, 12)
                    pe.sem_inc(tile_done, 24)
                pe.matmul(pt[:, n // 4, (n % 4) * P:(n % 4 + 1) * P], ones[:, :], diag[:, :],
                          start=True, stop=True).then_inc(bc_mm, 1)
            pe.wait_ge(row_rd, 2)
            pe.wait_ge(gb_rows, 2)
            transposes("o2", rows2, range(8))
            pe.wait_ge(tp_lo, TPJ["o2"] + 16)
            out_chunks(CH["out2"], UN["out2"], actT_hi, actT_lo, None, TILE["up"])
            pe.wait_ge(row_rd, 3)
            transposes("m2", rows2, range(8))
            pe.wait_ge(tp_lo, TPJ["m2"] + 16)

            def up_chunk(name, i, nh):
                for j in range(2 * nh):
                    tile(i, 12, UN[name] + j, 8, TILE[name] + j, 8 * CH[name] if j < 2 else None)
                pe.wait_ge(x_used, i * 8 + (TILE[name] + 2 * nh))
                pe.wait_ge(w_ready, i * 12 + (UN[name] + 3 * nh))
                for r in range(RT):
                    if r < 2:
                        pe.wait_ge(t_free, i * 8 + (TILE[name] + 2 * nh))
                    row(r, i, CH[name], hid_hi, hid_lo, 0, nh)

            with pe.Fori(0, 5) as i:
                up_chunk("up", i, 4)
            up_chunk("uplast", 0, 2)

        @block.scalar
        def _(act):
            def vec(out_ap, in_ap):
                act.dma_start(out_ap, in_ap).then_inc(vecs, 16)

            def spread(a, off, n):
                return bass.AP(a.tensor, off, [[0, P], [1, n]])

            vec(pw[:, :, :], w_pool.rearrange("g c d -> c g d"))
            vec(pscale[:, :], pool_scale[0].rearrange("(g p) -> p g", p=P))
            vec(sink[:, :], spread(attn_sinks, 0, 8))
            vec(c_col[:, :], c_2[0].rearrange("(k p) -> p k", p=P))
            vec(b_ada[:, :], b_ada_2[0].rearrange("(k p) -> p k", p=P))
            vec(b_gate[:, :], b_ple_gate[0].rearrange("(k p) -> p k", p=P))
            vec(gab[:, 0:4], g_a_2[0].rearrange("(k p) -> p k", p=P))
            vec(gab[:, 4:8], g_b_2[0].rearrange("(k p) -> p k", p=P))
            vec(cw[:, :, :], conv_w_2[0].rearrange("w (k p) -> p w k", p=P))
            vec(cb[:, :], conv_b_2[0].rearrange("(k p) -> p k", p=P))

            act.wait_ge(act_one, 1)
            act.activation(tmp512[:, :], eps_one[:, :], ACT.Copy).then_inc(ple_free, 1)

            def tp_plain(name, n, hi_of, lanes=1):
                for b in n:
                    job = TPJ[name] + b
                    act.wait_ge(tp_done, job + 1)
                    act.activation(hi_of(b), pt[:, job % 4, :], ACT.Copy).then_inc(tp_hi, 1)

            def tp_scaled(name, scale_of, bias_of):
                for b in range(16):
                    job = TPJ[name] + b
                    act.wait_ge(tp_done, job + 1)
                    if b >= 2:
                        act.wait_ge(tp_lo, job - 1)
                    kt = b % 8
                    bias = bias_of(kt) if bias_of else 0.0
                    act.activation(evac[:, 0, (b % 2) * HB:(b % 2 + 1) * HB], pt[:, job % 4, :], ACT.Identity,
                                   bias=bias, scale=scale_of(kt)).then_inc(tp_hi, 1)

            def to_actT(nk, k0=0):
                def f(b):
                    half, kt = b // nk, b % nk
                    return actT_hi[:, k0 + kt, half * HB:(half + 1) * HB]
                return f

            def tile_out(i, per, t, buf, func=ACT.Copy, **kw):
                act.wait_ge(tile_done, i * per + (t + 1))
                if not isinstance(i, int) or t + per * i >= 2:
                    act.wait_ge(x_used, i * per + (t - 1))
                act.activation(buf[:, t % 2, :], pd[:, t % 2, :], func, **kw).then_inc(t_free, 1)

            tp_plain("x", range(16), to_actT(8))
            act.wait_ge(vecs, 16 * 10)
            act.activation(c_act[:, :], c_col[:, :], ACT.Sigmoid).then_inc(c_ready, 1)
            for t in range(5):
                tile_out(0, 0, t, evac_att)
                if t:
                    act.wait_ge(pool_mm, t)
                    act.activation(ypool[:, t - 1, :], pt[:, 0:2, :].rearrange("p a b -> p (a b)"), ACT.Copy,
                                   scale=pscale[:, t - 1:t]).then_inc(pool_out, 1)
            tile_out(0, 0, 5, evac_att)

            def job_hi(i, n, kv, ends):
                for e, kind, half in ends:
                    act.wait_ge(jb_done, i * (2 * NJ2) + (n + e + 1))
                    src = pd[:, 0, half * HB:(half + 1) * HB]
                    cols = slice(half * HB, (half + 1) * HB)
                    if kind == "V":
                        act.activation(v_cols[:, cols], src, ACT.Copy).then_inc(jb_hi, 1)
                    elif kind == "T":
                        act.activation(kv["v"][0][:, 4 * half:4 * half + 4, :].rearrange("p a b -> p (a b)"),
                                       src, ACT.Copy).then_inc(jb_hi, 1)
                    elif kind == "Q":
                        act.activation(kv["q"][0][:, cols], src, ACT.Copy, scale=QSCALE).then_inc(jb_hi, 1)
                    else:
                        act.activation(kv["k"][0][:, cols], src, ACT.Copy).then_inc(jb_hi, 1)

            def soft_pair(prob, pT_hi, W, st, sinks, i, per, jobs):
                def exps(s):
                    n = (min(s % 8, W - 1) + 1) * P
                    act.wait_ge(nm_ready, i * per + (st + s + 1))
                    act.activation(prob[:, s % 2, 0:n], prob[:, s % 2, 0:n], ACT.Exp, bias=nmx[:, s:s + 1],
                                   accum_out=den[:, s:s + 1]).then_inc(p_ready, 1)

                def parts(s):
                    n = (min(s % 8, W - 1) + 1) * P
                    act.wait_ge(pt_done, i * per + (st + s + 1))
                    if s >= 2:
                        act.wait_ge(pv_done, i * per + (st + s - 1))
                    act.activation(pT_hi[:, s % 2, 0:n], ptT[:, 0:n], ACT.Copy).then_inc(pt_hi_s, 1)

                for s in range(16):
                    exps(s)
                    if s:
                        parts(s - 1)
                        jobs(s - 1)
                parts(15)
                jobs(15)
                if sinks is not None:
                    for hh in range(2):
                        h = sinks + 4 * hh
                        act.activation(sden[:, 8 * hh:8 * hh + 8], nmx[:, 8 * hh:8 * hh + 8], ACT.Exp,
                                       bias=sink[:, h:h + 1]).then_inc(sink_e, 1)

            for part in PLAN1[1]:
                job_hi(0, 0, att1[0], ended(part))
            for j in range(4):
                if j:
                    act.wait_ge(o_done, j)
                soft_pair(prob1, pT1_hi, W1, 16 * j, j, 0, 0,
                          lambda s: job_hi(0, NJ1 * (j + 1), att1[(j + 1) % 2], ended(PLAN1[1][s])) if j < 3 else None)
            act.wait_ge(o_done, 4)
            act.sem_inc(t_free, 4)
            act.dma_start(row_a[:, :], spread(ln1_g, 0, D)).then_inc(gb_in, 16)
            act.dma_start(row_b[:, :], spread(ln1_b, 0, D)).then_inc(gb_in, 16)
            act.wait_ge(tile_done, 10)
            for g in range(4):
                act.activation(actT_hi[:, g, :], ypool[:, g, :], ACT.Copy).then_inc(yp_hi, 1)
            tp_plain("o1", range(8), to_actT(4, 4))

            def std_of(n):
                act.wait_ge(stat_in, n + 1)
                act.activation(std[:, :], mv2[:, 1:2], ACT.Sqrt, bias=eps[:, 0:1]).then_inc(std_done, 1)

            def norm_rows(name, base):
                for r in range(6):
                    std_of(base + r)
                tp_plain(name, range(8), to_actT(8))
                std_of(base + 6)
                std_of(base + 7)

            norm_rows("h1", 0)
            tp_plain("h1", range(8, 16), to_actT(8))
            act.dma_start(row_a[:, :], spread(ln2_g, 0, D)).then_inc(gb_in, 16)
            act.dma_start(row_b[:, :], spread(ln2_b, 0, D)).then_inc(gb_in, 16)

            def ff_tiles(i):
                for j in range(4):
                    tile_out(i, 4, TILE["ff"] + j, evac, ACT.Relu)
                    for k in (2 * j, 2 * j + 1):
                        act.wait_ge(ada_used, i * 8 + (k + 1))
                        act.dma_start(ada_raw[:, k % 2, :], w_ada[k * P:(k + 1) * P, ds(i * AW, AW)])\
                            .then_inc(ada_in[k % 2], 16)

            with act.Fori(0, 7) as i:
                ff_tiles(i)
            ff_tiles(7)
            norm_rows("h2", 8)
            act.wait_ge(m_rows, 80)
            act.dma_start(p_rows[:, :, :], p.rearrange("(r q) n -> q r n", q=P)).then_inc(p_in, 16)
            tp_plain("h2", range(8, 16), to_actT(8))
            tp_plain("p", range(4), lambda b: hid_hi[:, b % 2, (b // 2) * HB:(b // 2 + 1) * HB])

            def gate_out(i, c):
                act.wait_ge(ple_done, i * 2 + (c + 1))
                act.wait_ge(gp_ready, i * 2 + (c + 1))
                act.activation(evac[:, 0, :], pd[:, 0, :], ACT.Copy).then_inc(ple_free, 1)
                act.wait_ge(tile_done, i * 2 + (TILE["gate"] + c + 1))
                act.activation(evac[:, 1, :], pd[:, 1, :], ACT.Sigmoid,
                               bias=b_gate[:, ds(i * 2 + c, 1)]).then_inc(t_free, 1)

            with act.Fori(0, 4) as i:
                gate_out(i, 0)
                gate_out(i, 1)

            def row_squares(n0):
                for r in range(RT):
                    act.activation(rows2[:, r, :], acc[:, r, :], ACT.Square,
                                   accum_out=ssq[:, r:r + 1]).then_inc(sq_done, 1)
                act.wait_ge(sq_done, n0 + RT)
                act.activation(rms[:, 0:8], ssq[:, 0:8], ACT.Sqrt, bias=eps[:, 1:2], scale=1.0 / D)\
                    .then_inc(ss_done, 1)

            act.wait_ge(x_used, TILE["in2a"])
            row_squares(0)
            tp_scaled("m1", lambda k: modT[:, 8 + k:9 + k], lambda k: modT[:, k:k + 1])

            rel_ap = rel_rev
            act.dma_start(ext.ap()[:, 511:767], rel_ap[:, 0:256]).then_inc(ext_in, 16)
            act.dma_start(ext.ap()[:, 0:511].unsqueeze(2), bass.AP(rel_rev.tensor, 0, [[257, 8], [0, 511], [1, 1]])).then_inc(ext_in, 16)
            act.wait_ge(ext_in, 32)
            act.wait_ge(mid_out, 16 * RT)
            for part in PLAN_ALONE[1]:
                job_hi(0, 4 * NJ1, att2[0], ended(part))
            with act.Fori(0, 2) as i:
                for pp in range(2):
                    def jobs(part):
                        job_hi(i, 4 * NJ1 + NJ2 * (pp + 1), att2[(pp + 1) % 2], ended(part))

                    act.wait_ge(o_done, i * 2 + (4 + pp))
                    act.dma_start(bias_up[:, :, :], bass.AP(ext, i * (4 * 768) + 2 * pp * 768,
                                                            [[1, P], [768, 2], [1, NA]])).then_inc(bias_in, 16)
                    jobs(PLAN_A[0])
                    for hh in range(2):
                        act.wait_ge(bias_mm, i * 4 + (2 * pp + hh + 1))
                        act.activation(bias2[:, hh, :], pt[:, 2:4, :].rearrange("p a b -> p (a b)")[:, 0:NA],
                                       ACT.Copy).then_inc(bias_cp, 1)
                    soft_pair(prob2, pT2_hi, WA, 64 + 16 * pp, None, i, 32, lambda s: jobs(PLAN_A[1][s]))

            def stick_pair(pair):
                def at(sem_, n):
                    act.wait_ge(sem_, NB * pair + n)

                def cols(s):
                    return bcols(*BSTEPS[s][1:])[1]

                for s in range(NB + 2):
                    if s < NB:
                        n = cols(s)
                        at(b_s, s + 1)
                        if s >= 3:
                            at(b_ws, s - 2)
                        act.activation(logit[:, s % 3, 0:n], pd[:, 1, (s % 2) * HB:(s % 2) * HB + n], ACT.Copy)\
                            .then_inc(b_l, 1)
                    if s >= 2:
                        at(b_sub, s - 1)
                        n = cols(s - 2)
                        act.activation(logit[:, (s - 2) % 3, 0:n], logit[:, (s - 2) % 3, 0:n], ACT.Exp)\
                            .then_inc(b_w, 1)
                    if s < NB:
                        n = cols(s)
                        at(b_t, s + 1)
                        act.activation(soft[:, s % 2, 0:n], soft[:, s % 2, 0:n], ACT.Exp).then_inc(b_exp, 1)
                        at(b_exp, s + 1)
                        act.activation(soft[:, s % 2, 0:n], soft[:, s % 2, 0:n], ACT.Ln, bias=1.0)\
                            .then_inc(b_ln, 1)
                    if 1 <= s <= NB and pair < 3:
                        job_hi(0, 4 * NJ1 + NJ2 * (5 + pair), att2[(pair + 1) % 2], ended(PLAN_B[1][s - 1]))

            act.preload_act_table_set("natural_log_exp_and_others")
            for pair in range(4):
                act.wait_ge(o_done, 8 + pair)
                stick_pair(pair)

            act.wait_ge(o_done, 12)
            act.sem_inc(t_free, 24)
            act.dma_start(acc[:, :, :], x_mid.rearrange("(r p) n -> p r n", p=P)).then_inc(mid_in, 16)
            for n in range(16):
                r, h = n // 2, n % 2
                if n >= 2:
                    act.wait_ge(sq_done, 8 + n - 1)
                act.activation(evac[:, 0, 0:HB] if n % 2 else evac[:, 0, HB:D], rows2[:, r, h * HB:(h + 1) * HB],
                               ACT.Square, accum_out=ssq[:, n:n + 1]).then_inc(sq_done, 1)
            act.wait_ge(sq_done, 24)
            act.activation(rms[:, 0:16], ssq[:, 0:16], ACT.Sqrt, bias=eps[:, 1:2], scale=1.0 / HB)\
                .then_inc(ss_done, 1)
            act.wait_ge(bc_mm, 16)
            ptf = pt[:, :, :].rearrange("p a b -> p (a b)")
            act.activation(row_a[:, :], ptf[:, 0:D], ACT.Copy).then_inc(gb_rows, 1)
            act.activation(row_b[:, :], ptf[:, D:2 * D], ACT.Copy).then_inc(gb_rows, 1)
            tp_scaled("o2", lambda k: gab[:, k:k + 1], None)
            act.wait_ge(row_done, 24)
            row_squares(24)
            tp_scaled("m2", lambda k: modT[:, 32 + k:33 + k], lambda k: modT[:, 24 + k:25 + k])

            def up_out(name, i, nh):
                for j in range(nh):
                    t = TILE[name] + 2 * j
                    tile_out(i, 8, t, evac)
                    tile_out(i, 8, t + 1, evac)
                    act.wait_ge(cv_done, i * 4 + (UPH[name] + j + 1))
                    act.activation(cv[:, 0, :], cv[:, 0, :], ACT.Silu).then_inc(silu_done, 1)

            with act.Fori(0, 5) as i:
                up_out("up", i, 4)
            up_out("uplast", 0, 2)
            act.wait_ge(x_used, TILE["uplast"] + 4)
            act.dma_start(row_g[:, :], spread(final_g_2, 0, D)).then_inc(g_in, 16)
            def store(r):
                act.wait_ge(fin_rdy, r + 1)
                act.dma_start(out[r * P:(r + 1) * P, :], evac[:, r % 2, :]).then_inc(stored[r % 2], 16)

            for r in range(RT):
                act.wait_ge(row_done, 24 + r + 1)
                act.activation(sq_junk[:, :], acc[:, r, :], ACT.Square,
                               accum_out=ssq[:, r:r + 1]).then_inc(sq_done, 1)
                act.wait_ge(sq_done, 32 + r + 1)
                act.activation(rms[:, r:r + 1], ssq[:, r:r + 1], ACT.Sqrt, bias=eps[:, 1:2], scale=1.0 / D)\
                    .then_inc(ss_done, 1)
                if r:
                    store(r - 1)
            store(RT - 1)
            act.wait_ge(stored[0], 64)
            act.wait_ge(stored[1], 64)

        @block.vector
        def _(dve):
            ch = Chain(dve, vchain)
            link = ch.link

            def split(hi, lo, src, sem_):
                link(dve.tensor_copy(hi, src))
                dve.tensor_tensor(lo, src, hi.bitcast(F32), ALU.subtract).then_inc(sem_, 1)

            dve.wait_ge(consts, 1)
            dve.memset(eps_one[:, :], 1.0).then_inc(act_one, 1)
            link(dve.tensor_copy(tri[:, :, :], tri_f[:, :, :]))
            link(dve.tensor_copy(wcount[:, :], wcnt_i[:, :]))
            link(dve.reciprocal(wcount[:, :], wcount[:, :]))

            def tp_lo_plain(name, n, hi_of, lo_of):
                for b in n:
                    job = TPJ[name] + b
                    dve.wait_ge(tp_hi, job + 1)
                    dve.tensor_tensor(lo_of(b), pt[:, job % 4, :], hi_of(b).bitcast(F32), ALU.subtract)\
                        .then_inc(tp_lo, 1)

            def tp_lo_scaled(name):
                for b in range(16):
                    job = TPJ[name] + b
                    half, kt = b // 8, b % 8
                    c = slice(half * HB, (half + 1) * HB)
                    dve.wait_ge(tp_hi, job + 1)
                    split(actT_hi[:, kt, c], actT_lo[:, kt, c], evac[:, 0, (b % 2) * HB:(b % 2 + 1) * HB], tp_lo)

            def T(t_, nk, k0=0):
                return lambda b: t_[:, k0 + b % nk, (b // nk) * HB:(b // nk + 1) * HB]

            tp_lo_plain("x", range(16), T(actT_hi, 8), T(actT_lo, 8))
            dve.wait_ge(vecs, 16 * 10)
            split(pwr_hi[:, :, :], pwr_lo[:, :, :], pw[:, :, :], pw_split)
            dve.wait_ge(c_ready, 1)
            dve.tensor_tensor(c_act[:, :], c_act[:, :], c_col[:, :], ALU.mult).then_inc(ada_used, 2)
            for g in range(4):
                dve.wait_ge(t_free, g + 1)
                u = evac_att[:, g % 2, :]
                if g:
                    dve.wait_ge(d_ready, g)
                src, w = u, 1
                for step in range(g + 1):
                    dst = sums[:, step % 2, :]
                    link(dve.tensor_copy(dst[:, 0:w], src[:, 0:w]))
                    link(dve.tensor_tensor(dst[:, w:S], src[:, w:S], src[:, 0:S - w], ALU.add))
                    src, w = dst, 2 * w
                link(dve.tensor_tensor(src[:, 0:w], src[:, 0:w], wcount[:, 0:w], ALU.mult))
                link(dve.tensor_tensor(src[:, 0:w], src[:, 0:w], u[:, 0:w], ALU.subtract))
                link(dve.scalar_tensor_tensor(out=src[:, w:S], in0=src[:, w:S], scalar=1.0 / w, in1=u[:, w:S],
                                              op0=ALU.mult, op1=ALU.subtract))
                dve.sem_inc(x_used, 1)
                if g:
                    dve.wait_ge(pool_mm, g)
                split(d_hi[:, :], d_lo[:, :], src, d_ready)
            dve.wait_ge(t_free, 5)
            split(att1[0]["k"][0][:, :], att1[0]["k"][1][:, :], evac_att[:, 0, :], x_used)
            dve.wait_ge(v_done, 1)
            split(att1[0]["v"][0][:, :, :].rearrange("p a b -> p (a b)"),
                  att1[0]["v"][1][:, :, :].rearrange("p a b -> p (a b)"), ptT[:, :], x_used)

            def job_lo(i, n, kv, ends):
                for e, kind, half in ends:
                    if kind == "V":
                        continue
                    dve.wait_ge(jb_hi, i * (2 * NJ2) + (n + e + 1))
                    src = pd[:, 0, half * HB:(half + 1) * HB]
                    cols = slice(half * HB, (half + 1) * HB)
                    if kind == "Q":
                        hi, lo = kv["q"]
                        dve.scalar_tensor_tensor(out=lo[:, cols], in0=src, scalar=QSCALE, in1=hi[:, cols].bitcast(F32),
                                                 op0=ALU.mult, op1=ALU.subtract).then_inc(jb_lo, 1)
                    elif kind == "K":
                        hi, lo = kv["k"]
                        dve.tensor_tensor(lo[:, cols], src, hi[:, cols].bitcast(F32), ALU.subtract).then_inc(jb_lo, 1)
                    else:
                        hi, lo = (t_[:, 4 * half:4 * half + 4, :].rearrange("p a b -> p (a b)") for t_ in kv["v"])
                        dve.tensor_tensor(lo, src, hi.bitcast(F32), ALU.subtract).then_inc(jb_lo, 1)

            def soft_pair(prob, pT_hi, pT_lo, W, bias_ap, st, sinks, o_out, i, per, jobs):
                def top(s):
                    n = (min(s % 8, W - 1) + 1) * P
                    dve.wait_ge(s_done, i * per + (st + s + 1))
                    if s >= 2:
                        dve.wait_ge(pt_done, i * per + (st + s - 1))
                    dve.memset(nmx[:, s:s + 1], 0.0)
                    link(dve.tensor_tensor_reduce(out=prob[:, s % 2, 0:n], in0=pd[:, 1, 0:n],
                                                  in1=bias_ap(s // 8)[:, W * P - n:W * P], scale=1.0,
                                                  scalar=-3e38, op0=ALU.add, op1=ALU.max,
                                                  accum_out=mx[:, s:s + 1]))
                    if sinks is None:
                        dve.tensor_scalar(nmx[:, s:s + 1], mx[:, s:s + 1], -1.0, None, ALU.mult)\
                            .then_inc(nm_ready, 1)
                    else:
                        h = sinks + 4 * (s // 8)
                        dve.tensor_scalar(nmx[:, s:s + 1], mx[:, s:s + 1], sink[:, h:h + 1], -1.0,
                                          ALU.max, ALU.mult).then_inc(nm_ready, 1)

                def low(s):
                    n = (min(s % 8, W - 1) + 1) * P
                    dve.wait_ge(pt_hi_s, i * per + (st + s + 1))
                    dve.tensor_tensor(pT_lo[:, s % 2, 0:n], ptT[:, 0:n], pT_hi[:, s % 2, 0:n].bitcast(F32),
                                      ALU.subtract).then_inc(pt_lo_s, 1)

                for s in range(16):
                    top(s)
                    if s:
                        low(s - 1)
                        jobs(s - 1)
                low(15)
                jobs(15)
                dve.wait_ge(pv_done, i * per + (st + 16))
                if sinks is not None:
                    dve.wait_ge(sink_e, 2 * (sinks + 1))
                    link(dve.tensor_tensor(den[:, :], den[:, :], sden[:, :], ALU.add))
                link(dve.reciprocal(rinv[:, :], den[:, :]))
                for hh in range(2):
                    last = dve.tensor_tensor(o_out(hh), pt[:, hh, :].rearrange("p (r c) -> p r c", c=64),
                                             rinv[:, 8 * hh:8 * hh + 8].unsqueeze(2).to_broadcast([P, 8, 64]),
                                             ALU.mult)
                last.then_inc(o_done, 1)

            for part in PLAN1[1]:
                job_lo(0, 0, att1[0], ended(part))
            for j in range(4):
                soft_pair(prob1, pT1_hi, pT1_lo, W1, lambda hh: bias1[:, j + 4 * hh, :], 16 * j, j,
                          lambda hh: o1[:, :, (j + 4 * hh) * 64:(j + 4 * hh + 1) * 64], 0, 0,
                          lambda s: job_lo(0, NJ1 * (j + 1), att1[(j + 1) % 2], ended(PLAN1[1][s]))
                          if j < 3 else None)
            dve.sem_inc(x_used, 4)
            for g in range(4):
                dve.wait_ge(yp_hi, g + 1)
                dve.tensor_tensor(actT_lo[:, g, :], ypool[:, g, :], actT_hi[:, g, :].bitcast(F32), ALU.subtract)\
                    .then_inc(yp_lo, 1)
            tp_lo_plain("o1", range(8), T(actT_hi, 4, 4), T(actT_lo, 4, 4))

            def pdr(r):
                return pd[:, r % 2, :]

            def stat(r):
                link(dve.bn_stats(out=stats[:, 0, :], in_=acc[:, r, 0:HB]))
                link(dve.bn_stats(out=stats[:, 1, :], in_=acc[:, r, HB:D]))
                dve.bn_aggr(out=mv2[:, :], in_=stats[:, :, :]).then_inc(stat_in, 1)

            def finish(r, n):
                dve.wait_ge(std_done, n)
                link(dve.reciprocal(rstd[:, :], std[:, :]))
                link(dve.scalar_tensor_tensor(out=nmr[:, :], in0=mv2[:, 0:1], scalar=-1.0, in1=rstd[:, :],
                                              op0=ALU.mult, op1=ALU.mult))
                link(dve.tensor_scalar(acc[:, r, :], acc[:, r, :], rstd[:, :], nmr[:, :], ALU.mult, ALU.add))
                link(dve.tensor_tensor(acc[:, r, :], acc[:, r, :], row_a[:, :], ALU.mult))
                dve.tensor_tensor(acc[:, r, :], acc[:, r, :], row_b[:, :], ALU.add).then_inc(row_done, 1)

            def add_row(r, scale=None):
                if scale is None:
                    return dve.tensor_tensor(acc[:, r, :], acc[:, r, :], pdr(r), ALU.add)
                return dve.scalar_tensor_tensor(out=acc[:, r, :], in0=acc[:, r, :], scalar=scale, in1=pdr(r),
                                                op0=ALU.mult, op1=ALU.add)

            def norm_chunk(ch_, name, base, extra=None):
                for r in range(RT):
                    dve.wait_ge(m_rows, 8 * ch_ + r + 1)
                    add_row(r).then_inc(m_free, 1)
                    if r == 0 and extra:
                        extra()
                    dve.wait_ge(m_free, 8 * ch_ + r + 1)
                    stat(r)
                    finish(r, base + r + 1)
                    if r == 5:
                        tp_lo_plain(name, range(8), T(actT_hi, 8), T(actT_lo, 8))
                tp_lo_plain(name, range(8, 16), T(actT_hi, 8), T(actT_lo, 8))
                if name == "h1":
                    for r in range(RT):
                        link(dve.tensor_scalar(acc[:, r, :], acc[:, r, :], ALPHA, None, ALU.mult))

            for r in range(RT):
                dve.wait_ge(x_back[r], 16)
                dve.wait_ge(m_rows, r + 1)
                add_row(r, ALPHA).then_inc(m_free, 1)
            dve.wait_ge(gb_in, 32)
            dve.wait_ge(m_free, 8)
            norm_chunk(1, "h1", 0)

            def ff_tiles(i):
                for j in range(4):
                    t = TILE["ff"] + j
                    xs = evac[:, t % 2, :]
                    dve.wait_ge(t_free, i * 4 + (t + 1))
                    link(dve.tensor_tensor(xs, xs, xs, ALU.mult))
                    dve.wait_ge(m_rows, i * 8 + 16)
                    split(hid_hi[:, j, :], hid_lo[:, j, :], xs, x_used)
                    for k in (2 * j, 2 * j + 1):
                        dve.wait_ge(ada_in[k % 2], i * 64 + 16 * (k // 2 + 1))
                        if k == 0:
                            ins = dve.tensor_scalar(ada_acc[:, :], ada_raw[:, 0, :], c_act[:, 0:1], None, ALU.mult)
                        else:
                            ins = dve.scalar_tensor_tensor(out=ada_acc[:, :], in0=ada_raw[:, k % 2, :],
                                                           scalar=c_act[:, k:k + 1], in1=ada_acc[:, :],
                                                           op0=ALU.mult, op1=ALU.add)
                        ins.then_inc(ada_used, 1)
                        dve.wait_ge(ada_used, i * 8 + (k + 3))
                dve.sem_inc(ada_full, 1)

            def mod_cols(i):
                dve.wait_ge(ada_mm, i + 1)
                link(dve.tensor_tensor(modT[:, ds(i * 6, 6)], pt[:, 3, 0:6], b_ada[:, ds(i * 6, 6)], ALU.add))

            with dve.Fori(0, 7) as i:
                ch.enter(i, 4 * 2 + 1)
                ff_tiles(i)
                for r in range(RT):
                    dve.wait_ge(m_rows, i * 8 + (16 + r + 1))
                    add_row(r).then_inc(m_free, 1)
                    if r == 0:
                        mod_cols(i)
            ch.leave(7)
            ff_tiles(7)
            dve.wait_ge(gb_in, 64)
            dve.wait_ge(m_free, 72)

            def last_mod():
                mod_cols(7)
                link(dve.tensor_scalar(modT[:, 8:16], modT[:, 8:16], 1.0, None, ALU.add))
                link(dve.tensor_scalar(modT[:, 32:40], modT[:, 32:40], 1.0, None, ALU.add))

            norm_chunk(9, "h2", 8, last_mod)
            hp = [lambda b: hid_hi[:, b % 2, (b // 2) * HB:(b // 2 + 1) * HB],
                  lambda b: hid_lo[:, b % 2, (b // 2) * HB:(b // 2 + 1) * HB]]
            tp_lo_plain("p", range(4), *hp)
            dve.sem_inc(gp_ready, 1)

            def gate_prod(i, c):
                dve.wait_ge(t_free, i * 2 + (TILE["gate"] + c + 1))
                dve.wait_ge(ple_free, i * 2 + (c + 2))
                dve.tensor_tensor(gprod[:, c, :], evac[:, 0, :], evac[:, 1, :], ALU.mult).then_inc(gp_ready, 1)

            def gate_add(i, c):
                dve.wait_ge(gp_mm, i * 2 + (c + 1))
                col = acc[:, :, ds((i * 2 + c) * P, P)]
                dve.tensor_tensor(col, col, pt[:, 2 * c:2 * c + 2, :].rearrange("p a (b n) -> p (a b) n", n=P),
                                  ALU.add).then_inc(x_used, 1)

            with dve.Fori(0, 4) as i:
                gate_prod(i, 0)
                gate_prod(i, 1)
                gate_add(i, 0)
                gate_add(i, 1)

            def scaled_rows(n, rd):
                dve.wait_ge(ss_done, n)
                link(dve.reciprocal(rinv[:, 0:8], rms[:, 0:8]))
                for r in range(RT):
                    last = dve.tensor_scalar(rows2[:, r, :], acc[:, r, :], rinv[:, r:r + 1], None, ALU.mult)
                last.then_inc(row_rd, 1)

            scaled_rows(1, 1)
            tp_lo_scaled("m1")

            def rows_of(i, col):
                return rows2[:, :, ds(i * 256 + col, 64)]

            for part in PLAN_ALONE[1]:
                job_lo(0, 4 * NJ1, att2[0], ended(part))
            with dve.Fori(0, 2) as i:
                ch.enter(i, 2 * (16 + 1))
                for pp in range(2):
                    dve.wait_ge(bias_cp, i * 4 + (2 * pp + 2))
                    dve.memset(bias2[0:64, :, 576:640], -BIG).then_inc(bias_rdy, 1)
                    dve.memset(bias2[64:128, :, 0:64], -BIG).then_inc(bias_rdy, 1)
                    dve.wait_ge(bias_rdy, i * 4 + (2 * pp + 2))
                    soft_pair(prob2, pT2_hi, pT2_lo, WA, lambda hh: bias2[:, hh, :], 64 + 16 * pp, None,
                              lambda hh: rows_of(i, (2 * pp + hh) * 64), i, 32,
                              lambda s: job_lo(i, 4 * NJ1 + NJ2 * (pp + 1), att2[(pp + 1) % 2],
                                               ended(PLAN_A[1][s])))
            ch.leave(2)

            def stick_pair(pair):
                def at(sem_, n):
                    dve.wait_ge(sem_, NB * pair + n)

                def geo(s):
                    hh, hf, kt = BSTEPS[s]
                    _, n, co = bcols(hf, kt)
                    return n, co, kt >= 4 * hf, 2 + (hh * 2 + hf) % 2

                for s in range(NB + 2):
                    if s >= 2:
                        n, co, onto, bank = geo(s - 2)
                        lg = logit[:, (s - 2) % 3, 0:n]
                        at(b_c, s - 1)
                        ins = dve.tensor_tensor(lg, lg, pt[:, bank, co:co + n], ALU.subtract)
                        if onto:
                            link(ins)
                            ins = dve.tensor_tensor(lg[:, 0:P], lg[:, 0:P], drop[:, :], ALU.add)
                        ins.then_inc(b_sub, 1)
                    if s < NB:
                        n = geo(s)[0]
                        at(b_l, s + 1)
                        dve.tensor_scalar(soft[:, s % 2, 0:n], logit[:, s % 3, 0:n], 30.0, None, ALU.min)\
                            .then_inc(b_t, 1)
                    if 1 <= s <= NB:
                        z = s - 1
                        n, co, onto, bank = geo(z)
                        sf = soft[:, z % 2, 0:n]
                        at(b_ln, z + 1)
                        link(dve.tensor_tensor(sf, sf, logit[:, z % 3, 0:n], ALU.max))
                        if onto:
                            link(dve.tensor_tensor(sf[:, 0:P], sf[:, 0:P], keep[:, :], ALU.mult))
                        split(sp_hi[:, z % 2, 0:n], sp_lo[:, z % 2, 0:n], sf, b_sp)
                    if s >= 2:
                        z = s - 2
                        n = geo(z)[0]
                        at(b_w, z + 1)
                        split(wt_hi[:, z % 2, 0:n], wt_lo[:, z % 2, 0:n], logit[:, z % 3, 0:n], b_ws)
                    if 1 <= s <= NB and pair < 3:
                        job_lo(0, 4 * NJ1 + NJ2 * (5 + pair), att2[(pair + 1) % 2], ended(PLAN_B[1][s - 1]))
                at(b_pv, NB)
                for hh in range(2):
                    last = dve.tensor_copy(rows_of(0, HB + (2 * pair + hh) * 64),
                                           pt[:, hh, :].rearrange("p (r c) -> p r c", c=64))
                last.then_inc(o_done, 1)

            for pair in range(4):
                stick_pair(pair)
            dve.sem_inc(x_used, 24)

            for n in range(16):
                if n:
                    dve.wait_ge(bc_mm, n)
                col = 16 + n if n < 8 else 40 + n - 8
                dve.tensor_scalar(diag[:, :], ident[:, :], modT[:, col:col + 1], None, ALU.mult)\
                    .then_inc(diag_rdy, 1)
            dve.wait_ge(ss_done, 2)
            link(dve.reciprocal(rinv[:, :], rms[:, :]))
            for n in range(16):
                r, h = n // 2, n % 2
                last = dve.tensor_scalar(rows2[:, r, h * HB:(h + 1) * HB], rows2[:, r, h * HB:(h + 1) * HB],
                                         rinv[:, n:n + 1], None, ALU.mult)
            last.then_inc(row_rd, 1)
            tp_lo_scaled("o2")

            def gated_row(r, row_gate, gt, mf, sem_wait):
                sem_wait()
                dve.wait_ge(m_free, mf)
                link(dve.tensor_tensor(gt[:, :], pdr(r), row_gate[:, :], ALU.mult))
                dve.tensor_tensor(acc[:, r, :], acc[:, r, :], gt[:, :], ALU.add).then_inc(m_free, 1)

            dve.wait_ge(gb_rows, 2)
            dve.wait_ge(mid_in, 16)
            for c in range(2):
                for r in range(RT):
                    ch_ = CH["out2"] + c
                    gated_row(r, row_a, gated1, 8 * ch_ + r, lambda: dve.wait_ge(m_rows, 8 * ch_ + r + 1))
                    if c:
                        dve.wait_ge(m_free, 8 * ch_ + r + 1)
                        dve.sem_inc(row_done, 1)
            scaled_rows(3, 3)
            tp_lo_scaled("m2")

            def up_tiles(name, i, nh):
                for j in range(nh):
                    dve.wait_ge(x_used, i * 8 + (TILE[name] + 2 * j))
                    for v in range(2):
                        t = TILE[name] + 2 * j + v
                        f = i * 4 + (UPH[name] + j + 22 * v)
                        u = evac[:, t % 2, :]
                        y = cv[:, v, :]
                        dve.wait_ge(t_free, i * 8 + (t + 1))
                        link(dve.tensor_scalar(y, u, cw[:, 2, ds(f, 1)], cb[:, ds(f, 1)], ALU.mult, ALU.add))
                        link(dve.scalar_tensor_tensor(out=y[:, 1:S], in0=u[:, 0:S - 1], scalar=cw[:, 1, ds(f, 1)],
                                                      in1=y[:, 1:S], op0=ALU.mult, op1=ALU.add))
                        ins = dve.scalar_tensor_tensor(out=y[:, 2:S], in0=u[:, 0:S - 2], scalar=cw[:, 0, ds(f, 1)],
                                                       in1=y[:, 2:S], op0=ALU.mult, op1=ALU.add)
                        if v == 0:
                            ins.then_inc(cv_done, 1)
                            dve.wait_ge(cv_done, i * 4 + (UPH[name] + j + 1))
                            dve.sem_inc(x_used, 1)
                        else:
                            link(ins)
                    dve.wait_ge(silu_done, i * 4 + (UPH[name] + j + 1))
                    link(dve.tensor_tensor(cv[:, 0, :], cv[:, 0, :], cv[:, 1, :], ALU.mult))
                    dve.wait_ge(m_rows, i * 8 + 8 * CH[name])
                    split(hid_hi[:, j, :], hid_lo[:, j, :], cv[:, 0, :], x_used)

            with dve.Fori(0, 5) as i:
                ch.enter(i, 4 * (2 + 3 + 2) + 8)
                up_tiles("up", i, 4)
                for r in range(RT):
                    gated_row(r, row_b, gated2, i * 8 + (8 * CH["up"] + r), lambda: dve.wait_ge(m_rows, i * 8 + (8 * CH["up"] + r + 1)))
            ch.leave(5)
            up_tiles("uplast", 0, 2)
            for r in range(RT):
                gated_row(r, row_b, gated2, 8 * CH["uplast"] + r, lambda: dve.wait_ge(m_rows, 8 * CH["uplast"] + r + 1))
                dve.wait_ge(m_free, 8 * CH["uplast"] + r + 1)
                dve.sem_inc(row_done, 1)
            dve.wait_ge(g_in, 16)
            for r in range(RT):
                dve.wait_ge(ss_done, 4 + r)
                link(dve.reciprocal(rinv[:, r:r + 1], rms[:, r:r + 1]))
                if r >= 2:
                    dve.wait_ge(stored[r % 2], 16 * (r // 2))
                dve.scalar_tensor_tensor(out=evac[:, r % 2, :], in0=acc[:, r, :], scalar=rinv[:, r:r + 1],
                                         in1=row_g[:, :], op0=ALU.mult, op1=ALU.mult).then_inc(fin_rdy, 1)


_INS = ["x", "p", "w_in", "w_pool", "pool_scale", "attn_sinks", "w_out", "ln1_g", "ln1_b", "w_ff1", "w_ff2",
        "ln2_g", "ln2_b", "w_ple", "w_ple_gate", "b_ple_gate", "c_2", "w_ada_2", "b_ada_2", "w_in_2",
        "rel_bias_2", "g_a_2", "g_b_2", "w_out_2", "w_up_2", "conv_w_2", "conv_b_2", "w_down_2", "final_g_2"]


def kernel(**inputs):
    import numpy as _np
    import concourse.bacc as _bacc
    from concourse import mybir as _mybir
    from concourse.bass_utils import run_bass_kernel_spmd as _run

    nc = _bacc.Bacc("TRN2", target_bir_lowering=False, num_devices=1, dynamic_dma_scratch_size=1024)
    arrays, args = {}, []
    for name in _INS:
        a = _np.asarray(inputs[name])
        if name == "rel_bias_2":
            a = a[0, :, ::-1]
        a = _np.ascontiguousarray(a)
        arrays[f"in_{name}"] = a
        args.append(nc.dram_tensor(f"in_{name}", a.shape, _mybir.dt.from_np(a.dtype), kind="ExternalInput").ap())
    args.append(nc.dram_tensor("out_0", (1, S, D), F32, kind="ExternalOutput").ap())
    build(nc, *args)
    r = _run(nc, [arrays], core_ids=[0])
    return r.results[0]["out_0"]
```

```python
import concourse.bass as bass
from concourse import mybir
from contextlib import ExitStack

F32 = mybir.dt.float32
F32R = mybir.dt.float32r
I32 = mybir.dt.int32
ALU = mybir.AluOpType
ACT = mybir.ActivationFunctionType
ds = bass.ds

P = 128
D = 1024
S = 1024
KT = D // P
RT = S // P
HB = 512
ALPHA = 2.0 ** 0.25
LN_EPS = 1e-5
RMS_EPS = 1e-6
QSCALE = 0.125
DFF = 4096
DFF2 = 2816
W1 = 2
WA = 5
BIG = 1e30

SEGMENTS = [
    ("in", 1, ["S"] * 6 + ["D"] * 4),
    ("out", 1, ["M"] * 8),
    ("ffa", 1, ["S"] * 3),
    ("ff", 7, ["M", "M", "S", "M", "M"] + ["S"] * 3),
    ("ffb", 1, ["M", "M", "S", "M", "M"]),
    ("gate", 4, ["D"] * 2),
    ("in2a", 2, ["S"] * 6),
    ("in2b", 2, ["S"] * 6),
    ("out2", 1, ["M"] * 8),
    ("upa", 1, ["S"] * 3),
    ("up", 5, ["M", "M", "S", "M", "M"] + ["S"] * 7),
    ("upb", 1, ["M", "M", "S"]),
]


def stream_table():
    table, unit, tile, chunk, loads = {}, 0, 0, 0, [0, 0]
    for name, n, units in SEGMENTS:
        rows, at = [], list(loads)
        t = 0
        for c, u in enumerate(units):
            slot = (unit + c) % 2
            at[slot] += 32 if u == "D" else 16
            rows.append((u, slot, at[slot], t))
            t += u != "M"
        per = [at[0] - loads[0], at[1] - loads[1]]
        table[name] = dict(n=n, rows=rows, unit=unit, tile=tile, chunk=chunk, per=per,
                           tiles=t, units=len(units))
        unit += n * len(units)
        tile += n * t
        chunk += n * ((units.count("M") + 3) // 4)
        loads = [loads[0] + n * per[0], loads[1] + n * per[1]]
    return table


SEG = stream_table()


class Chain:

    def __init__(self, eng, sem):
        self.eng, self.sem, self.base, self.n, self.at = eng, sem, 0, 0, None

    def enter(self, i, per):
        self.base += self.n
        self.at, self.per, self.n = i, per, 0

    def leave(self, times):
        assert self.n == self.per, (self.n, self.per)
        self.base, self.at, self.n = self.base + times * self.per, None, 0

    def link(self, ins):
        ins.then_inc(self.sem, 1)
        self.n += 1
        if self.at is None:
            self.eng.wait_ge(self.sem, self.base + self.n)
        else:
            self.eng.wait_ge(self.sem, self.at * self.per + (self.base + self.n))


def build(nc, x, p, w_in, w_pool, pool_scale, attn_sinks, w_out, ln1_g, ln1_b, w_ff1, w_ff2,
          ln2_g, ln2_b, w_ple, w_ple_gate, b_ple_gate, c_2, w_ada_2, b_ada_2, w_in_2, rel_rev,
          g_a_2, g_b_2, w_out_2, w_up_2, conv_w_2, conv_b_2, w_down_2, final_g_2, out):
    x, p, w_in, w_pool, w_out = x[0], p[0, 0], w_in[0], w_pool[0], w_out[0]
    w_ff1, w_ff2, w_ple, w_ple_gate = w_ff1[0], w_ff2[0], w_ple[0], w_ple_gate[0]
    w_ada, w_in2, w_out2, w_up, w_down = w_ada_2[0], w_in_2[0], w_out_2[0], w_up_2[0], w_down_2[0]
    out = out[0]

    ctx = ExitStack()
    with ctx:
        ctx.enter_context(nc.allow_non_contiguous_dma("per-feature vectors go to partitions"))

        def sem(name):
            return ctx.enter_context(nc.semaphore(name))

        top = [(nc.sbuf_base + 63) // 64 * 64]

        def region(nbytes):
            at = top[0]
            top[0] += nbytes
            return at

        def place(name, shape, dt, at):
            return nc.alloc_sbuf_tensor_at(name, shape, dt, offset=at)

        KB = 1024
        R_T = region(64 * KB)
        R_A = region(32 * KB)
        R_H = region(32 * KB)
        R_M = region(32 * KB)
        R_S = region(20 * KB)
        R_W = region(10 * KB)
        R_B = region(26 * KB)

        def small(name, shape, dt=F32):
            n = 4
            for s_ in shape[1:]:
                n *= s_
            return place(name, shape, dt, region((n + 31) // 32 * 32))

        actT_hi = place("actT_hi", [P, KT, S], F32R, R_T)
        actT_lo = place("actT_lo", [P, KT, S], F32R, R_T + 32 * KB)
        acc = place("acc", [P, RT, D], F32, R_A)
        ypool = place("ypool", [P, 4, S], F32, R_A)
        o1 = place("o1", [P, RT, HB], F32, R_A + 16 * KB)
        hid_hi = place("hid_hi", [P, 4, S], F32R, R_H)
        hid_lo = place("hid_lo", [P, 4, S], F32R, R_H + 16 * KB)
        rows2 = place("rows2", [P, RT, D], F32, R_H)
        rows3 = place("rows3", [P, RT, D], F32, R_M)
        p_rows = place("p_rows", [P, RT, 256], F32, R_H + 8 * KB)
        mv_hi = place("mv_hi", [P, 4, D], F32R, R_M)
        mv_lo = place("mv_lo", [P, 4, D], F32R, R_M + 16 * KB)

        def qkv_set(name, q_at, kv_at):
            return dict(
                q=(place(f"q_hi{name}", [P, S], F32R, q_at), place(f"q_lo{name}", [P, S], F32R, q_at + 4 * KB)),
                k=(place(f"k_hi{name}", [P, S], F32R, kv_at), place(f"k_lo{name}", [P, S], F32R, kv_at + 4 * KB)),
                v=(place(f"v_hi{name}", [P, RT, P], F32R, kv_at + 8 * KB),
                   place(f"v_lo{name}", [P, RT, P], F32R, kv_at + 12 * KB)))

        att1 = [qkv_set("1a", R_M, R_H + 8 * KB)]
        att1.append(dict(att1[0], q=(place("q_hi1b", [P, S], F32R, R_H + 24 * KB),
                                     place("q_lo1b", [P, S], F32R, R_H + 28 * KB))))
        att2 = [qkv_set("2a", R_M, R_M + 8 * KB), qkv_set("2b", R_A, R_A + 8 * KB)]
        evac_att = place("evac_att", [P, 2, S], F32, R_M + 24 * KB)
        v_cols = place("v_cols", [P, S], F32, R_A + 24 * KB)
        mw_hi = place("mw_hi", [P, 4, D], F32R, R_H)
        mw_lo = place("mw_lo", [P, 4, D], F32R, R_H + 16 * KB)
        st_hi = place("st_hi", [P, 2, 10, P], F32R, R_S)
        st_lo = place("st_lo", [P, 2, 10, P], F32R, R_S + 10 * KB)
        raw = place("raw", [P, 2, 10 * P], F32, R_W)
        evac = place("evac", [P, 2, S], F32, R_B)
        row_a = place("row_a", [P, D], F32, R_B + 8 * KB)
        row_b = place("row_b", [P, D], F32, R_B + 12 * KB)
        gprod = place("gprod", [P, 2, S], F32, R_B + 8 * KB)
        AW = 6 * D // 8
        ada_raw = place("ada_raw", [P, 2, AW], F32, R_B + 16 * KB)
        ada_acc = place("ada_acc", [P, AW], F32, R_B + 22 * KB)
        gated1 = place("gated1", [P, D], F32, R_B + 16 * KB)
        gated2 = place("gated2", [P, D], F32, R_B + 8 * KB)
        cv = place("cv", [P, 2, S], F32, R_B + 16 * KB)
        sq_junk = place("sq_junk", [P, D], F32, R_B + 20 * KB)
        row_g = place("row_g", [P, D], F32, R_B + 16 * KB)
        bias1 = place("bias1", [P, 8, 2 * P], F32, R_B)
        sums = place("sums", [P, 2, S], F32, R_B + 8 * KB)
        d_hi = place("d_hi", [P, S], F32R, R_B + 16 * KB)
        d_lo = place("d_lo", [P, S], F32R, R_B + 20 * KB)
        prob1 = place("prob1", [P, 2, 2 * P], F32, R_B + 8 * KB)
        pT1_hi = place("pT1_hi", [P, 2, 2 * P], F32R, R_B + 10 * KB)
        pT1_lo = place("pT1_lo", [P, 2, 2 * P], F32R, R_B + 12 * KB)
        NA = WA * P
        prob2 = place("prob2", [P, 2, NA], F32, R_B)
        pT2_hi = place("pT2_hi", [P, 2, NA], F32R, R_B + 5 * KB)
        pT2_lo = place("pT2_lo", [P, 2, NA], F32R, R_B + 10 * KB)
        bias2 = place("bias2", [P, 2, NA], F32, R_B + 15 * KB)
        bias_up = place("bias_up", [P, 2, NA], F32, R_B + 20 * KB)
        logit = place("logit", [P, 3, HB], F32, R_B)
        soft = place("soft", [P, 2, HB], F32, R_B + 6 * KB)
        sp_hi = place("sp_hi", [P, 2, HB], F32R, R_B + 10 * KB)
        sp_lo = place("sp_lo", [P, 2, HB], F32R, R_B + 14 * KB)
        wt_hi = place("wt_hi", [P, 2, HB], F32R, R_B + 18 * KB)
        wt_lo = place("wt_lo", [P, 2, HB], F32R, R_B + 22 * KB)
        pw = place("pw", [P, 4, P], F32, R_H)
        pwr_hi = place("pwr_hi", [P, 4, P], F32R, R_H + 2 * KB)
        pwr_lo = place("pwr_lo", [P, 4, P], F32R, R_H + 4 * KB)
        tri_f = place("tri_f", [P, 2, P], F32, R_H + 6 * KB)
        ident = small("ident", [P, P])
        flip = small("flip", [P, P])
        tri = small("tri", [P, 2, P], F32R)
        keep = small("keep", [P, P])
        drop = small("drop", [P, P])
        ones = small("ones", [P, P])
        diag = place("diag", [P, 16, P], F32, R_T + 32 * KB)
        modT = small("modT", [P, 48])
        b_ada = small("b_ada", [P, 48])
        c_col = small("c_col", [P, 8])
        c_act = small("c_act", [P, 8])
        pscale = small("pscale", [P, 4])
        b_gate = small("b_gate", [P, 8])
        gab = small("gab", [P, 8])
        cw = small("cw", [P, 3, 44])
        cb = small("cb", [P, 44])
        sink = small("sink", [P, 8])
        wcount = small("wcount", [P, 16])
        stats = small("stats", [P, 2, 6])
        mv2 = small("mv2", [P, 2, 2])
        std = small("std", [P, 2])
        rstd = small("rstd", [P, 1])
        nmr = small("nmr", [P, 1])
        ssq = small("ssq", [P, 16])
        rms = small("rms", [P, 16])
        rinv = small("rinv", [P, 16])
        mx = small("mx", [P, 16])
        nmx = small("nmx", [P, 16])
        den = small("den", [P, 16])
        sden = small("sden", [P, 16])
        eps = small("eps", [P, 2])
        tmp512 = small("tmp512", [P, 1])
        eps_one = small("eps_one", [P, 1])
        wcnt_i = small("wcnt_i", [P, 16], I32)
        assert top[0] <= nc.sbuf_usable_end, top[0]

        pd = ctx.enter_context(nc.psum_tensor("pd", [P, 2, 2 * HB], F32))
        pt = ctx.enter_context(nc.psum_tensor("pt", [P, 4, HB], F32))

        x_mid = nc.dram_tensor("x_mid", [S, D], F32).ap()
        ptT = pt[:, 2:4, :].rearrange("p a b -> p (a b)")

        ext = nc.dram_tensor("rel_ext", [8, 768], F32)

        raw_in = [sem("raw_in0"), sem("raw_in1")]
        split_hi = sem("split_hi")
        w_ready = sem("w_ready")
        tile_done = sem("tile_done")
        m_rows = sem("m_rows")
        t_free = sem("t_free")
        x_used = sem("x_used")
        m_free = sem("m_free")
        tp_done = sem("tp_done")
        tp_hi = sem("tp_hi")
        tp_lo = sem("tp_lo")
        jb_done = sem("jb_done")
        jb_hi = sem("jb_hi")
        jb_lo = sem("jb_lo")
        loads = sem("loads")
        mid_out = sem("mid_out")
        mid_in = sem("mid_in")
        x_in = [sem("x_in0"), sem("x_in1")]
        x_back = [sem(f"x_back{r}") for r in range(RT)]
        consts = sem("consts")
        setup = sem("setup")
        gsetup = sem("gsetup")
        vecs = sem("vecs")
        vchain = sem("vchain")
        achain = sem("achain")
        d_ready = sem("d_ready")
        pool_mm = sem("pool_mm")
        pool_out = sem("pool_out")
        pw_split = sem("pw_split")
        v_done = sem("v_done")
        s_done = sem("s_done")
        nm_ready = sem("nm_ready")
        p_ready = sem("p_ready")
        pt_done = sem("pt_done")
        pt_hi_s = sem("pt_hi_s")
        pt_lo_s = sem("pt_lo_s")
        pv_done = sem("pv_done")
        sink_e = sem("sink_e")
        yp_hi = sem("yp_hi")
        yp_lo = sem("yp_lo")
        row_rd = sem("row_rd")
        bias_cp = sem("bias_cp")
        gb_rows = sem("gb_rows")
        cv_done = sem("cv_done")
        silu_done = sem("silu_done")
        g_in = sem("g_in")
        act_one = sem("act_one")
        o_done = sem("o_done")
        row_done = sem("row_done")
        stat_in = sem("stat_in")
        std_done = sem("std_done")
        gb_in = sem("gb_in")
        ada_in = [sem("ada_in0"), sem("ada_in1")]
        ada_used = sem("ada_used")
        ada_full = sem("ada_full")
        ada_mm = sem("ada_mm")
        c_ready = sem("c_ready")
        p_in = sem("p_in")
        ple_done = sem("ple_done")
        ple_free = sem("ple_free")
        gp_ready = sem("gp_ready")
        gp_mm = sem("gp_mm")
        gp_added = sem("gp_added")
        ss_done = sem("ss_done")
        sq_done = sem("sq_done")
        diag_rdy = sem("diag_rdy")
        bc_mm = sem("bc_mm")
        ext_in = sem("ext_in")
        ext_out = sem("ext_out")
        bias_in = sem("bias_in")
        bias_mm = sem("bias_mm")
        bias_rdy = sem("bias_rdy")
        b_s = sem("b_s")
        b_l = sem("b_l")
        b_t = sem("b_t")
        b_exp = sem("b_exp")
        b_ln = sem("b_ln")
        b_sp = sem("b_sp")
        b_c = sem("b_c")
        b_sub = sem("b_sub")
        b_w = sem("b_w")
        b_ws = sem("b_ws")
        b_pv = sem("b_pv")
        fin_rdy = sem("fin_rdy")
        stored = [sem("stored0"), sem("stored1")]

        def row_base(name):
            return {"h1": 0, "h2": 8}[name]

        TILE = {n: SEG[n]["tile"] for n in SEG}
        CH = {n: SEG[n]["chunk"] for n in SEG}
        UN = {n: SEG[n]["unit"] for n in SEG}
        T_FF, T_UP = TILE["ffa"], TILE["upa"]
        NC2 = SEG["up"]["n"]
        order = [s_[0] for s_ in SEGMENTS]

        TPJ, n_ = {}, 0
        for name, k in (("x", 16), ("o1", 8), ("h1", 16), ("h2", 16), ("p", 4), ("m1", 16), ("o2", 16), ("m2", 16)):
            TPJ[name] = n_
            n_ += k

        BSTEPS = [(hh, hf, kt) for hh in range(2) for hf in range(2) for kt in range(4 * hf + 3, -1, -1)]
        NB = len(BSTEPS)

        def bcols(hf, kt):
            q0 = max(kt * P, hf * HB)
            return q0, (hf + 1) * HB - q0, q0 - hf * HB

        JOBS1 = [("Q", 0), ("Q", 1)]
        JOBS2 = [("V", 0), ("V", 1), ("Q", 0), ("Q", 1), ("K", 0), ("K", 1), ("T", 0), ("T", 1)]
        NJ1, NJ2, NL2 = len(JOBS1), len(JOBS2), 6

        def job_plan(jobs, before, steps, total):
            work = [(e, kind, half, k) for e, (kind, half) in enumerate(jobs) if kind != "T" for k in range(KT)]
            parts = [[] for _ in range(total)]
            rest = work[before:]
            for g, w in enumerate(rest):
                parts[g * steps // len(rest)].append(w)
            for e, (kind, half) in enumerate(jobs):
                if kind == "T":
                    parts[total - 2 + half].append((e, kind, half, KT - 1))
            return work[:before], parts

        def s_at(W, s):
            return (s % 2) * HB if W * P <= HB else 0

        def ahead(W):
            return 2 if W * P <= HB else 1

        PLAN1 = job_plan(JOBS1, 0, 14, 16)
        PLAN_A = job_plan(JOBS2, KT, 14, 16)
        PLAN_B = job_plan(JOBS2, 0, 21, NB)
        PLAN_ALONE = job_plan(JOBS2, 0, 14, 16)

        def ended(part):
            return [(e, kind, half) for e, kind, half, k in part if k == KT - 1]

        block = ctx.enter_context(nc.Block())

        @block.sync
        def _(sp):
            w_in_t = w_in.rearrange("(k p) n -> p k n", p=P)
            ff1_t = w_ff1.rearrange("(k p) n -> p k n", p=P)
            gate_t = w_ple_gate.rearrange("(k p) n -> p k n", p=P)
            ple_t = w_ple.rearrange("(k p) n -> p k n", p=P)
            in2_t = w_in2.rearrange("(k p) n -> p k n", p=P)
            up_t = w_up.rearrange("(k p) n -> p k n", p=P)

            def raw_k(slot, a, b):
                return raw[:, slot, a * P:b * P].rearrange("p (k n) -> p k n", n=P)

            def room(name, i, c):
                g = UN[name] + c
                if i is None:
                    if g >= 2:
                        sp.wait_ge(w_ready, g - 1)
                else:
                    sp.wait_ge(w_ready, i * SEG[name]["units"] + (g - 1))

            for r in range(RT):
                sp.dma_start(acc[:, r, :], x[r * P:(r + 1) * P, :]).then_inc(x_in[r // 4], 16)
            for c, (u, slot, _, _) in enumerate(SEG["in"]["rows"]):
                room("in", None, c)
                if c < 6:
                    col = c * P if c < 4 else 1024 + (c - 4) * P
                    sp.dma_start(raw_k(slot, 0, 8), w_in_t[:, :, col:col + P]).then_inc(raw_in[slot], 16)
                else:
                    for hh in range(2):
                        col = 512 + 64 * (c - 6) + 256 * hh
                        sp.dma_start(raw_k(slot, 0, 8)[:, :, 64 * hh:64 * hh + 64],
                                     w_in_t[:, :, col:col + 64]).then_inc(raw_in[slot], 16)
            def out_unit(c):
                room("out", None, c)
                slot = SEG["out"]["rows"][c][1]
                sp.dma_start(raw[:, slot, 0:D], w_out[c * P:(c + 1) * P, :]).then_inc(raw_in[slot], 16)

            for c in range(6):
                out_unit(c)
            sp.wait_ge(tp_done, TPJ["o1"] + 8)
            sp.wait_ge(yp_lo, 4)
            for r in range(RT):
                sp.dma_start(acc[:, r, :], x[r * P:(r + 1) * P, :]).then_inc(x_back[r], 16)
            for c in range(6, 8):
                out_unit(c)

            def ff_units(name, i, i0):
                m, t = 0, 0 if name == "ffa" else 3
                for c, (u, slot, _, _) in enumerate(SEG[name]["rows"]):
                    room(name, None if isinstance(i, int) else i, c)
                    if u == "S":
                        sp.dma_start(raw_k(slot, 0, 8), ff1_t[:, :, ds((i * 4 + (4 * i0 + t)) * P, P)])\
                            .then_inc(raw_in[slot], 16)
                        t += 1
                    else:
                        sp.dma_start(raw[:, slot, 0:D], w_ff2[ds((i * 4 + (4 * i0 + m)) * P, P), :])\
                            .then_inc(raw_in[slot], 16)
                        m += 1

            ff_units("ffa", 0, 0)
            with sp.Fori(0, SEG["ff"]["n"]) as i:
                ff_units("ff", i, 0)
            ff_units("ffb", 0, SEG["ff"]["n"])
            with sp.Fori(0, SEG["gate"]["n"]) as i:
                for c, (u, slot, _, _) in enumerate(SEG["gate"]["rows"]):
                    room("gate", i, c)
                    sp.dma_start(raw_k(slot, 0, 8), gate_t[:, :, ds((i * 2 + c) * P, P)]).then_inc(raw_in[slot], 16)
                    sp.dma_start(raw_k(slot, 8, 10), ple_t[:, :, ds((i * 2 + c) * P, P)]).then_inc(raw_in[slot], 16)
            sp.wait_ge(x_used, TILE["in2a"])
            for r in range(RT):
                sp.dma_start(x_mid[r * P:(r + 1) * P, :], acc[:, r, :]).then_inc(mid_out, 16)
            for name, base in (("in2a", 0), ("in2b", 1536)):
                with sp.Fori(0, SEG[name]["n"]) as i:
                    for c, (u, slot, _, _) in enumerate(SEG[name]["rows"]):
                        room(name, i, c)
                        at = (base + (c + 2) % 3 * 512) // P + c // 3
                        sp.dma_start(raw_k(slot, 0, 8), in2_t[:, :, ds((i * 2 + at) * P, P)]).then_inc(raw_in[slot], 16)
            for c, (u, slot, _, _) in enumerate(SEG["out2"]["rows"]):
                room("out2", None, c)
                sp.dma_start(raw[:, slot, 0:D], w_out2[c * P:(c + 1) * P, :]).then_inc(raw_in[slot], 16)

            def up_units(name, i, i0):
                m, t = 0, 0 if name == "upa" else 3
                for c, (u, slot, _, _) in enumerate(SEG[name]["rows"]):
                    room(name, None if isinstance(i, int) else i, c)
                    sp.sem_inc(loads, 1)
                    if u == "S":
                        col = (i * 4 + (t // 2 + (t % 2) * (DFF2 // P) + i0 * 4)) * P
                        sp.dma_start(raw_k(slot, 0, 8), up_t[:, :, ds(col, P)]).then_inc(raw_in[slot], 16)
                        t += 1
                    else:
                        row = (i * 4 + (m + i0 * 4)) * P
                        sp.dma_start(raw[:, slot, 0:D], w_down[ds(row, P), :]).then_inc(raw_in[slot], 16)
                        m += 1

            up_units("upa", 0, 0)
            with sp.Fori(0, NC2) as i:
                up_units("up", i, 0)
            up_units("upb", 0, NC2)
            for r in range(RT):
                sp.wait_ge(fin_rdy, r + 1)
                sp.dma_start(out[r * P:(r + 1) * P, :], evac[:, r % 2, :]).then_inc(stored[r % 2], 16)
            sp.wait_ge(stored[0], 64)
            sp.wait_ge(stored[1], 64)

        @block.gpsimd
        def _(pool):
            g_n = [0]

            def then(ins):
                g_n[0] += 1
                ins.then_inc(gsetup, 1)

            then(pool.memset(ident[:, :], 0.0))
            then(pool.memset(flip[:, :], 0.0))
            then(pool.memset(ones[:, :], 1.0))
            then(pool.memset(tri_f[:, :, :], 1.0))
            then(pool.memset(keep[:, :], 1.0))
            then(pool.memset(drop[:, :], 0.0))
            then(pool.memset(eps[:, 0:1], LN_EPS))
            then(pool.memset(eps[:, 1:2], RMS_EPS))
            then(pool.iota(wcnt_i[:, :], pattern=[[1, 16]], base=1, channel_multiplier=0))
            then(pool.iota(bias1[:, 0, :].bitcast(I32), pattern=[[1, 2 * P]], base=-P, channel_multiplier=-1))
            pool.wait_ge(gsetup, g_n[0])
            then(pool.tensor_copy(bias1[:, 7, :], bias1[:, 0, :].bitcast(I32)))
            then(pool.affine_select(out=ident[:, :], in_=ident[:, :], compare_op=ALU.not_equal, fill=1.0,
                                    base=0, pattern=[[-1, P]], channel_multiplier=1))
            then(pool.affine_select(out=flip[:, :], in_=flip[:, :], compare_op=ALU.not_equal, fill=1.0,
                                    base=-(P - 1), pattern=[[1, P]], channel_multiplier=1))
            then(pool.affine_select(out=tri_f[:, 0, :], in_=tri_f[:, 0, :], compare_op=ALU.is_ge, fill=0.0,
                                    base=0, pattern=[[-1, P]], channel_multiplier=1))
            then(pool.affine_select(out=tri_f[:, 1, :], in_=tri_f[:, 1, :], compare_op=ALU.is_gt, fill=0.0,
                                    base=0, pattern=[[1, P]], channel_multiplier=-1))
            then(pool.affine_select(out=keep[:, :], in_=keep[:, :], compare_op=ALU.is_gt, fill=0.0,
                                    base=0, pattern=[[1, P]], channel_multiplier=-1))
            then(pool.affine_select(out=drop[:, :], in_=drop[:, :], compare_op=ALU.is_gt, fill=-BIG,
                                    base=0, pattern=[[1, P]], channel_multiplier=-1))
            pool.wait_ge(gsetup, g_n[0])
            for h in range(8):
                if h == 7:
                    pool.wait_ge(gsetup, g_n[0])
                then(pool.tensor_scalar(bias1[:, h, :], bias1[:, 7, :], 2.0 ** -(h + 1), None, ALU.mult))
            pool.wait_ge(gsetup, g_n[0])
            then(pool.affine_select(out=bias1[:, :, :], in_=bias1[:, :, :], compare_op=ALU.is_ge, fill=-BIG,
                                    base=P, pattern=[[0, 8], [-1, 2 * P]], channel_multiplier=1))
            pool.wait_ge(gsetup, g_n[0])
            pool.affine_select(out=bias1[:, :, :], in_=bias1[:, :, :], compare_op=ALU.is_gt, fill=-BIG,
                               base=0, pattern=[[0, 8], [1, 2 * P]], channel_multiplier=-1).then_inc(consts, 1)

            def split(name, i, c):
                seg = SEG[name]
                u, slot, load, t = seg["rows"][c]
                g, size = UN[name] + c, (10 * P if name == "gate" else 8 * P)
                at = 0 if i is None else i

                def val(per, base):
                    return base if i is None else at * per + base
                pool.wait_ge(raw_in[slot], val(seg["per"][slot], load))
                if u == "M":
                    m = sum(r_[0] == "M" for r_ in seg["rows"][:c])
                    j, ch = m % 4, CH[name] + m // 4
                    if name == "out" and m == 0:
                        pool.wait_ge(s_done, 48)
                    if name == "out2" and m == 0:
                        pool.wait_ge(b_pv, 3 * NB)
                    if name in ("out", "out2") and m >= 4:
                        if m == 4 and name == "out":
                            pool.wait_ge(pv_done, 64)
                        elif m == 4:
                            pool.wait_ge(tp_done, TPJ["o2"] + 16)
                        hi, lo = mw_hi[:, j, :], mw_lo[:, j, :]
                    else:
                        if j == 0 and ch > 0:
                            pool.wait_ge(m_rows, val(8, 8 * ch))
                        hi, lo = mv_hi[:, j, :], mv_lo[:, j, :]
                else:
                    T = TILE[name] + t
                    if name in ("in2a", "in2b"):
                        w = T - TILE["in2a"] - 2
                        pool.wait_ge(jb_done, val(2 * NJ2, 4 * NJ1 + NJ2 * (w // 3) + 2 * (w % 3) + 2))
                    elif name == "in" and T >= 8:
                        pool.wait_ge(jb_done, NJ1 * (T - 7))
                    elif i is not None or T >= 2:
                        pool.wait_ge(tile_done, val(seg["tiles"], T - 1))
                    hi = st_hi[:, T % 2, 0:size // P, :].rearrange("p k n -> p (k n)")
                    lo = st_lo[:, T % 2, 0:size // P, :].rearrange("p k n -> p (k n)")
                src = raw[:, slot, 0:size]
                nk = size // P
                pool.tensor_tensor(hi.rearrange("p (k n) -> p k n", n=P), src.rearrange("p (k n) -> p k n", n=P),
                                   ones[:, :].unsqueeze(1).to_broadcast([P, nk, P]), ALU.mult).then_inc(split_hi, 1)
                pool.wait_ge(split_hi, val(seg["units"], g + 1))
                pool.tensor_tensor(lo, src, hi.bitcast(F32), ALU.subtract).then_inc(w_ready, 1)

            for name in order:
                if name == "up":
                    pool.wait_ge(tp_done, TPJ["m2"] + 16)
                if name == "in2a":
                    pool.wait_ge(tile_done, TILE["in2a"])
                if SEG[name]["n"] == 1:
                    for c in range(SEG[name]["units"]):
                        split(name, None, c)
                else:
                    with pool.Fori(0, SEG[name]["n"]) as i:
                        for c in range(SEG[name]["units"]):
                            split(name, i, c)

        @block.tensor
        def _(pe):
            pe.wait_ge(consts, 1)

            def passes(out_ap, a_hi, a_lo, b_hi, b_lo, start, stop, check=False):
                pe.matmul(out_ap, a_hi, b_hi, start=start, stop=False, skip_group_check=check)
                pe.matmul(out_ap, a_hi, b_lo, start=False, stop=False, skip_group_check=check)
                return pe.matmul(out_ap, a_lo, b_hi, start=False, stop=stop, skip_group_check=check)

            def transposes(name, src, kts, halves=(0, 1)):
                for half in halves:
                    for n, kt in enumerate(kts):
                        job = TPJ[name] + half * len(kts) + n
                        if job >= 4:
                            pe.wait_ge(tp_lo, job - 3)
                        for r in range(4):
                            last = pe.transpose(pt[:, job % 4, r * P:(r + 1) * P],
                                                src[:, half * 4 + r, kt * P:(kt + 1) * P], ident[:, :])
                        last.then_inc(tp_done, 1)

            def tile_mm(slot, halves=None, nk=8):
                for half in range(2):
                    if halves:
                        halves(half)
                    for k in range(nk):
                        last = passes(pd[:, slot, half * HB:(half + 1) * HB], st_hi[:, slot, k, :],
                                      st_lo[:, slot, k, :], actT_hi[:, k, half * HB:(half + 1) * HB],
                                      actT_lo[:, k, half * HB:(half + 1) * HB], k == 0, k == nk - 1)
                return last

            def turned(name):
                return lambda half: pe.wait_ge(tp_lo, TPJ[name] + 8 * (half + 1))

            def tile(i, per_u, u, per_t, t, rows=None, halves=None):
                pe.wait_ge(w_ready, i * per_u + (u + 1))
                if not isinstance(i, int) or t + per_t * i >= 2:
                    pe.wait_ge(t_free, i * per_t + (t - 1))
                if rows is not None:
                    pe.wait_ge(m_free, i * 8 + rows)
                tile_mm(t % 2, halves).then_inc(tile_done, 1)

            def row_mm(r, hi, lo, ks, nk, w):
                slot = (r + 1) % 2
                for n in range(2):
                    for j in range(nk):
                        last = passes(pd[:, slot, n * HB:(n + 1) * HB], hi[:, ks + j, r * P:(r + 1) * P],
                                      lo[:, ks + j, r * P:(r + 1) * P], w[0][:, j, n * HB:(n + 1) * HB],
                                      w[1][:, j, n * HB:(n + 1) * HB], j == 0, j == nk - 1)
                last.then_inc(m_rows, 1)

            def row(r, i, ch, hi, lo, ks, nk, w, tiles=None):
                if r < 2 and tiles is not None:
                    pe.wait_ge(t_free, tiles)
                if not isinstance(i, int) or 8 * (ch + i) + r >= 2:
                    pe.wait_ge(m_free, i * 8 + (8 * ch + r - 1))
                row_mm(r, hi, lo, ks, nk, w)

            for half in range(2):
                pe.wait_ge(x_in[half], 64)
                transposes("x", acc, range(8), (half,))

            def pool_mix(g):
                pe.wait_ge(d_ready, g + 1)
                pe.wait_ge(pw_split, 1)
                if g:
                    pe.wait_ge(pool_out, g)
                for half in range(2):
                    last = passes(pt[:, half, :], pwr_hi[:, g, :], pwr_lo[:, g, :],
                                  d_hi[:, half * HB:(half + 1) * HB], d_lo[:, half * HB:(half + 1) * HB],
                                  True, True)
                last.then_inc(pool_mm, 1)

            def v_rows(t):
                pe.wait_ge(t_free, t + 1)
                for r in range(RT):
                    last = pe.transpose(pt[:, 2 + r // 4, (r % 4) * P:(r % 4 + 1) * P],
                                        evac_att[:, t % 2, r * P:(r + 1) * P], ident[:, :])
                last.then_inc(v_done, 1)

            def product(bank, slot, half, k):
                return passes(pd[:, 0, bank * HB:(bank + 1) * HB], st_hi[:, slot, k, :], st_lo[:, slot, k, :],
                              actT_hi[:, k, half * HB:(half + 1) * HB], actT_lo[:, k, half * HB:(half + 1) * HB],
                              k == 0, k == KT - 1)

            def jobs1(j, part):
                for e, _, half, k in part:
                    if k == 0:
                        if half == 0:
                            pe.wait_ge(w_ready, 7 + j)
                        if j:
                            pe.wait_ge(jb_lo, NJ1 * j + e - 1)
                    last = product(half, j % 2, half, k)
                    if k == KT - 1:
                        last.then_inc(jb_done, 1)

            def jobs2(i, q, part):
                for e, kind, half, k in part:
                    if k == 0 or kind == "T":
                        if kind != "T" and half == 0:
                            pe.wait_ge(w_ready, i * 6 + (UN["in2a"] + 3 * q + e // 2 + 1))
                        if e in (2, 3):
                            pe.wait_ge(jb_hi, i * (2 * NJ2) + (4 * NJ1 + NJ2 * q + e - 1))
                        elif e < 2:
                            pe.wait_ge(jb_lo, i * (2 * NL2) + (4 * NJ1 + NL2 * q + e - 1))
                        else:
                            pe.wait_ge(jb_lo, i * (2 * NL2) + (4 * NJ1 + NL2 * q + e - 3))
                    if kind == "T":
                        for r in range(4):
                            last = pe.transpose(pd[:, 0, half * HB + r * P:half * HB + (r + 1) * P],
                                                v_cols[:, (4 * half + r) * P:(4 * half + r + 1) * P], ident[:, :])
                    else:
                        last = product(half, (3 * q + e // 2) % 2, half, k)
                    if k == KT - 1:
                        last.then_inc(jb_done, 1)

            def soft_pair(W, prob, pT_hi, pT_lo, kv, st, i, per, pair, qk_ready, v_ready, before, beside):
                (q_hi, q_lo), (k_hi, k_lo), (v_hi, v_lo) = kv["q"], kv["k"], kv["v"]

                def scores(s):
                    hh, qt = s // 8, s % 8
                    n = min(qt, W - 1) + 1
                    k0 = (qt - n + 1) * P
                    if s >= ahead(W):
                        pe.wait_ge(nm_ready, i * per + (st + s + 1 - ahead(W)))
                    elif s == 0:
                        qk_ready()
                    b = slice(64 * hh, 64 * hh + 64)
                    for c0 in range(0, n * P, HB):
                        c1 = min(c0 + HB, n * P)
                        last = passes(pd[:, 1, s_at(W, s) + c0:s_at(W, s) + c1], q_hi[b, qt * P:(qt + 1) * P],
                                      q_lo[b, qt * P:(qt + 1) * P], k_hi[b, k0 + c0:k0 + c1],
                                      k_lo[b, k0 + c0:k0 + c1], True, True)
                    last.then_inc(s_done, 1)

                def turn(s):
                    pe.wait_ge(p_ready, i * per + (st + s + 1))
                    if s >= ahead(W):
                        pe.wait_ge(pt_lo_s, i * per + (st + s + 1 - ahead(W)))
                    for j in range(min(s % 8, W - 1) + 1):
                        last = pe.transpose(ptT[:, s_at(W, s) + j * P:s_at(W, s) + (j + 1) * P],
                                            prob[:, s % 2, j * P:(j + 1) * P], ident[:, :])
                    last.then_inc(pt_done, 1)

                def outputs(s):
                    hh, qt = s // 8, s % 8
                    n = min(qt, W - 1) + 1
                    if s == 0:
                        v_ready()
                        if st or pair:
                            pe.wait_ge(o_done, i * 2 + pair)
                    pe.wait_ge(pt_lo_s, i * per + (st + s + 1))
                    for j in range(n):
                        kt = qt - n + 1 + j
                        last = passes(pt[:, hh, qt * 64:(qt + 1) * 64], pT_hi[:, s % 2, j * P:(j + 1) * P],
                                      pT_lo[:, s % 2, j * P:(j + 1) * P], v_hi[:, kt, 64 * hh:64 * hh + 64],
                                      v_lo[:, kt, 64 * hh:64 * hh + 64], j == 0, j == n - 1)
                    last.then_inc(pv_done, 1)

                scores(0)
                before()
                for s in range(16):
                    if s + 1 < 16:
                        scores(s + 1)
                    beside(s)
                    turn(s)
                    if s:
                        outputs(s - 1)
                outputs(15)

            for t in range(6):
                tile(0, 0, t, 0, t, None, turned("x") if t == 0 else None)
                if t == 5:
                    pool_mix(3)
                elif 1 <= t <= 3:
                    pool_mix(t - 1)
            v_rows(5)
            pe.wait_ge(t_free, 6)
            for part in PLAN1[1]:
                jobs1(0, part)

            def nothing(s=0):
                pass

            for j in range(4):
                soft_pair(W1, prob1, pT1_hi, pT1_lo, att1[j % 2], 16 * j, 0, 0, j,
                          lambda: pe.wait_ge(jb_lo, NJ1 * j + 2),
                          lambda: pe.wait_ge(x_used, 6),
                          nothing, lambda s: jobs1(j + 1, PLAN1[1][s]) if j < 3 else None)
            pe.wait_ge(o_done, 4)
            pe.sem_inc(tile_done, 4)
            transposes("o1", o1, range(4))

            def out_chunks(ch, u, hi, lo, name, tiles, second=None):
                for c in range(2):
                    pe.wait_ge(w_ready, u + 4 * c + 4)
                    for r in range(RT):
                        if second and (c, r) == (0, 4):
                            second()
                        row(r, 0, ch + c, hi, lo, 4 * c, 4, (mw_hi, mw_lo) if c else (mv_hi, mv_lo), tiles)
                        if c == 1 and name and r == 6:
                            pe.wait_ge(row_done, row_base(name) + 4)
                            transposes(name, acc, range(8), (0,))
                if name:
                    pe.wait_ge(row_done, row_base(name) + 8)
                    transposes(name, acc, range(8), (1,))

            pe.wait_ge(yp_lo, 4)
            pe.wait_ge(tp_lo, TPJ["o1"] + 8)
            out_chunks(0, UN["out"], actT_hi, actT_lo, "h1", 10)


            def chunk_tile(name, i, j, n, rows=None):
                unit = j - 3 if j < 3 else 2 if j == 3 else j + 1
                per = SEG[name]["units"]
                tile(i, per, UN[name] + unit, n, (T_FF if name == "ff" else T_UP) + j, rows)

            def ff_chunk(i, last=False):
                for j in (1, 2, 3):
                    chunk_tile("ff", i, j, 4, 8 * CH["ff"] - 2 + j if j < 3 else None)
                if not last:
                    chunk_tile("ff", i, 4, 4)
                pe.wait_ge(x_used, i * 4 + (T_FF + 4))
                pe.wait_ge(w_ready, i * 8 + (UN["ff"] + 5))
                for r in range(RT):
                    if r < 2:
                        pe.wait_ge(t_free, i * 4 + (T_FF + 4 + (r == 1 and not last)))
                    row(r, i, CH["ff"], hid_hi, hid_lo, 0, 4, (mv_hi, mv_lo))
                    if r == 0:
                        pe.wait_ge(ada_full, i + 1)
                        for j in range(AW // P):
                            ada = pe.matmul(pt[:, 3, j:j + 1], ada_acc[:, j * P:(j + 1) * P], ones[:, 0:1],
                                            start=True, stop=True)
                        ada.then_inc(ada_mm, 1)
                    if last and r == 6:
                        pe.wait_ge(row_done, 12)
                        transposes("h2", acc, range(8), (0,))

            tile(0, 0, UN["ffa"], 0, T_FF, 16, turned("h1"))
            with pe.Fori(0, 7) as i:
                ff_chunk(i)
            ff_chunk(7, True)
            pe.wait_ge(row_done, 16)
            transposes("h2", acc, range(8), (1,))
            pe.wait_ge(p_in, 16)
            transposes("p", p_rows, range(2))
            pe.wait_ge(tp_lo, TPJ["p"] + 4)

            def gate_tile(i, c):
                pe.wait_ge(w_ready, i * 2 + (UN["gate"] + c + 1))
                pe.wait_ge(m_free, 80)
                pe.wait_ge(ple_free, i * 2 + (c + 1))
                for half in range(2):
                    for k in range(2):
                        last = passes(pd[:, 0, half * HB:(half + 1) * HB], st_hi[:, c, 8 + k, :],
                                      st_lo[:, c, 8 + k, :], hid_hi[:, k, half * HB:(half + 1) * HB],
                                      hid_lo[:, k, half * HB:(half + 1) * HB], k == 0, k == 1)
                last.then_inc(ple_done, 1)
                pe.wait_ge(t_free, i * 2 + (TILE["gate"] + c))
                for half in range(2):
                    for k in range(8):
                        last = passes(pd[:, 1, half * HB:(half + 1) * HB], st_hi[:, c, k, :],
                                      st_lo[:, c, k, :], actT_hi[:, k, half * HB:(half + 1) * HB],
                                      actT_lo[:, k, half * HB:(half + 1) * HB], k == 0, k == 7)
                last.then_inc(tile_done, 1)

            def gate_back(i, c):
                pe.wait_ge(gp_ready, i * 2 + (c + 2))
                pe.wait_ge(x_used, i * 2 + (TILE["gate"] + c - 1))
                for r in range(RT):
                    last = pe.transpose(pt[:, 2 * c + r // 4, (r % 4) * P:(r % 4 + 1) * P],
                                        gprod[:, c, r * P:(r + 1) * P], ident[:, :])
                last.then_inc(gp_mm, 1)

            with pe.Fori(0, 4) as i:
                gate_tile(i, 0)
                gate_tile(i, 1)
                gate_back(i, 0)
                gate_back(i, 1)

            def norm_transposes(name, rows, src=rows2):
                for half in range(2):
                    pe.wait_ge(row_rd, rows + 4 * (half + 1))
                    transposes(name, src, range(8), (half,))

            norm_transposes("m1", 0)

            def bias_flip(i, pp):
                pe.wait_ge(bias_in, i * 32 + (16 * pp + 16))
                for hh in range(2):
                    if hh:
                        pe.wait_ge(bias_cp, i * 4 + (2 * pp + hh))
                    for c0 in range(0, NA, HB):
                        c1 = min(c0 + HB, NA)
                        last = pe.matmul(pt[:, 2 + c0 // HB, 0:c1 - c0], flip[:, :], bias_up[:, hh, c0:c1],
                                         start=True, stop=True)
                    last.then_inc(bias_mm, 1)

            pe.wait_ge(t_free, TILE["in2a"])
            pe.wait_ge(tp_lo, TPJ["m1"] + 8)
            for part in PLAN_ALONE[1]:
                for e, kind, half, k in part:
                    if (e, k) == (1, 0):
                        pe.wait_ge(tp_lo, TPJ["m1"] + 16)
                    jobs2(0, 0, [(e, kind, half, k)])

            def a_ready(i, pp, n):
                pe.wait_ge(jb_lo, i * (2 * NL2) + (4 * NJ1 + NL2 * pp + n))

            with pe.Fori(0, 2) as i:
                for pp in range(2):
                    def before():
                        jobs2(i, pp + 1, PLAN_A[0])
                        bias_flip(i, pp)

                    soft_pair(WA, prob2, pT2_hi, pT2_lo, att2[pp], 64 + 16 * pp, i, 32, 4 + pp,
                              lambda: a_ready(i, pp, 4), lambda: a_ready(i, pp, 6),
                              before, lambda s: jobs2(i, pp + 1, PLAN_A[1][s]))

            def stick_pair(pair, kv):
                (q_hi, q_lo), (k_hi, k_lo), (v_hi, v_lo) = kv["q"], kv["k"], kv["v"]

                def at(sem_, n):
                    pe.wait_ge(sem_, NB * pair + n)

                def seg(s):
                    return BSTEPS[s][0] * 2 + BSTEPS[s][1]

                def scores(s):
                    hh, hf, kt = BSTEPS[s]
                    q0, n, _ = bcols(hf, kt)
                    if s >= 2:
                        at(b_l, s - 1)
                    elif s == 0:
                        pe.wait_ge(jb_lo, 4 * NJ1 + NL2 * (4 + pair) + 4)
                    b = slice(64 * hh, 64 * hh + 64)
                    passes(pd[:, 1, (s % 2) * HB:(s % 2) * HB + n], k_hi[b, kt * P:(kt + 1) * P], k_lo[b, kt * P:(kt + 1) * P],
                           q_hi[b, q0:q0 + n], q_lo[b, q0:q0 + n], True, True).then_inc(b_s, 1)

                def sums_of(s, which, sm):
                    hh, hf, kt = BSTEPS[s]
                    _, n, co = bcols(hf, kt)
                    first = which == 0 and (s == 0 or seg(s) != seg(s - 1))
                    o = pt[:, 2 + seg(s) % 2, co:co + n]
                    pe.matmul(o, tri[:, which, :], sp_hi[:, s % 2, 0:n], start=first, stop=False,
                              skip_group_check=True)
                    last = pe.matmul(o, tri[:, which, :], sp_lo[:, s % 2, 0:n], start=False, stop=True,
                                     skip_group_check=True)
                    if sm is not None:
                        last.then_inc(sm, 1)

                def outputs(s):
                    hh, hf, kt = BSTEPS[s]
                    q0, n, _ = bcols(hf, kt)
                    if s == 0:
                        pe.wait_ge(jb_lo, 4 * NJ1 + NL2 * (5 + pair))
                        pe.wait_ge(o_done, 8 + pair)
                    at(b_ws, s + 1)
                    for j in range(n // P):
                        qt = q0 // P + j
                        last = passes(pt[:, hh, qt * 64:(qt + 1) * 64], wt_hi[:, s % 2, j * P:(j + 1) * P],
                                      wt_lo[:, s % 2, j * P:(j + 1) * P], v_hi[:, kt, 64 * hh:64 * hh + 64],
                                      v_lo[:, kt, 64 * hh:64 * hh + 64], s % 12 == 0 and j == 0, False, True)
                    last.then_inc(b_pv, 1)

                scores(0)
                for s in range(NB + 2):
                    if s + 1 < NB:
                        scores(s + 1)
                    if s < NB and pair < 3:
                        jobs2(0, 5 + pair, PLAN_B[1][s])
                    if 2 <= s:
                        at(b_sub, s - 1)
                        if s - 1 < NB and seg(s - 1) == seg(s - 2):
                            sums_of(s - 2, 1, None)
                    if 1 <= s <= NB:
                        at(b_sp, s)
                        sums_of(s - 1, 0, b_c)
                    if 2 <= s:
                        outputs(s - 2)

            for pair in range(4):
                stick_pair(pair, att2[pair % 2])

            pe.wait_ge(o_done, 12)
            pe.sem_inc(tile_done, 24)
            pe.wait_ge(diag_rdy, 1)
            for n in range(16):
                last = pe.matmul(pt[:, n // 4, (n % 4) * P:(n % 4 + 1) * P], ones[:, :], diag[:, n, :],
                                 start=True, stop=True)
            last.then_inc(bc_mm, 1)
            pe.wait_ge(gb_rows, 2)
            norm_transposes("o2", 8)
            pe.wait_ge(tp_lo, TPJ["o2"] + 8)
            out_chunks(CH["out2"], UN["out2"], actT_hi, actT_lo, None, TILE["upa"],
                       lambda: pe.wait_ge(tp_lo, TPJ["o2"] + 16))
            norm_transposes("m2", 16, rows3)

            def up_chunk(i, nh, last=False):
                for j in range(1, 2 * nh + (not last)):
                    chunk_tile("up", i, j, 8, 8 * CH["up"] - 2 + j if j < 3 else None)
                pe.wait_ge(x_used, i * 8 + (T_UP + 2 * nh))
                pe.wait_ge(w_ready, i * 12 + (UN["up"] + nh + (nh > 2)))
                for r in range(RT):
                    if r < 2:
                        pe.wait_ge(t_free, i * 8 + (T_UP + 2 * nh + (r == 1 and not last)))
                    row(r, i, CH["up"], hid_hi, hid_lo, 0, nh, (mv_hi, mv_lo))

            tile(0, 0, UN["upa"], 0, T_UP, 8 * CH["up"], turned("m2"))
            with pe.Fori(0, NC2) as i:
                up_chunk(i, 4)
            up_chunk(NC2, 2, True)

        @block.scalar
        def _(act):
            def vec(out_ap, in_ap):
                act.dma_start(out_ap, in_ap).then_inc(vecs, 16)

            def spread(a, off, n):
                return bass.AP(a.tensor, off, [[0, P], [1, n]])

            vec(pw[:, :, :], w_pool.rearrange("g c d -> c g d"))
            vec(pscale[:, :], pool_scale[0].rearrange("(g p) -> p g", p=P))
            vec(sink[:, :], spread(attn_sinks, 0, 8))
            vec(c_col[:, :], c_2[0].rearrange("(k p) -> p k", p=P))
            vec(b_ada[:, :], b_ada_2[0].rearrange("(k p) -> p k", p=P))
            vec(b_gate[:, :], b_ple_gate[0].rearrange("(k p) -> p k", p=P))
            vec(gab[:, 0:4], g_a_2[0].rearrange("(k p) -> p k", p=P))
            vec(gab[:, 4:8], g_b_2[0].rearrange("(k p) -> p k", p=P))
            vec(cw[:, :, :], conv_w_2[0].rearrange("w (k p) -> p w k", p=P))
            vec(cb[:, :], conv_b_2[0].rearrange("(k p) -> p k", p=P))

            act.wait_ge(act_one, 1)
            act.activation(tmp512[:, :], eps_one[:, :], ACT.Copy).then_inc(ple_free, 1)

            def tp_plain(name, n, hi_of, lanes=1):
                for b in n:
                    job = TPJ[name] + b
                    act.wait_ge(tp_done, job + 1)
                    act.activation(hi_of(b), pt[:, job % 4, :], ACT.Copy).then_inc(tp_hi, 1)

            def tp_scaled(name, scale_of, bias_of):
                for b in range(16):
                    job = TPJ[name] + b
                    act.wait_ge(tp_done, job + 1)
                    if b >= 2:
                        act.wait_ge(tp_lo, job - 1)
                    kt = b % 8
                    bias = bias_of(kt) if bias_of else 0.0
                    act.activation(evac[:, 0, (b % 2) * HB:(b % 2 + 1) * HB], pt[:, job % 4, :], ACT.Identity,
                                   bias=bias, scale=scale_of(kt)).then_inc(tp_hi, 1)

            def to_actT(nk, k0=0):
                def f(b):
                    half, kt = b // nk, b % nk
                    return actT_hi[:, k0 + kt, half * HB:(half + 1) * HB]
                return f

            def tile_out(i, per, t, buf, func=ACT.Copy, **kw):
                act.wait_ge(tile_done, i * per + (t + 1))
                if not isinstance(i, int) or t + per * i >= 2:
                    act.wait_ge(x_used, i * per + (t - 1))
                act.activation(buf[:, t % 2, :], pd[:, t % 2, :], func, **kw).then_inc(t_free, 1)

            tp_plain("x", range(16), to_actT(8))
            act.wait_ge(vecs, 16 * 10)
            act.activation(c_act[:, :], c_col[:, :], ACT.Sigmoid).then_inc(c_ready, 1)
            for t in range(5):
                tile_out(0, 0, t, evac_att)
                if t:
                    act.wait_ge(pool_mm, t)
                    act.activation(ypool[:, t - 1, :], pt[:, 0:2, :].rearrange("p a b -> p (a b)"), ACT.Copy,
                                   scale=pscale[:, t - 1:t]).then_inc(pool_out, 1)
            tile_out(0, 0, 5, evac_att)

            def job_hi(i, n, kv, ends):
                for e, kind, half in ends:
                    act.wait_ge(jb_done, i * (2 * NJ2) + (n + e + 1))
                    src = pd[:, 0, half * HB:(half + 1) * HB]
                    cols = slice(half * HB, (half + 1) * HB)
                    if kind == "V":
                        act.activation(v_cols[:, cols], src, ACT.Copy).then_inc(jb_hi, 1)
                    elif kind == "T":
                        act.activation(kv["v"][0][:, 4 * half:4 * half + 4, :].rearrange("p a b -> p (a b)"),
                                       src, ACT.Copy).then_inc(jb_hi, 1)
                    elif kind == "Q":
                        act.activation(kv["q"][0][:, cols], src, ACT.Copy, scale=QSCALE).then_inc(jb_hi, 1)
                    else:
                        act.activation(kv["k"][0][:, cols], src, ACT.Copy).then_inc(jb_hi, 1)

            def soft_pair(prob, pT_hi, W, st, sinks, i, per, jobs):
                def exps(s):
                    n = (min(s % 8, W - 1) + 1) * P
                    act.wait_ge(nm_ready, i * per + (st + s + 1))
                    act.activation(prob[:, s % 2, 0:n], prob[:, s % 2, 0:n], ACT.Exp, bias=nmx[:, s:s + 1],
                                   accum_out=den[:, s:s + 1]).then_inc(p_ready, 1)

                def parts(s):
                    n = (min(s % 8, W - 1) + 1) * P
                    act.wait_ge(pt_done, i * per + (st + s + 1))
                    if s >= 2:
                        act.wait_ge(pv_done, i * per + (st + s - 1))
                    act.activation(pT_hi[:, s % 2, 0:n], ptT[:, s_at(W, s):s_at(W, s) + n], ACT.Copy).then_inc(pt_hi_s, 1)

                for s in range(16):
                    exps(s)
                    if s:
                        parts(s - 1)
                        jobs(s - 1)
                parts(15)
                jobs(15)
                if sinks is not None:
                    for hh in range(2):
                        h = sinks + 4 * hh
                        act.activation(sden[:, 8 * hh:8 * hh + 8], nmx[:, 8 * hh:8 * hh + 8], ACT.Exp,
                                       bias=sink[:, h:h + 1]).then_inc(sink_e, 1)

            def beside1(j, s):
                if j < 3:
                    job_hi(0, NJ1 * (j + 1), att1[(j + 1) % 2], ended(PLAN1[1][s]))
                elif s < 8 and s % 2 == 0:
                    if s == 0:
                        act.wait_ge(jb_done, 4 * NJ1)
                    act.activation(actT_hi[:, s // 2, :], ypool[:, s // 2, :], ACT.Copy).then_inc(yp_hi, 1)

            for part in PLAN1[1]:
                job_hi(0, 0, att1[0], ended(part))
            for j in range(4):
                if j:
                    act.wait_ge(o_done, j)
                soft_pair(prob1, pT1_hi, W1, 16 * j, j, 0, 0, lambda s: beside1(j, s))
            act.wait_ge(o_done, 4)
            act.sem_inc(t_free, 4)
            act.dma_start(row_a[:, :], spread(ln1_g, 0, D)).then_inc(gb_in, 16)
            act.dma_start(row_b[:, :], spread(ln1_b, 0, D)).then_inc(gb_in, 16)
            tp_plain("o1", range(8), to_actT(4, 4))

            def std_of(n):
                act.wait_ge(stat_in, n + 1)
                act.activation(std[:, n % 2:n % 2 + 1], mv2[:, n % 2, 1:2], ACT.Sqrt, bias=eps[:, 0:1]).then_inc(std_done, 1)

            def norm_rows(name, base):
                for r in range(7):
                    std_of(base + r)
                tp_plain(name, range(8), to_actT(8))
                std_of(base + 7)

            norm_rows("h1", 0)
            tp_plain("h1", range(8, 16), to_actT(8))
            act.dma_start(row_a[:, :], spread(ln2_g, 0, D)).then_inc(gb_in, 16)
            act.dma_start(row_b[:, :], spread(ln2_b, 0, D)).then_inc(gb_in, 16)

            def ff_tiles(i, last=False):
                for j in range(4):
                    if not last or j < 3:
                        tile_out(i, 4, T_FF + j + 1, evac, ACT.Relu)
                    for k in (2 * j, 2 * j + 1):
                        act.wait_ge(ada_used, i * 8 + (k + 1))
                        act.dma_start(ada_raw[:, k % 2, :], w_ada[k * P:(k + 1) * P, ds(i * AW, AW)])\
                            .then_inc(ada_in[k % 2], 16)

            tile_out(0, 0, T_FF, evac, ACT.Relu)
            with act.Fori(0, 7) as i:
                ff_tiles(i)
            ff_tiles(7, True)
            norm_rows("h2", 8)
            act.wait_ge(m_rows, 80)
            act.dma_start(p_rows[:, :, :], p.rearrange("(r q) n -> q r n", q=P)).then_inc(p_in, 16)
            tp_plain("h2", range(8, 16), to_actT(8))
            tp_plain("p", range(4), lambda b: hid_hi[:, b % 2, (b // 2) * HB:(b // 2 + 1) * HB])

            def gate_out(i, c):
                act.wait_ge(ple_done, i * 2 + (c + 1))
                act.wait_ge(gp_ready, i * 2 + (c + 1))
                act.activation(evac[:, 0, :], pd[:, 0, :], ACT.Copy).then_inc(ple_free, 1)
                act.wait_ge(tile_done, i * 2 + (TILE["gate"] + c + 1))
                act.activation(evac[:, 1, :], pd[:, 1, :], ACT.Sigmoid,
                               bias=b_gate[:, ds(i * 2 + c, 1)]).then_inc(t_free, 1)

            with act.Fori(0, 4) as i:
                gate_out(i, 0)
                gate_out(i, 1)

            def row_squares(n0, dst, rows=None):
                def root(r):
                    act.wait_ge(sq_done, n0 + r + 1)
                    act.activation(rms[:, r:r + 1], ssq[:, r:r + 1], ACT.Sqrt, bias=eps[:, 1:2], scale=1.0 / D)\
                        .then_inc(ss_done, 1)

                for r in range(RT):
                    if rows is not None:
                        act.wait_ge(row_done, rows + r + 1)
                    act.activation(dst[:, r, :], acc[:, r, :], ACT.Square,
                                   accum_out=ssq[:, r:r + 1]).then_inc(sq_done, 1)
                    if r:
                        root(r - 1)
                root(RT - 1)

            act.wait_ge(x_used, TILE["in2a"])
            row_squares(0, rows2)
            tp_scaled("m1", lambda k: modT[:, 8 + k:9 + k], lambda k: modT[:, k:k + 1])

            rel_ap = rel_rev
            act.dma_start(ext.ap()[:, 511:767], rel_ap[:, 0:256]).then_inc(ext_in, 16)
            act.dma_start(ext.ap()[:, 0:511].unsqueeze(2), bass.AP(rel_rev.tensor, 0, [[257, 8], [0, 511], [1, 1]])).then_inc(ext_in, 16)
            act.wait_ge(ext_in, 32)
            act.wait_ge(mid_out, 16 * RT)
            for part in PLAN_ALONE[1]:
                job_hi(0, 4 * NJ1, att2[0], ended(part))
            with act.Fori(0, 2) as i:
                for pp in range(2):
                    def jobs(part):
                        job_hi(i, 4 * NJ1 + NJ2 * (pp + 1), att2[(pp + 1) % 2], ended(part))

                    act.wait_ge(o_done, i * 2 + (4 + pp))
                    act.dma_start(bias_up[:, :, :], bass.AP(ext, i * (4 * 768) + 2 * pp * 768,
                                                            [[1, P], [768, 2], [1, NA]])).then_inc(bias_in, 16)
                    jobs(PLAN_A[0])
                    for hh in range(2):
                        act.wait_ge(bias_mm, i * 4 + (2 * pp + hh + 1))
                        act.activation(bias2[:, hh, :], pt[:, 2:4, :].rearrange("p a b -> p (a b)")[:, 0:NA],
                                       ACT.Copy).then_inc(bias_cp, 1)
                    soft_pair(prob2, pT2_hi, WA, 64 + 16 * pp, None, i, 32, lambda s: jobs(PLAN_A[1][s]))

            def stick_pair(pair):
                def at(sem_, n):
                    act.wait_ge(sem_, NB * pair + n)

                def cols(s):
                    return bcols(*BSTEPS[s][1:])[1]

                for s in range(NB + 2):
                    if s < NB:
                        n = cols(s)
                        at(b_s, s + 1)
                        if s >= 3:
                            at(b_ws, s - 2)
                        act.activation(logit[:, s % 3, 0:n], pd[:, 1, (s % 2) * HB:(s % 2) * HB + n], ACT.Copy)\
                            .then_inc(b_l, 1)
                    if s >= 2:
                        at(b_sub, s - 1)
                        n = cols(s - 2)
                        act.activation(logit[:, (s - 2) % 3, 0:n], logit[:, (s - 2) % 3, 0:n], ACT.Exp)\
                            .then_inc(b_w, 1)
                    if s < NB:
                        n = cols(s)
                        at(b_t, s + 1)
                        act.activation(soft[:, s % 2, 0:n], soft[:, s % 2, 0:n], ACT.Exp).then_inc(b_exp, 1)
                        at(b_exp, s + 1)
                        act.activation(soft[:, s % 2, 0:n], soft[:, s % 2, 0:n], ACT.Ln, bias=1.0)\
                            .then_inc(b_ln, 1)
                    if 1 <= s <= NB and pair < 3:
                        job_hi(0, 4 * NJ1 + NJ2 * (5 + pair), att2[(pair + 1) % 2], ended(PLAN_B[1][s - 1]))

            act.preload_act_table_set("natural_log_exp_and_others")
            for pair in range(4):
                act.wait_ge(o_done, 8 + pair)
                stick_pair(pair)

            act.wait_ge(o_done, 12)
            act.sem_inc(t_free, 24)
            act.dma_start(acc[:, :, :], x_mid.rearrange("(r p) n -> p r n", p=P)).then_inc(mid_in, 16)
            ptf = pt[:, :, :].rearrange("p a b -> p (a b)")
            for n in range(16):
                r, h = n // 2, n % 2
                if n == 4:
                    act.wait_ge(bc_mm, 1)
                    act.activation(row_a[:, :], ptf[:, 0:D], ACT.Copy).then_inc(gb_rows, 1)
                    act.activation(row_b[:, :], ptf[:, D:2 * D], ACT.Copy).then_inc(gb_rows, 1)
                if n >= 2:
                    act.wait_ge(sq_done, 8 + n - 1)
                act.activation(evac[:, 0, 0:HB] if n % 2 else evac[:, 0, HB:D], rows2[:, r, h * HB:(h + 1) * HB],
                               ACT.Square, accum_out=ssq[:, n:n + 1]).then_inc(sq_done, 1)
                if h:
                    act.wait_ge(sq_done, 8 + n + 1)
                    act.activation(rms[:, n - 1:n + 1], ssq[:, n - 1:n + 1], ACT.Sqrt, bias=eps[:, 1:2],
                                   scale=1.0 / HB).then_inc(ss_done, 1)
            tp_scaled("o2", lambda k: gab[:, k:k + 1], None)
            row_squares(24, rows3, 16)
            tp_scaled("m2", lambda k: modT[:, 32 + k:33 + k], lambda k: modT[:, 24 + k:25 + k])

            def up_out(i, nh, last=False):
                for j in range(nh):
                    tile_out(i, 8, T_UP + 2 * j + 1, evac)
                    act.wait_ge(cv_done, i * 4 + (j + 1))
                    act.activation(cv[:, 0, :], cv[:, 0, :], ACT.Silu).then_inc(silu_done, 1)
                    if not last or j < nh - 1:
                        tile_out(i, 8, T_UP + 2 * j + 2, evac)

            tile_out(0, 0, T_UP, evac)
            with act.Fori(0, NC2) as i:
                up_out(i, 4)
            up_out(NC2, 2, True)
            act.wait_ge(x_used, (T_UP + 8 * NC2) + 4)
            act.dma_start(row_g[:, :], spread(final_g_2, 0, D)).then_inc(g_in, 16)
            for r in range(RT):
                act.wait_ge(row_done, 24 + r + 1)
                act.activation(sq_junk[:, :], acc[:, r, :], ACT.Square,
                               accum_out=ssq[:, r:r + 1]).then_inc(sq_done, 1)
                act.wait_ge(sq_done, 32 + r + 1)
                act.activation(rms[:, r:r + 1], ssq[:, r:r + 1], ACT.Sqrt, bias=eps[:, 1:2], scale=1.0 / D)\
                    .then_inc(ss_done, 1)

        @block.vector
        def _(dve):
            ch = Chain(dve, vchain)
            link = ch.link

            def split(hi, lo, src, sem_):
                link(dve.tensor_copy(hi, src))
                dve.tensor_tensor(lo, src, hi.bitcast(F32), ALU.subtract).then_inc(sem_, 1)

            dve.wait_ge(consts, 1)
            dve.memset(eps_one[:, :], 1.0).then_inc(act_one, 1)
            link(dve.tensor_copy(tri[:, :, :], tri_f[:, :, :]))
            link(dve.tensor_copy(wcount[:, :], wcnt_i[:, :]))
            link(dve.reciprocal(wcount[:, :], wcount[:, :]))

            def tp_lo_plain(name, n, hi_of, lo_of):
                for b in n:
                    job = TPJ[name] + b
                    dve.wait_ge(tp_hi, job + 1)
                    dve.tensor_tensor(lo_of(b), pt[:, job % 4, :], hi_of(b).bitcast(F32), ALU.subtract)\
                        .then_inc(tp_lo, 1)

            def tp_lo_scaled(name):
                for b in range(16):
                    job = TPJ[name] + b
                    half, kt = b // 8, b % 8
                    c = slice(half * HB, (half + 1) * HB)
                    dve.wait_ge(tp_hi, job + 1)
                    split(actT_hi[:, kt, c], actT_lo[:, kt, c], evac[:, 0, (b % 2) * HB:(b % 2 + 1) * HB], tp_lo)

            def T(t_, nk, k0=0):
                return lambda b: t_[:, k0 + b % nk, (b // nk) * HB:(b // nk + 1) * HB]

            tp_lo_plain("x", range(16), T(actT_hi, 8), T(actT_lo, 8))
            dve.wait_ge(vecs, 16 * 10)
            split(pwr_hi[:, :, :], pwr_lo[:, :, :], pw[:, :, :], pw_split)
            dve.wait_ge(c_ready, 1)
            dve.tensor_tensor(c_act[:, :], c_act[:, :], c_col[:, :], ALU.mult).then_inc(ada_used, 2)
            for g in range(4):
                dve.wait_ge(t_free, g + 1)
                u = evac_att[:, g % 2, :]
                if g:
                    dve.wait_ge(d_ready, g)
                src, w = u, 1
                for step in range(g + 1):
                    dst = sums[:, step % 2, :]
                    link(dve.tensor_copy(dst[:, 0:w], src[:, 0:w]))
                    link(dve.tensor_tensor(dst[:, w:S], src[:, w:S], src[:, 0:S - w], ALU.add))
                    src, w = dst, 2 * w
                link(dve.tensor_tensor(src[:, 0:w], src[:, 0:w], wcount[:, 0:w], ALU.mult))
                link(dve.tensor_tensor(src[:, 0:w], src[:, 0:w], u[:, 0:w], ALU.subtract))
                link(dve.scalar_tensor_tensor(out=src[:, w:S], in0=src[:, w:S], scalar=1.0 / w, in1=u[:, w:S],
                                              op0=ALU.mult, op1=ALU.subtract))
                dve.sem_inc(x_used, 1)
                if g:
                    dve.wait_ge(pool_mm, g)
                split(d_hi[:, :], d_lo[:, :], src, d_ready)
            dve.wait_ge(t_free, 5)
            split(att1[0]["k"][0][:, :], att1[0]["k"][1][:, :], evac_att[:, 0, :], x_used)
            dve.wait_ge(v_done, 1)
            split(att1[0]["v"][0][:, :, :].rearrange("p a b -> p (a b)"),
                  att1[0]["v"][1][:, :, :].rearrange("p a b -> p (a b)"), ptT[:, :], x_used)

            def job_lo(i, n, kv, ends):
                for e, kind, half in ends:
                    if kind == "V":
                        continue
                    dve.wait_ge(jb_hi, i * (2 * NJ2) + (n + e + 1))
                    src = pd[:, 0, half * HB:(half + 1) * HB]
                    cols = slice(half * HB, (half + 1) * HB)
                    if kind == "Q":
                        hi, lo = kv["q"]
                        dve.scalar_tensor_tensor(out=lo[:, cols], in0=src, scalar=QSCALE, in1=hi[:, cols].bitcast(F32),
                                                 op0=ALU.mult, op1=ALU.subtract).then_inc(jb_lo, 1)
                    elif kind == "K":
                        hi, lo = kv["k"]
                        dve.tensor_tensor(lo[:, cols], src, hi[:, cols].bitcast(F32), ALU.subtract).then_inc(jb_lo, 1)
                    else:
                        hi, lo = (t_[:, 4 * half:4 * half + 4, :].rearrange("p a b -> p (a b)") for t_ in kv["v"])
                        dve.tensor_tensor(lo, src, hi.bitcast(F32), ALU.subtract).then_inc(jb_lo, 1)

            def soft_pair(prob, pT_hi, pT_lo, W, bias_ap, st, sinks, o_out, i, per, jobs):
                def top(s):
                    n = (min(s % 8, W - 1) + 1) * P
                    dve.wait_ge(s_done, i * per + (st + s + 1))
                    if s >= 2:
                        dve.wait_ge(pt_done, i * per + (st + s - 1))
                    dve.memset(nmx[:, s:s + 1], 0.0)
                    link(dve.tensor_tensor_reduce(out=prob[:, s % 2, 0:n], in0=pd[:, 1, s_at(W, s):s_at(W, s) + n],
                                                  in1=bias_ap(s // 8)[:, W * P - n:W * P], scale=1.0,
                                                  scalar=-3e38, op0=ALU.add, op1=ALU.max,
                                                  accum_out=mx[:, s:s + 1]))
                    if sinks is None:
                        dve.tensor_scalar(nmx[:, s:s + 1], mx[:, s:s + 1], -1.0, None, ALU.mult)\
                            .then_inc(nm_ready, 1)
                    else:
                        h = sinks + 4 * (s // 8)
                        dve.tensor_scalar(nmx[:, s:s + 1], mx[:, s:s + 1], sink[:, h:h + 1], -1.0,
                                          ALU.max, ALU.mult).then_inc(nm_ready, 1)

                def low(s):
                    n = (min(s % 8, W - 1) + 1) * P
                    dve.wait_ge(pt_hi_s, i * per + (st + s + 1))
                    dve.tensor_tensor(pT_lo[:, s % 2, 0:n], ptT[:, s_at(W, s):s_at(W, s) + n], pT_hi[:, s % 2, 0:n].bitcast(F32),
                                      ALU.subtract).then_inc(pt_lo_s, 1)

                for s in range(16):
                    top(s)
                    if s:
                        low(s - 1)
                        jobs(s - 1)
                low(15)
                jobs(15)
                dve.wait_ge(pv_done, i * per + (st + 16))
                if sinks is not None:
                    dve.wait_ge(sink_e, 2 * (sinks + 1))
                    link(dve.tensor_tensor(den[:, :], den[:, :], sden[:, :], ALU.add))
                link(dve.reciprocal(rinv[:, :], den[:, :]))
                for hh in range(2):
                    last = dve.tensor_tensor(o_out(hh), pt[:, hh, :].rearrange("p (r c) -> p r c", c=64),
                                             rinv[:, 8 * hh:8 * hh + 8].unsqueeze(2).to_broadcast([P, 8, 64]),
                                             ALU.mult)
                last.then_inc(o_done, 1)

            def beside1(j, s):
                if j < 3:
                    job_lo(0, NJ1 * (j + 1), att1[(j + 1) % 2], ended(PLAN1[1][s]))
                elif s < 8 and s % 2 == 0:
                    g = s // 2
                    dve.wait_ge(yp_hi, g + 1)
                    dve.tensor_tensor(actT_lo[:, g, :], ypool[:, g, :], actT_hi[:, g, :].bitcast(F32),
                                      ALU.subtract).then_inc(yp_lo, 1)

            for part in PLAN1[1]:
                job_lo(0, 0, att1[0], ended(part))
            for j in range(4):
                soft_pair(prob1, pT1_hi, pT1_lo, W1, lambda hh: bias1[:, j + 4 * hh, :], 16 * j, j,
                          lambda hh: o1[:, :, (j + 4 * hh) * 64:(j + 4 * hh + 1) * 64], 0, 0,
                          lambda s: beside1(j, s))
            dve.sem_inc(x_used, 4)
            tp_lo_plain("o1", range(8), T(actT_hi, 4, 4), T(actT_lo, 4, 4))

            def pdr(r):
                return pd[:, (r + 1) % 2, :]

            def stat(r):
                link(dve.bn_stats(out=stats[:, 0, :], in_=acc[:, r, 0:HB]))
                link(dve.bn_stats(out=stats[:, 1, :], in_=acc[:, r, HB:D]))
                dve.bn_aggr(out=mv2[:, r % 2, :], in_=stats[:, :, :]).then_inc(stat_in, 1)

            def finish(r, n):
                dve.wait_ge(std_done, n)
                link(dve.reciprocal(rstd[:, :], std[:, r % 2:r % 2 + 1]))
                link(dve.scalar_tensor_tensor(out=nmr[:, :], in0=mv2[:, r % 2, 0:1], scalar=-1.0, in1=rstd[:, :],
                                              op0=ALU.mult, op1=ALU.mult))
                link(dve.tensor_scalar(acc[:, r, :], acc[:, r, :], rstd[:, :], nmr[:, :], ALU.mult, ALU.add))
                link(dve.tensor_tensor(acc[:, r, :], acc[:, r, :], row_a[:, :], ALU.mult))
                dve.tensor_tensor(acc[:, r, :], acc[:, r, :], row_b[:, :], ALU.add).then_inc(row_done, 1)

            def add_row(r, scale=None):
                if scale is None:
                    return dve.tensor_tensor(acc[:, r, :], acc[:, r, :], pdr(r), ALU.add)
                return dve.scalar_tensor_tensor(out=acc[:, r, :], in0=acc[:, r, :], scalar=scale, in1=pdr(r),
                                                op0=ALU.mult, op1=ALU.add)

            def norm_chunk(ch_, name, base, extra=None):
                for r in range(RT):
                    dve.wait_ge(m_rows, 8 * ch_ + r + 1)
                    add_row(r).then_inc(m_free, 1)
                    if r == 0 and extra:
                        extra()
                    dve.wait_ge(m_free, 8 * ch_ + r + 1)
                    stat(r)
                    if r:
                        finish(r - 1, base + r)
                    if r == 6:
                        tp_lo_plain(name, range(8), T(actT_hi, 8), T(actT_lo, 8))
                finish(7, base + 8)
                tp_lo_plain(name, range(8, 16), T(actT_hi, 8), T(actT_lo, 8))
                if name == "h1":
                    for r in range(RT):
                        link(dve.tensor_scalar(acc[:, r, :], acc[:, r, :], ALPHA, None, ALU.mult))

            for r in range(RT):
                dve.wait_ge(x_back[r], 16)
                dve.wait_ge(m_rows, r + 1)
                add_row(r, ALPHA).then_inc(m_free, 1)
            dve.wait_ge(gb_in, 32)
            dve.wait_ge(m_free, 8)
            norm_chunk(1, "h1", 0)

            def ff_tiles(i):
                for j in range(4):
                    t = T_FF + j
                    xs = evac[:, t % 2, :]
                    dve.wait_ge(t_free, i * 4 + (t + 1))
                    link(dve.tensor_tensor(xs, xs, xs, ALU.mult))
                    dve.wait_ge(m_rows, i * 8 + 16)
                    split(hid_hi[:, j, :], hid_lo[:, j, :], xs, x_used)
                    for k in (2 * j, 2 * j + 1):
                        dve.wait_ge(ada_in[k % 2], i * 64 + 16 * (k // 2 + 1))
                        if k == 0:
                            ins = dve.tensor_scalar(ada_acc[:, :], ada_raw[:, 0, :], c_act[:, 0:1], None, ALU.mult)
                        else:
                            ins = dve.scalar_tensor_tensor(out=ada_acc[:, :], in0=ada_raw[:, k % 2, :],
                                                           scalar=c_act[:, k:k + 1], in1=ada_acc[:, :],
                                                           op0=ALU.mult, op1=ALU.add)
                        ins.then_inc(ada_used, 1)
                        dve.wait_ge(ada_used, i * 8 + (k + 3))
                dve.sem_inc(ada_full, 1)

            def mod_cols(i):
                dve.wait_ge(ada_mm, i + 1)
                link(dve.tensor_tensor(modT[:, ds(i * 6, 6)], pt[:, 3, 0:6], b_ada[:, ds(i * 6, 6)], ALU.add))

            with dve.Fori(0, 7) as i:
                ch.enter(i, 4 * 2 + 1)
                ff_tiles(i)
                for r in range(RT):
                    dve.wait_ge(m_rows, i * 8 + (16 + r + 1))
                    add_row(r).then_inc(m_free, 1)
                    if r == 0:
                        mod_cols(i)
            ch.leave(7)
            ff_tiles(7)
            dve.wait_ge(gb_in, 64)
            dve.wait_ge(m_free, 72)

            def last_mod():
                mod_cols(7)
                link(dve.tensor_scalar(modT[:, 8:16], modT[:, 8:16], 1.0, None, ALU.add))
                link(dve.tensor_scalar(modT[:, 32:40], modT[:, 32:40], 1.0, None, ALU.add))

            norm_chunk(9, "h2", 8, last_mod)
            hp = [lambda b: hid_hi[:, b % 2, (b // 2) * HB:(b // 2 + 1) * HB],
                  lambda b: hid_lo[:, b % 2, (b // 2) * HB:(b // 2 + 1) * HB]]
            tp_lo_plain("p", range(4), *hp)
            dve.sem_inc(gp_ready, 1)

            def gate_prod(i, c):
                dve.wait_ge(t_free, i * 2 + (TILE["gate"] + c + 1))
                dve.wait_ge(ple_free, i * 2 + (c + 2))
                dve.tensor_tensor(gprod[:, c, :], evac[:, 0, :], evac[:, 1, :], ALU.mult).then_inc(gp_ready, 1)

            def gate_add(i, c):
                dve.wait_ge(gp_mm, i * 2 + (c + 1))
                col = acc[:, :, ds((i * 2 + c) * P, P)]
                dve.tensor_tensor(col, col, pt[:, 2 * c:2 * c + 2, :].rearrange("p a (b n) -> p (a b) n", n=P),
                                  ALU.add).then_inc(x_used, 1)

            with dve.Fori(0, 4) as i:
                gate_prod(i, 0)
                gate_prod(i, 1)
                gate_add(i, 0)
                gate_add(i, 1)

            def scaled_row(r, n, dst):
                dve.wait_ge(ss_done, n + r + 1)
                link(dve.reciprocal(rinv[:, r:r + 1], rms[:, r:r + 1]))
                dve.tensor_scalar(dst[:, r, :], acc[:, r, :], rinv[:, r:r + 1], None, ALU.mult)\
                    .then_inc(row_rd, 1)

            for r in range(RT):
                scaled_row(r, 0, rows2)
            tp_lo_scaled("m1")

            def rows_of(i, col):
                return rows2[:, :, ds(i * 256 + col, 64)]

            for part in PLAN_ALONE[1]:
                job_lo(0, 4 * NJ1, att2[0], ended(part))
            with dve.Fori(0, 2) as i:
                ch.enter(i, 2 * (16 + 1))
                for pp in range(2):
                    dve.wait_ge(bias_cp, i * 4 + (2 * pp + 2))
                    dve.memset(bias2[0:64, :, 576:640], -BIG).then_inc(bias_rdy, 1)
                    dve.memset(bias2[64:128, :, 0:64], -BIG).then_inc(bias_rdy, 1)
                    dve.wait_ge(bias_rdy, i * 4 + (2 * pp + 2))
                    soft_pair(prob2, pT2_hi, pT2_lo, WA, lambda hh: bias2[:, hh, :], 64 + 16 * pp, None,
                              lambda hh: rows_of(i, (2 * pp + hh) * 64), i, 32,
                              lambda s: job_lo(i, 4 * NJ1 + NJ2 * (pp + 1), att2[(pp + 1) % 2],
                                               ended(PLAN_A[1][s])))
            ch.leave(2)

            def stick_pair(pair):
                def at(sem_, n):
                    dve.wait_ge(sem_, NB * pair + n)

                def geo(s):
                    hh, hf, kt = BSTEPS[s]
                    _, n, co = bcols(hf, kt)
                    return n, co, kt >= 4 * hf, 2 + (hh * 2 + hf) % 2

                for s in range(NB + 2):
                    if s >= 2:
                        n, co, onto, bank = geo(s - 2)
                        lg = logit[:, (s - 2) % 3, 0:n]
                        at(b_c, s - 1)
                        ins = dve.tensor_tensor(lg, lg, pt[:, bank, co:co + n], ALU.subtract)
                        if onto:
                            link(ins)
                            ins = dve.tensor_tensor(lg[:, 0:P], lg[:, 0:P], drop[:, :], ALU.add)
                        ins.then_inc(b_sub, 1)
                    if s < NB:
                        n = geo(s)[0]
                        at(b_l, s + 1)
                        dve.tensor_scalar(soft[:, s % 2, 0:n], logit[:, s % 3, 0:n], 30.0, None, ALU.min)\
                            .then_inc(b_t, 1)
                    if 1 <= s <= NB:
                        z = s - 1
                        n, co, onto, bank = geo(z)
                        sf = soft[:, z % 2, 0:n]
                        at(b_ln, z + 1)
                        link(dve.tensor_tensor(sf, sf, logit[:, z % 3, 0:n], ALU.max))
                        if onto:
                            link(dve.tensor_tensor(sf[:, 0:P], sf[:, 0:P], keep[:, :], ALU.mult))
                        split(sp_hi[:, z % 2, 0:n], sp_lo[:, z % 2, 0:n], sf, b_sp)
                    if s >= 2:
                        z = s - 2
                        n = geo(z)[0]
                        at(b_w, z + 1)
                        split(wt_hi[:, z % 2, 0:n], wt_lo[:, z % 2, 0:n], logit[:, z % 3, 0:n], b_ws)
                    if 1 <= s <= NB and pair < 3:
                        job_lo(0, 4 * NJ1 + NJ2 * (5 + pair), att2[(pair + 1) % 2], ended(PLAN_B[1][s - 1]))
                at(b_pv, NB)
                for hh in range(2):
                    last = dve.tensor_copy(rows_of(0, HB + (2 * pair + hh) * 64),
                                           pt[:, hh, :].rearrange("p (r c) -> p r c", c=64))
                last.then_inc(o_done, 1)

            for pair in range(4):
                stick_pair(pair)
            dve.sem_inc(x_used, 24)

            for n in range(16):
                col = 16 + n if n < 8 else 40 + n - 8
                last = dve.tensor_scalar(diag[:, n, :], ident[:, :], modT[:, col:col + 1], None, ALU.mult)
            last.then_inc(diag_rdy, 1)
            for r in range(RT):
                dve.wait_ge(ss_done, 8 + r + 1)
                link(dve.reciprocal(rinv[:, 2 * r:2 * r + 2], rms[:, 2 * r:2 * r + 2]))
                for h in range(2):
                    last = dve.tensor_scalar(rows2[:, r, h * HB:(h + 1) * HB], rows2[:, r, h * HB:(h + 1) * HB],
                                             rinv[:, 2 * r + h:2 * r + h + 1], None, ALU.mult)
                last.then_inc(row_rd, 1)
            tp_lo_scaled("o2")

            def gated_row(r, row_gate, gt, mf, sem_wait):
                sem_wait()
                dve.wait_ge(m_free, mf)
                link(dve.tensor_tensor(gt[:, :], pdr(r), row_gate[:, :], ALU.mult))
                dve.tensor_tensor(acc[:, r, :], acc[:, r, :], gt[:, :], ALU.add).then_inc(m_free, 1)

            dve.wait_ge(gb_rows, 2)
            dve.wait_ge(mid_in, 16)
            for c in range(2):
                for r in range(RT):
                    ch_ = CH["out2"] + c
                    gated_row(r, row_a, gated1, 8 * ch_ + r, lambda: dve.wait_ge(m_rows, 8 * ch_ + r + 1))
                    if c:
                        dve.wait_ge(m_free, 8 * ch_ + r + 1)
                        dve.sem_inc(row_done, 1)
                        if r:
                            scaled_row(r - 1, 16, rows3)
            scaled_row(RT - 1, 16, rows3)
            tp_lo_scaled("m2")

            def up_tiles(i, nh):
                for j in range(nh):
                    dve.wait_ge(x_used, i * 8 + (T_UP + 2 * j))
                    for v in range(2):
                        t = T_UP + 2 * j + v
                        f = i * 4 + (j + 22 * v)
                        u = evac[:, t % 2, :]
                        y = cv[:, v, :]
                        dve.wait_ge(t_free, i * 8 + (t + 1))
                        link(dve.tensor_scalar(y, u, cw[:, 2, ds(f, 1)], cb[:, ds(f, 1)], ALU.mult, ALU.add))
                        link(dve.scalar_tensor_tensor(out=y[:, 1:S], in0=u[:, 0:S - 1], scalar=cw[:, 1, ds(f, 1)],
                                                      in1=y[:, 1:S], op0=ALU.mult, op1=ALU.add))
                        ins = dve.scalar_tensor_tensor(out=y[:, 2:S], in0=u[:, 0:S - 2], scalar=cw[:, 0, ds(f, 1)],
                                                       in1=y[:, 2:S], op0=ALU.mult, op1=ALU.add)
                        if v == 0:
                            ins.then_inc(cv_done, 1)
                            dve.wait_ge(cv_done, i * 4 + (j + 1))
                            dve.sem_inc(x_used, 1)
                        else:
                            link(ins)
                    dve.wait_ge(silu_done, i * 4 + (j + 1))
                    link(dve.tensor_tensor(cv[:, 0, :], cv[:, 0, :], cv[:, 1, :], ALU.mult))
                    dve.wait_ge(m_rows, i * 8 + 8 * CH["up"])
                    split(hid_hi[:, j, :], hid_lo[:, j, :], cv[:, 0, :], x_used)

            with dve.Fori(0, 5) as i:
                ch.enter(i, 4 * (2 + 3 + 2) + 8)
                up_tiles(i, 4)
                for r in range(RT):
                    gated_row(r, row_b, gated2, i * 8 + (8 * CH["up"] + r), lambda: dve.wait_ge(m_rows, i * 8 + (8 * CH["up"] + r + 1)))
            ch.leave(5)
            up_tiles(NC2, 2)
            def final_row(r):
                dve.wait_ge(ss_done, 24 + r + 1)
                link(dve.reciprocal(rinv[:, r:r + 1], rms[:, r:r + 1]))
                if r >= 2:
                    dve.wait_ge(stored[r % 2], 16 * (r // 2))
                dve.scalar_tensor_tensor(out=evac[:, r % 2, :], in0=acc[:, r, :], scalar=rinv[:, r:r + 1],
                                         in1=row_g[:, :], op0=ALU.mult, op1=ALU.mult).then_inc(fin_rdy, 1)

            for r in range(RT):
                gated_row(r, row_b, gated2, 8 * CH["upb"] + r, lambda: dve.wait_ge(m_rows, 8 * CH["upb"] + r + 1))
                dve.wait_ge(m_free, 8 * CH["upb"] + r + 1)
                dve.sem_inc(row_done, 1)
                if r == 0:
                    dve.wait_ge(g_in, 16)
                else:
                    final_row(r - 1)
            final_row(RT - 1)


_INS = ["x", "p", "w_in", "w_pool", "pool_scale", "attn_sinks", "w_out", "ln1_g", "ln1_b", "w_ff1", "w_ff2",
        "ln2_g", "ln2_b", "w_ple", "w_ple_gate", "b_ple_gate", "c_2", "w_ada_2", "b_ada_2", "w_in_2",
        "rel_bias_2", "g_a_2", "g_b_2", "w_out_2", "w_up_2", "conv_w_2", "conv_b_2", "w_down_2", "final_g_2"]


def kernel(**inputs):
    import numpy as _np
    import concourse.bacc as _bacc
    from concourse import mybir as _mybir
    from concourse.bass_utils import run_bass_kernel_spmd as _run

    nc = _bacc.Bacc("TRN2", target_bir_lowering=False, num_devices=1, dynamic_dma_scratch_size=1024)
    arrays, args = {}, []
    for name in _INS:
        a = _np.asarray(inputs[name])
        if name == "rel_bias_2":
            a = a[0, :, ::-1]
        a = _np.ascontiguousarray(a)
        arrays[f"in_{name}"] = a
        args.append(nc.dram_tensor(f"in_{name}", a.shape, _mybir.dt.from_np(a.dtype), kind="ExternalInput").ap())
    args.append(nc.dram_tensor("out_0", (1, S, D), F32, kind="ExternalOutput").ap())
    build(nc, *args)
    r = _run(nc, [arrays], core_ids=[0])
    return r.results[0]["out_0"]
```
